# Optimizing a Trainium2 kernel written in Bass

```python
import jax, jax.numpy as jnp
from jax import lax
import numpy as np

D_MODEL = 1024
BATCH = 1
SEQ = 256
DEPTH = 2

N_A_LAYERS = DEPTH // 2
N_B_LAYERS = DEPTH - N_A_LAYERS

LRU_WIDTH = D_MODEL * 3 // 2
LRU_BLOCKS = 16
LRU_BLOCK_W = LRU_WIDTH // LRU_BLOCKS
CONV_WIDTH = 4
LRU_C = 8.0

N_Q_HEADS = 16
N_KV_HEADS = 2
GROUP = N_Q_HEADS // N_KV_HEADS
HEAD_DIM = 64
ATT_WIDTH = N_Q_HEADS * HEAD_DIM
WINDOW = 128
BLOCK = 128

EPS = 1e-6


def rmsnorm(x, g):
    x32 = x.astype(jnp.float32)
    y = x32 * lax.rsqrt(jnp.mean(x32 * x32, axis=-1, keepdims=True) + EPS)
    return (y * g.astype(jnp.float32)).astype(x.dtype)

def causal_depthwise_conv(u, w, b):
    r = u.shape[-1]
    out = lax.conv_general_dilated(
        u, w.astype(u.dtype)[:, None, :], window_strides=(1,),
        padding=[(CONV_WIDTH - 1, 0)],
        dimension_numbers=("NWC", "WIO", "NWC"),
        feature_group_count=r)
    return out + b.astype(u.dtype)

def _linear_combine(c1, c2):
    a1, b1 = c1
    a2, b2 = c2
    return a1 * a2, a2 * b1 + b2

def rglru_layer(x, norm_g, w_in, conv_w, conv_b, wr, br, wi, bi, lam, w_out):
    bsz, seq, _ = x.shape
    h = rmsnorm(x, norm_g)
    u = h @ w_in
    xb, gate = u[..., :LRU_WIDTH], u[..., LRU_WIDTH:]
    xb = causal_depthwise_conv(xb, conv_w, conv_b)
    xs = xb.reshape(bsz, seq, LRU_BLOCKS, LRU_BLOCK_W)
    r = jax.nn.sigmoid((jnp.einsum('bshi,hij->bshj', xs, wr).reshape(bsz, seq, LRU_WIDTH) + br).astype(jnp.float32))
    i = jax.nn.sigmoid((jnp.einsum('bshi,hij->bshj', xs, wi).reshape(bsz, seq, LRU_WIDTH) + bi).astype(jnp.float32))
    log_a = -LRU_C * r * jax.nn.softplus(-lam.astype(jnp.float32))
    a = jnp.exp(log_a)
    b = jnp.sqrt(-jnp.expm1(2.0 * log_a)) * (i * xb.astype(jnp.float32))
    _, hs = lax.associative_scan(_linear_combine, (a, b), axis=1)
    y = hs.astype(x.dtype) * jax.nn.silu(gate)
    return x + y @ w_out

def sliding_window_sink_attention(q, k, v, sinks):
    bsz, seq = q.shape[0], q.shape[1]
    nb = seq // BLOCK
    qb = q.reshape(bsz, nb, BLOCK, N_KV_HEADS, GROUP, HEAD_DIM)

    def band(t):
        cur = t.reshape(bsz, nb, BLOCK, N_KV_HEADS, HEAD_DIM)
        prev = jnp.concatenate([jnp.zeros_like(cur[:, :1]), cur[:, :-1]], axis=1)
        return jnp.concatenate([prev, cur], axis=2)

    kb, vb = band(k), band(v)
    scale = HEAD_DIM ** -0.5
    s = jnp.einsum('bnqkgd,bnskd->bnkgqs', qb, kb).astype(jnp.float32) * scale

    qi = jnp.arange(BLOCK)[:, None] + BLOCK
    kj = jnp.arange(2 * BLOCK)[None, :]
    dist = qi - kj
    abs_k = jnp.arange(nb)[:, None, None] * BLOCK - BLOCK + kj[None]
    valid = (dist >= 0)[None] & (dist < WINDOW)[None] & (abs_k >= 0)

    slopes = jnp.exp2(-8.0 * jnp.arange(1, N_Q_HEADS + 1, dtype=jnp.float32) / N_Q_HEADS)
    slopes = slopes.reshape(N_KV_HEADS, GROUP)
    alibi = -slopes[:, :, None, None] * dist.astype(jnp.float32)[None, None]

    s = jnp.where(valid[None, :, None, None], s + alibi[None, None], -jnp.inf)
    sink = sinks.astype(jnp.float32).reshape(N_KV_HEADS, GROUP)[None, None, :, :, None, None]
    m = jnp.maximum(jnp.max(s, axis=-1, keepdims=True), sink)
    p = jnp.exp(s - m)
    denom = jnp.sum(p, axis=-1, keepdims=True) + jnp.exp(sink - m)
    p = (p / denom).astype(v.dtype)
    o = jnp.einsum('bnkgqs,bnskd->bnqkgd', p, vb)
    return o.reshape(bsz, seq, ATT_WIDTH)

def swa_layer(x, k, v, norm_g, w_in, q_norm_g, sinks, w_out):
    bsz, seq, _ = x.shape
    h = rmsnorm(x, norm_g)
    u = h @ w_in
    q, gate = u[..., :ATT_WIDTH], u[..., ATT_WIDTH:]
    q = rmsnorm(q.reshape(bsz, seq, N_Q_HEADS, HEAD_DIM), q_norm_g)
    o = sliding_window_sink_attention(q, k, v, sinks)
    y = o * jax.nn.silu(gate)
    return x + y @ w_out

def first_inputs(seed: int = 0) -> dict:
    key = jax.random.key(seed)
    ks = jax.random.split(key, 20)
    nA, nB, R, D = N_A_LAYERS, N_B_LAYERS, LRU_WIDTH, D_MODEL
    f32 = jnp.float32
    nrm = lambda k, shape, s: jax.random.normal(k, shape, f32) * s
    x = jax.random.normal(ks[0], (BATCH, SEQ, D), f32)
    a_norm_g = 1.0 + nrm(ks[1], (nA, D), 0.02)
    a_w_in = nrm(ks[2], (nA, D, 2 * R), D ** -0.5)
    a_conv_w = nrm(ks[3], (nA, CONV_WIDTH, R), CONV_WIDTH ** -0.5)
    a_conv_b = nrm(ks[4], (nA, R), 0.01)
    a_gate_r_w = nrm(ks[5], (nA, LRU_BLOCKS, LRU_BLOCK_W, LRU_BLOCK_W), LRU_BLOCK_W ** -0.5)
    a_gate_r_b = nrm(ks[6], (nA, R), 0.01)
    a_gate_i_w = nrm(ks[7], (nA, LRU_BLOCKS, LRU_BLOCK_W, LRU_BLOCK_W), LRU_BLOCK_W ** -0.5)
    a_gate_i_b = nrm(ks[8], (nA, R), 0.01)
    a8 = jax.random.uniform(ks[9], (nA, R), f32, 0.9, 0.999)
    a0 = a8 ** (1.0 / LRU_C)
    a_lambda = jnp.log(a0) - jnp.log1p(-a0)
    a_w_out = nrm(ks[10], (nA, R, D), R ** -0.5)
    kv_norm_g = 1.0 + nrm(ks[11], (D,), 0.02)
    w_kv = nrm(ks[12], (D, 2 * N_KV_HEADS * HEAD_DIM), D ** -0.5)
    k_norm_g = 1.0 + nrm(ks[13], (HEAD_DIM,), 0.02)
    b_norm_g = 1.0 + nrm(ks[14], (nB, D), 0.02)
    b_w_in = nrm(ks[15], (nB, D, 2 * ATT_WIDTH), D ** -0.5)
    q_norm_g = 1.0 + nrm(ks[16], (nB, HEAD_DIM), 0.02)
    sinks = nrm(ks[17], (nB, N_Q_HEADS), 0.5)
    b_w_out = nrm(ks[18], (nB, ATT_WIDTH, D), ATT_WIDTH ** -0.5)
    return {"x": x, "a_norm_g": a_norm_g, "a_w_in": a_w_in, "a_conv_w": a_conv_w,
            "a_conv_b": a_conv_b, "a_gate_r_w": a_gate_r_w, "a_gate_r_b": a_gate_r_b,
            "a_gate_i_w": a_gate_i_w, "a_gate_i_b": a_gate_i_b, "a_lambda": a_lambda,
            "a_w_out": a_w_out, "kv_norm_g": kv_norm_g, "w_kv": w_kv, "k_norm_g": k_norm_g,
            "b_norm_g": b_norm_g, "b_w_in": b_w_in, "q_norm_g": q_norm_g, "sinks": sinks,
            "b_w_out": b_w_out}

def first_block(x, a_norm_g, a_w_in, a_conv_w, a_conv_b, a_gate_r_w, a_gate_r_b,
              a_gate_i_w, a_gate_i_b, a_lambda, a_w_out, kv_norm_g, w_kv, k_norm_g,
              b_norm_g, b_w_in, q_norm_g, sinks, b_w_out):
    bsz, seq, _ = x.shape
    k = v = None
    for layer in range(DEPTH):
        if layer < N_A_LAYERS:
            l = layer
            x = rglru_layer(x, a_norm_g[l], a_w_in[l], a_conv_w[l], a_conv_b[l],
                            a_gate_r_w[l], a_gate_r_b[l], a_gate_i_w[l], a_gate_i_b[l],
                            a_lambda[l], a_w_out[l])
            if layer == N_A_LAYERS - 1:
                kv = rmsnorm(x, kv_norm_g) @ w_kv
                kv = kv.reshape(bsz, seq, 2, N_KV_HEADS, HEAD_DIM)
                k = rmsnorm(kv[:, :, 0], k_norm_g)
                v = kv[:, :, 1]
        else:
            l = layer - N_A_LAYERS
            x = swa_layer(x, k, v, b_norm_g[l], b_w_in[l], q_norm_g[l], sinks[l], b_w_out[l])
    return x


DEPTH_2 = 1

N_HEADS_MOBA = 8
N_HEADS_SB = 8
D_MOBA = N_HEADS_MOBA * HEAD_DIM
D_SB = N_HEADS_SB * HEAD_DIM
MOBA_BLOCK = 256
MOBA_TOP_K = 3
Q_CHUNK = 128
ROPE_THETA = 500000.0
ROPE_DIM = HEAD_DIM // 4
D_FF = 2816
FFN_RES = 0.5
D_IN = 3 * D_MOBA + 3 * D_SB + 2 * D_MODEL
NEG = -1e30


def rms_norm(x, g):
    x32 = x.astype(jnp.float32)
    y = x32 * lax.rsqrt(jnp.mean(x32 * x32, axis=-1, keepdims=True) + EPS)
    return y.astype(x.dtype) * g

def swiglu(x, w_gate, w_up, w_down):
    return (jax.nn.silu(x @ w_gate) * (x @ w_up)) @ w_down

def partial_rotary(x, positions):
    half = ROPE_DIM // 2
    inv_freq = ROPE_THETA ** (-jnp.arange(half, dtype=jnp.float32) * 2.0 / ROPE_DIM)
    ang = positions.astype(jnp.float32)[:, None, :, None] * inv_freq
    cos = jnp.cos(ang).astype(x.dtype)
    sin = jnp.sin(ang).astype(x.dtype)
    x1, x2, rest = x[..., :half], x[..., half:ROPE_DIM], x[..., ROPE_DIM:]
    return jnp.concatenate([x1 * cos - x2 * sin, x2 * cos + x1 * sin, rest], axis=-1)

def split_heads(x, n):
    b, t, _ = x.shape
    return x.reshape(b, t, n, HEAD_DIM).transpose(0, 2, 1, 3)

def merge_heads(x):
    b, h, t, d = x.shape
    return x.transpose(0, 2, 1, 3).reshape(b, t, h * d)

def moba_attention(q, k, v):
    B, H, T, hd = q.shape
    nb = -(-T // MOBA_BLOCK)
    pad = nb * MOBA_BLOCK - T
    k_pad = jnp.pad(k, ((0, 0), (0, 0), (0, pad), (0, 0)))
    v_pad = jnp.pad(v, ((0, 0), (0, 0), (0, pad), (0, 0)))
    kb = k_pad.reshape(B, H, nb, MOBA_BLOCK, hd)
    vb = v_pad.reshape(B, H, nb, MOBA_BLOCK, hd)
    k_mean = jnp.mean(kb.astype(jnp.float32), axis=3)
    k_sel = min(MOBA_TOP_K, nb)
    scale = hd ** -0.5
    bi = jnp.arange(B)[:, None, None, None]
    hi = jnp.arange(H)[None, :, None, None]
    offs = jnp.arange(MOBA_BLOCK)
    blk_ids = jnp.arange(nb)

    def chunk(c):
        start = c * Q_CHUNK
        qc = lax.dynamic_slice_in_dim(q, start, Q_CHUNK, axis=2)
        t = start + jnp.arange(Q_CHUNK)
        own = start // MOBA_BLOCK
        gate = jnp.einsum('bhqd,bhnd->bhqn', qc.astype(jnp.float32), k_mean)
        gate = jnp.where(blk_ids < own, gate, NEG)
        _, idx = lax.top_k(gate, k_sel)
        valid = idx < own
        ks = kb[bi, hi, idx]
        vs = vb[bi, hi, idx]
        s_sel = jnp.einsum('bhqd,bhqkld->bhqkl', qc, ks).astype(jnp.float32) * scale
        s_sel = jnp.where(valid[..., None], s_sel, NEG).reshape(B, H, Q_CHUNK, k_sel * MOBA_BLOCK)
        k_own = lax.dynamic_index_in_dim(kb, own, axis=2, keepdims=False)
        v_own = lax.dynamic_index_in_dim(vb, own, axis=2, keepdims=False)
        s_own = jnp.einsum('bhqd,bhld->bhql', qc, k_own).astype(jnp.float32) * scale
        pos_own = own * MOBA_BLOCK + offs
        s_own = jnp.where(pos_own[None, :] <= t[:, None], s_own, NEG)
        p = jax.nn.softmax(jnp.concatenate([s_sel, s_own], axis=-1), axis=-1).astype(v.dtype)
        p_sel = p[..., :k_sel * MOBA_BLOCK].reshape(B, H, Q_CHUNK, k_sel, MOBA_BLOCK)
        p_own = p[..., k_sel * MOBA_BLOCK:]
        return (jnp.einsum('bhqkl,bhqkld->bhqd', p_sel, vs)
                + jnp.einsum('bhql,bhld->bhqd', p_own, v_own))

    out = lax.map(chunk, jnp.arange(T // Q_CHUNK))
    return out.transpose(1, 2, 0, 3, 4).reshape(B, H, T, hd)

def stick_breaking_attention(q, k, v):
    B, H, T, hd = q.shape
    scale = hd ** -0.5
    s_pos = jnp.arange(T)

    def chunk(c):
        start = c * Q_CHUNK
        qc = lax.dynamic_slice_in_dim(q, start, Q_CHUNK, axis=2)
        t = start + jnp.arange(Q_CHUNK)
        z = jnp.einsum('bhqd,bhsd->bhqs', qc, k).astype(jnp.float32) * scale
        past = s_pos[None, :] < t[:, None]
        log_fail = jnp.where(past, jax.nn.log_sigmoid(-z), 0.0)
        later = lax.cumsum(log_fail, axis=3, reverse=True) - log_fail
        w = jnp.where(past, jnp.exp(jax.nn.log_sigmoid(z) + later), 0.0)
        return jnp.einsum('bhqs,bhsd->bhqd', w.astype(v.dtype), v)

    out = lax.map(chunk, jnp.arange(T // Q_CHUNK))
    return out.transpose(1, 2, 0, 3, 4).reshape(B, H, T, hd)

def hybrid_mixer(u, positions, w_in, b_gate, w_branch_moba, w_branch_sb, w_out):
    proj = u @ w_in
    cuts = [D_MOBA, 2 * D_MOBA, 3 * D_MOBA, 3 * D_MOBA + D_SB, 3 * D_MOBA + 2 * D_SB,
            3 * D_MOBA + 3 * D_SB, 3 * D_MOBA + 3 * D_SB + D_MODEL]
    q_a, k_a, v_a, q_b, k_b, v_b, g_a, g_b = jnp.split(proj, cuts, axis=-1)
    q_a = partial_rotary(split_heads(q_a, N_HEADS_MOBA), positions)
    k_a = partial_rotary(split_heads(k_a, N_HEADS_MOBA), positions)
    y_a = merge_heads(moba_attention(q_a, k_a, split_heads(v_a, N_HEADS_MOBA)))
    y_b = merge_heads(stick_breaking_attention(split_heads(q_b, N_HEADS_SB),
                                               split_heads(k_b, N_HEADS_SB),
                                               split_heads(v_b, N_HEADS_SB)))
    gates = jax.nn.sigmoid(jnp.concatenate([g_a, g_b], axis=-1) + b_gate)
    gate_a, gate_b = gates[..., :D_MODEL], gates[..., D_MODEL:]
    merged = gate_a * (y_a @ w_branch_moba) + gate_b * (y_b @ w_branch_sb)
    return merged @ w_out

def second_inputs(seed: int = 0) -> dict:
    key = jax.random.key(seed)
    ks = jax.random.split(key, 18)

    def w(k, shape, fan_in):
        return jax.random.normal(k, shape, jnp.float32) * fan_in ** -0.5

    def gain(k):
        return 1.0 + 0.05 * jax.random.normal(k, (DEPTH_2, D_MODEL), jnp.float32)

    return {
        "x": jax.random.normal(ks[0], (BATCH, SEQ, D_MODEL), jnp.float32),
        "positions": jnp.broadcast_to(jnp.arange(SEQ, dtype=jnp.int32), (BATCH, SEQ)),
        "ffn1_norm": gain(ks[1]),
        "ffn1_w_gate": w(ks[2], (DEPTH_2, D_MODEL, D_FF), D_MODEL),
        "ffn1_w_up": w(ks[3], (DEPTH_2, D_MODEL, D_FF), D_MODEL),
        "ffn1_w_down": w(ks[4], (DEPTH_2, D_FF, D_MODEL), D_FF),
        "mix_norm": gain(ks[5]),
        "w_in": w(ks[6], (DEPTH_2, D_MODEL, D_IN), D_MODEL),
        "b_gate": 0.02 * jax.random.normal(ks[7], (DEPTH_2, 2 * D_MODEL), jnp.float32),
        "w_branch_moba": w(ks[8], (DEPTH_2, D_MOBA, D_MODEL), D_MOBA),
        "w_branch_sb": w(ks[9], (DEPTH_2, D_SB, D_MODEL), D_SB),
        "w_out": w(ks[10], (DEPTH_2, D_MODEL, D_MODEL), D_MODEL),
        "ffn2_norm": gain(ks[11]),
        "ffn2_w_gate": w(ks[12], (DEPTH_2, D_MODEL, D_FF), D_MODEL),
        "ffn2_w_up": w(ks[13], (DEPTH_2, D_MODEL, D_FF), D_MODEL),
        "ffn2_w_down": w(ks[14], (DEPTH_2, D_FF, D_MODEL), D_FF),
        "final_norm": 1.0 + 0.05 * jax.random.normal(ks[15], (D_MODEL,), jnp.float32),
    }

def second_block(x, positions, ffn1_norm, ffn1_w_gate, ffn1_w_up, ffn1_w_down, mix_norm, w_in,
              b_gate, w_branch_moba, w_branch_sb, w_out, ffn2_norm, ffn2_w_gate, ffn2_w_up,
              ffn2_w_down, final_norm):
    h = x
    for l in range(DEPTH_2):
        h = h + FFN_RES * swiglu(rms_norm(h, ffn1_norm[l]), ffn1_w_gate[l], ffn1_w_up[l], ffn1_w_down[l])
        h = h + hybrid_mixer(rms_norm(h, mix_norm[l]), positions, w_in[l], b_gate[l],
                             w_branch_moba[l], w_branch_sb[l], w_out[l])
        h = h + FFN_RES * swiglu(rms_norm(h, ffn2_norm[l]), ffn2_w_gate[l], ffn2_w_up[l], ffn2_w_down[l])
    return rms_norm(h, final_norm)


def setup_inputs(seed=0):
    out = dict(first_inputs(seed))
    for name, value in second_inputs(seed + 1).items():
        if name != "x":
            out[name + "_2"] = value
    return out


def reference(
    x, a_norm_g, a_w_in, a_conv_w, a_conv_b, a_gate_r_w, a_gate_r_b, a_gate_i_w, a_gate_i_b,
    a_lambda, a_w_out, kv_norm_g, w_kv, k_norm_g, b_norm_g, b_w_in, q_norm_g, sinks, b_w_out,
    positions_2, ffn1_norm_2, ffn1_w_gate_2, ffn1_w_up_2, ffn1_w_down_2, mix_norm_2, w_in_2,
    b_gate_2, w_branch_moba_2, w_branch_sb_2, w_out_2, ffn2_norm_2, ffn2_w_gate_2, ffn2_w_up_2,
    ffn2_w_down_2, final_norm_2,
):
    x = first_block(
        x, a_norm_g, a_w_in, a_conv_w, a_conv_b, a_gate_r_w, a_gate_r_b, a_gate_i_w, a_gate_i_b,
        a_lambda, a_w_out, kv_norm_g, w_kv, k_norm_g, b_norm_g, b_w_in, q_norm_g, sinks,
        b_w_out,
    )
    return second_block(
        x, positions_2, ffn1_norm_2, ffn1_w_gate_2, ffn1_w_up_2, ffn1_w_down_2, mix_norm_2,
        w_in_2, b_gate_2, w_branch_moba_2, w_branch_sb_2, w_out_2, ffn2_norm_2, ffn2_w_gate_2,
        ffn2_w_up_2, ffn2_w_down_2, final_norm_2,
    )


_drawn_inputs = setup_inputs


def setup_inputs(seed=0):
    import zlib

    import numpy as np

    out = dict(_drawn_inputs(seed))
    spreads = {}
    factors = {'a_norm_g': 5.197,
     'a_gate_r_b': 8.0,
     'a_gate_i_b': 8.0,
     'kv_norm_g': 8.0,
     'k_norm_g': 8.0,
     'b_norm_g': 8.0,
     'q_norm_g': 8.0,
     'sinks': 41.343,
     'ffn1_norm_2': 21.744,
     'mix_norm_2': 21.824,
     'b_gate_2': 200.0,
     'ffn2_norm_2': 23.864}
    for name, (base, spread) in spreads.items():
        noise = np.random.default_rng([zlib.crc32(name.encode()), seed]).standard_normal(out[name].shape)
        drawn = base * np.exp(spread * noise) if base else spread * noise
        out[name] = __import__('jax').numpy.asarray(drawn.astype(out[name].dtype))
    for name, factor in factors.items():
        out[name] = (out[name] * factor).astype(out[name].dtype)
    return out
```

```python
from contextlib import ExitStack

import numpy as np

import concourse.bass as bass
from concourse import mybir

F32 = mybir.dt.float32
F32R = mybir.dt.float32r
I32 = mybir.dt.int32
ACT = mybir.ActivationFunctionType
ALU = mybir.AluOpType

P = 128
T = 256
TB = T // P
D = 1024
KD = D // P
LRU = 1536
LT = LRU // P
LB = 96
LG = 4
CONV = 4
LRU_C = 8.0
HD = 64
NQ = 16
NH = 8
DFF = 2816
FT = DFF // P
EPS = 1e-6
SCALE = HD ** -0.5
FFN_RES = 0.5
SLOPES = [float(np.float32(2.0 ** (-8.0 * (h + 1) / NQ))) for h in range(NQ)]
SC = T + P
BIG = 1e30
TWO_PI = 2.0 * np.pi
ROUND = 1.5 * 2.0 ** 23
TURN_1 = 6.28125
TURN_2 = float(np.float32(np.round((TWO_PI - TURN_1) * 2.0 ** 19) / 2.0 ** 19))
TURN_PARTS = [TURN_1, TURN_2, TWO_PI - TURN_1 - TURN_2]
PI_LOW = float(np.nextafter(np.float32(np.pi), np.float32(0)))

HALF = 4 * T
RING = 4
GATE_COLS = 896
GATE_TILES = [(0, 0, 0), (1, 0, 256), (0, 1, 128), (1, 1, 384), (2, 1, 640), (1, 2, 512), (2, 2, 768)]
GATE_PIECES = [(0, 0, 96, 0, 0), (1, 0, 32, 96, 96), (1, 32, 64, 0, 256 + 96),
               (2, 0, 64, 64, 256 + 192), (2, 64, 32, 0, 640 + 64), (3, 0, 96, 32, 640 + 160)]

C_X, C_G, C_AO, C_KV, C_Q, C_BG, C_BO, C_F1, C_D1 = 0, 6, 12, 18, 19, 23, 27, 31, 53
C_MIX, C_BR, C_WO, C_F2, C_D2, C_END = 64, 84, 88, 92, 114, 125
H_RI = 2 * C_G


def half_of(chunk):
    return 2 * chunk + (2 * LG if chunk >= C_G else 0)


A_NORM, CONV_W, CONV_B, BR, BI, LAM = 0, 8, 56, 68, 80, 92
ROWS_A = 104
KV_G, B_G, F1_G, MIX_G, F2_G, FIN_G, B_GATE, K_G, Q_G, FREQ = 0, 8, 16, 24, 32, 40, 48, 64, 65, 66
ROWS_B = 67

IDENT, PERM, TRI, E0, E1, DIST, CMASK, SBMASK, BLK2 = 0, 128, 256, 384, 512, 640, 896, 1152, 1536
N_CONST = 1538


def constants():
    c = np.zeros((P, N_CONST), np.float32)
    p = np.arange(P)[:, None]
    j = np.arange(P)[None, :]
    c[:, IDENT:IDENT + P] = p == j
    same = p // HD == j // HD
    c[:, PERM:PERM + P] = same * (1.0 * ((p % HD == j % HD - 8) & (j % HD < 16) & (j % HD >= 8))
                                  - 1.0 * ((p % HD == j % HD + 8) & (j % HD < 8)))
    c[:, TRI:TRI + P] = p >= j
    c[:, E0:E0 + P] = p == j % HD
    c[:, E1:E1 + P] = p == HD + j % HD
    k = np.arange(T)[None, :]
    dist = P + p - k
    c[:, DIST:DIST + T] = np.where((dist >= 0) & (dist < P), dist, np.float32(1e33))
    c[:, CMASK:CMASK + T] = np.where(dist >= 0, 0.0, -BIG)
    past = np.where(p < j, 0.0, -BIG)
    c[:, SBMASK:SBMASK + P] = past
    c[:, SBMASK + T:SBMASK + SC] = past
    c[:, BLK2] = np.arange(P) < HD
    c[:, BLK2 + 1] = np.arange(P) >= HD
    freq = np.zeros((1, P), np.float32)
    half = np.float32(500000.0) ** (-np.arange(8, dtype=np.float32) * np.float32(2.0) / np.float32(16))
    for h in range(2):
        freq[0, h * HD:h * HD + 8] = half
        freq[0, h * HD + 8:h * HD + 16] = half
    return c, freq


def build(nc, I, out):
    ctx = ExitStack()
    with ctx:
        def sb(name, shape, dt=F32):
            return ctx.enter_context(nc.sbuf_tensor(name, shape, dt))

        def sem(name):
            return ctx.enter_context(nc.semaphore(name))

        stage = sb("stage", [P, 2, 2, HALF])
        w_hi = sb("w_hi", [P, RING, HALF], F32R)
        w_lo = sb("w_lo", [P, RING, HALF], F32R)
        gate_st = sb("gate_st", [P, 2, 2, GATE_COLS])
        xres = sb("xres", [P, KD, T])
        a_hi = sb("a_hi", [P, 30, T], F32R)
        a_lo = sb("a_lo", [P, 30, T], F32R)
        arena = sb("arena", [P, 62, T])
        rows_a = sb("rows_a", [ROWS_A, P])
        rows_b = sb("rows_b", [ROWS_B, P])
        par_a = sb("par_a", [P, ROWS_A])
        par_b = sb("par_b", [P, ROWS_B])
        con = sb("con", [P, N_CONST])
        ones = sb("ones", [P, P])
        eps = sb("eps", [P, 1])
        pos = sb("pos", [P, T], I32)
        sink = sb("sink", [P, NQ])
        cosine = sb("cosine", [P, T])
        sine = sb("sine", [P, T])
        half_pi = sb("half_pi", [P, 1])
        q_gain = sb("q_gain", [P, 1])
        lam = sb("lam", [P, 8, LT])
        std = sb("std", [P, 8])
        rstd = sb("rstd", [P, 8])
        top = sb("top", [P, 2 * (NQ + NH)])
        ntop = sb("ntop", [P, 2 * (NQ + NH)])
        rsum = sb("rsum", [P, 2 * (NQ + NH)])
        esink = sb("esink", [P, 2 * (NQ + NH)])
        rden = sb("rden", [P, 2 * (NQ + NH)])
        bank = [ctx.enter_context(nc.psum_tensor(f"bank{b}", [P, 512], F32)) for b in range(8)]

        def tiles(t, n=1):
            return arena[:, t:t + n, :].rearrange("p t n -> p (t n)")

        flat = arena[:, :, :].rearrange("p t n -> p (t n)")
        SQ, XNF = 24, 32
        XB, GATE, RR, II, AA = 0, 12, 24, 36, 48

        gate_hi = tiles(AA, 14).rearrange("p (g w n) -> p g w n", g=2, w=2)


        x_in, con_in, rows_a_in, rows_b_in = sem("x_in"), sem("con_in"), sem("rows_a_in"), sem("rows_b_in")
        pos_in, sink_in, id_in = sem("pos_in"), sem("sink_in"), sem("id_in")
        stage_in = [sem("stage_in0"), sem("stage_in1")]
        gate_in = [sem("gate_in0"), sem("gate_in1")]
        set_done = sem("set_done")
        hi_done, w_done, ring_free = sem("hi_done"), sem("w_done"), sem("ring_free")
        acc_done, x_ready, sq_ready, ms_ready = sem("acc_done"), sem("x_ready"), sem("sq_ready"), sem("ms_ready")
        std_ready, rstd_ready, rb_ready = sem("std_ready"), sem("rstd_ready"), sem("rb_ready")
        xn_ready, xh_ready, xl_ready = sem("xn_ready"), sem("xh_ready"), sem("xl_ready")
        par_t, par_ready, lam_e, lam_step, lam_ready = (
            sem(n) for n in ("par_t", "par_ready", "lam_e", "lam_step", "lam_ready"))
        conv_b, conv_s, conv_x, xbh, xbl = sem("conv_b"), sem("conv_s"), sem("conv_x"), sem("xbh"), sem("xbl")
        ri_sig = sem("ri_sig")
        lru_a, lru_t, lru_aa, lru_m, lru_s, lru_bx, lru_b, lru_h, lru_silu = (
            sem(n) for n in ("lru_a", "lru_t", "lru_aa", "lru_m", "lru_s", "lru_bx", "lru_b", "lru_h", "lru_silu"))
        gate_raw, y_f, y_hi, y_lo = sem("gate_raw"), sem("y_f"), sem("y_hi"), sem("y_lo")
        qg_ready = sem("qg_ready")
        q_raw, hn_sq, hn_ms, hn_std, hn_rstd, hn_rb, hn_done = (
            sem(n) for n in ("q_raw", "hn_sq", "hn_ms", "hn_std", "hn_rstd", "hn_rb", "hn_done"))
        kdup_ps, kdup_ready = sem("kdup_ps"), sem("kdup_ready")
        bias_ready, s_done, s_max, s_neg, p_exp, den_sum, den_inv, p_norm, t_done, t_out, o_done, o_out = (
            sem(n) for n in ("bias_ready", "s_done", "s_max", "s_neg", "p_exp", "den_sum", "den_inv", "p_norm",
                             "t_done", "t_out", "o_done", "o_out"))
        silu_b, yb_f, yb_hi, yb_lo = sem("silu_b"), sem("yb_f"), sem("yb_hi"), sem("yb_lo")
        ff_silu, ff_f, ff_hi, ff_lo = sem("ff_silu"), sem("ff_f"), sem("ff_hi"), sem("ff_lo")
        trig_s, trig_r, trig_abs, trig_ready = sem("trig_s"), sem("trig_r"), sem("trig_abs"), sem("trig_ready")
        m_raw, rope_p, rope_a, rope_done = sem("m_raw"), sem("rope_p"), sem("rope_a"), sem("rope_done")
        z_done, z_sb, sb_abs, sb_exp, sb_ln, sp_done, c_done, d_done, w_exp = (
            sem(n) for n in ("z_done", "z_sb", "sb_abs", "sb_exp", "sb_ln", "sp_done", "c_done", "d_done", "w_exp"))
        ym_hi, ym_lo, g_sig = sem("ym_hi"), sem("ym_lo"), sem("g_sig")
        br_done, mg_a, mg_b, mg_f, mg_hi, mg_lo = (
            sem(n) for n in ("br_done", "mg_a", "mg_b", "mg_f", "mg_hi", "mg_lo"))
        fin_t, fin_sb, out_done = sem("fin_t"), sem("fin_sb"), sem("out_done")

        def source(n):
            if H_RI <= n < H_RI + 2 * LG:
                g, w = divmod(n - H_RI, 2)
                return (gate_st, gate_hi)[g // 2][:, g % 2, w, :], gate_in[g // 2], 16 * 2 * len(GATE_PIECES)
            chunk = (n if n < H_RI else n - 2 * LG) // 2
            return stage[:, chunk % 2, n % 2, :], stage_in[chunk % 2], 16 * (chunk // 2 + 1)

        def wide(t3):
            return t3.rearrange("p t n -> p (t n)")

        def score_buf(n):
            return flat[:, 24 * T + (n % 3) * SC:24 * T + (n % 3 + 1) * SC]

        def prob_t(n):
            return flat[:, 29 * T + (n % 2) * SC:29 * T + (n % 2 + 1) * SC]

        def stick_z(n):
            return flat[:, 24 * T + (n % 5) * SC:24 * T + (n % 5 + 1) * SC]

        def stick_sp(n):
            return flat[:, 56 * T + (n % 2) * SC:56 * T + (n % 2 + 1) * SC]

        def stick_ln(n):
            return flat[:, 48 * T + (n % 3) * SC:48 * T + (n % 3 + 1) * SC]

        ident = con[:, IDENT:IDENT + P]
        GAINS = [par_a[:, A_NORM:A_NORM + KD]] + [par_b[:, g:g + KD] for g in (KV_G, B_G, F1_G, MIX_G, F2_G, FIN_G)]

        block = ctx.enter_context(nc.Block())

        @block.sync
        def _(sp):
            xt = I["x"].rearrange("o (b p) d -> p (o b) d", p=P)
            sp.dma_start(tiles(0, 8).rearrange("p (b d) -> p b d", b=TB), xt).then_inc(x_in, 16)

            def load(chunk, src, first=None):
                if first is not None:
                    sp.wait_ge(w_done, first)
                dst = stage[:, chunk % 2, :, :]
                sp.dma_start(dst.rearrange("p a (b n) -> p (a b) n", n=src.shape[-1]), src)\
                  .then_inc(stage_in[chunk % 2], 16)

            def col(w, j):
                return w.rearrange("(k p) n -> p k n", p=P)[:, :, bass.ds(j * T, T)]

            def row(w, j):
                return w[bass.ds(j * T, T), :].rearrange("(k p) n -> p k n", p=P)

            def split(chunk):
                return half_of(chunk) + 2

            def stream(chunk, n, view):
                j = 0
                while j < n and (j + chunk < 2 or (j + chunk) - 2 < C_G <= (j + chunk) + 1):
                    load(chunk + j, view(j), split(chunk + j - 2) if chunk + j >= 2 else None)
                    j += 1
                turns = (n - j) // 2
                if turns > 1:
                    base = split(chunk + j - 2)
                    with sp.Fori(0, turns) as i:
                        for b in range(2):
                            load(chunk + j + b, view(i * 2 + (j + b)), base + 2 * b + i * 4)
                    j += 2 * turns
                for r in range(j, n):
                    load(chunk + r, view(r), split(chunk + r - 2))

            def pairs(chunk, wa, wb):
                base = split(chunk - 2)
                with sp.Fori(0, DFF // T) as i:
                    load(chunk, col(wa, i), base + i * 4)
                    load(chunk + 1, col(wb, i), base + 2 + i * 4)

            w_in, w_out = I["a_w_in"][0], I["a_w_out"][0]
            stream(C_X, 6, lambda j: col(w_in, j))
            stream(C_G, 6, lambda j: col(w_in, j + 6))
            stream(C_AO, 6, lambda j: row(w_out, j))
            stream(C_KV, 1, lambda j: col(I["w_kv"], j))
            stream(C_Q, 8, lambda j: col(I["b_w_in"][0], j))
            stream(C_BO, 4, lambda j: row(I["b_w_out"][0], j))
            pairs(C_F1, I["ffn1_w_gate_2"][0], I["ffn1_w_up_2"][0])
            stream(C_D1, 11, lambda j: row(I["ffn1_w_down_2"][0], j))
            stream(C_MIX, 20, lambda j: col(I["w_in_2"][0], j))
            stream(C_BR, 2, lambda j: row(I["w_branch_moba_2"][0], j))
            stream(C_BR + 2, 2, lambda j: row(I["w_branch_sb_2"][0], j))
            stream(C_WO, 4, lambda j: row(I["w_out_2"][0], j))
            pairs(C_F2, I["ffn2_w_gate_2"][0], I["ffn2_w_up_2"][0])
            stream(C_D2, 11, lambda j: row(I["ffn2_w_down_2"][0], j))

            o = out.rearrange("o (b p) (h n) -> (o b) h p n", p=P, h=2)
            for q, (half, b) in enumerate([(0, 0), (0, 1), (1, 0), (1, 1)]):
                sp.wait_ge(fin_sb, q + 1)
                sp.dma_start(o[b, half], tiles(8 + 2 * q, 2)).then_inc(out_done, 16)
            sp.wait_ge(out_done, 64)

        @block.gpsimd
        def _(pool):
            pool.dma_start(ident, I["constants"][:, IDENT:IDENT + P]).then_inc(id_in, 16)
            for first, name, n in ((A_NORM, "a_norm_g", KD), (CONV_B, "a_conv_b", LT), (BR, "a_gate_r_b", LT),
                                   (BI, "a_gate_i_b", LT), (LAM, "a_lambda", LT)):
                pool.dma_start(rows_a[first:first + n, :], I[name].rearrange("o (k p) -> (o k) p", p=P))\
                    .then_inc(rows_a_in, 16)
            pool.dma_start(rows_a[CONV_W:CONV_W + CONV * LT, :],
                           I["a_conv_w"].rearrange("o c (k p) -> (o c k) p", p=P)).then_inc(rows_a_in, 16)
            pool.memset(ones[:, :], 1.0).then_inc(set_done, 1)
            pool.memset(eps[:, :], EPS).then_inc(set_done, 1)
            pool.memset(half_pi[:, :], float(np.pi / 2)).then_inc(set_done, 1)
            pool.memset(gate_st[:, :, :, :], 0.0).then_inc(set_done, 1)
            pool.memset(tiles(AA, 14), 0.0).then_inc(set_done, 1)

            for pair, place in enumerate((gate_st, gate_hi)):
                pool.wait_ge(set_done, 4 + pair)
                for w, name in enumerate(("a_gate_r_w", "a_gate_i_w")):
                    blocks = I[name][0].rearrange("(g b) i j -> b i g j", b=4)
                    for b, r, n, p, c in GATE_PIECES:
                        pool.dma_start(place[p:p + n, :, w, c:c + LB], blocks[b, r:r + n, 2 * pair:2 * pair + 2, :])\
                            .then_inc(gate_in[pair], 16)
            for first, name, n in ((F1_G, "ffn1_norm_2", KD), (MIX_G, "mix_norm_2", KD), (F2_G, "ffn2_norm_2", KD),
                                   (B_GATE, "b_gate_2", 2 * KD), (B_G, "b_norm_g", KD)):
                pool.dma_start(rows_b[first:first + n, :], I[name].rearrange("o (k p) -> (o k) p", p=P))\
                    .then_inc(rows_b_in, 16)
            for first, name in ((KV_G, "kv_norm_g"), (FIN_G, "final_norm_2")):
                pool.dma_start(rows_b[first:first + KD, :], I[name].rearrange("(k p) -> k p", p=P))\
                    .then_inc(rows_b_in, 16)
            for h in range(2):
                pool.dma_start(rows_b[K_G:K_G + 1, h * HD:(h + 1) * HD], I["k_norm_g"].rearrange("(o d) -> o d", o=1))\
                    .then_inc(rows_b_in, 16)
                pool.dma_start(rows_b[Q_G:Q_G + 1, h * HD:(h + 1) * HD], I["q_norm_g"]).then_inc(rows_b_in, 16)
            pool.dma_start(rows_b[FREQ:FREQ + 1, :], I["freq"]).then_inc(rows_b_in, 16)
            pool.dma_start(con[:, P:N_CONST], I["constants"][:, P:N_CONST]).then_inc(con_in, 16)
            pool.dma_start(pos[:, :], I["positions_2"].to_broadcast([P, T])).then_inc(pos_in, 16)
            pool.dma_start(sink[:, :], I["sinks"].to_broadcast([P, NQ])).then_inc(sink_in, 16)
            pool.wait_ge(xbl, 6)
            for g in range(LG):
                pool.wait_ge(ri_sig, 2 * g + 2)
                pool.tensor_tensor(tiles(II + 3 * g, 3), tiles(II + 3 * g, 3), tiles(XB + 3 * g, 3), ALU.mult)\
                    .then_inc(lru_bx, 1)
            for g in range(LG):
                pool.wait_ge(lru_a, g + 1)
                pool.wait_ge(lru_bx, g + 1)
                pool.tensor_tensor(tiles(XB + 3 * g, 3), tiles(AA + 3 * g, 3), tiles(AA + 3 * g, 3), ALU.mult)\
                    .then_inc(lru_aa, 1)
            pool.wait_ge(con_in, 16)
            for h in range(NQ):
                if h >= 3:
                    pool.wait_ge(s_max, 2 * (h - 2))
                else:
                    pool.wait_ge(hn_done, 5)
                pool.tensor_scalar(tiles(53 + h % 3), con[:, DIST:DIST + T], -SLOPES[h], 1.0, ALU.mult, ALU.mult)\
                    .then_inc(bias_ready, 1)

        @block.tensor
        def _(pe):
            SPLIT = ((w_hi, a_hi), (w_hi, a_lo), (w_lo, a_hi))

            def passes(dst, slot, c, k, start, stop):
                for n, (w, a) in enumerate(SPLIT):
                    mm = pe.matmul(dst, w[:, slot, c:c + P],
                                   a[:, k, :] if isinstance(k, int) else wide(a[:, bass.ds(k, 1), :]),
                                   start=start and n == 0, stop=stop and n == 2, skip_group_check=True)
                return mm

            def by_token(dst, slot, c, n, k, tb, start, stop):
                for i, (w, a) in enumerate(SPLIT):
                    mm = pe.matmul(dst, a[:, k, tb * P:(tb + 1) * P], w[:, slot, c:c + n],
                                   start=start and i == 0, stop=stop and i == 2, skip_group_check=True)
                return mm

            def col_half(chunk, h, b, first_tile=0, normed=None, ready=None, token=()):
                half = half_of(chunk) + h
                pe.wait_ge(w_done, half + 1 if ready is None else ready)
                for kk in range(4):
                    k = 4 * h + kk
                    if normed is not None:
                        pe.wait_ge(xl_ready, KD * normed + k + 1)
                    if len(token) == 2:
                        for tb in range(TB):
                            mm = by_token(bank[b][:, tb * T:(tb + 1) * T], half % RING, kk * T, T,
                                          first_tile + k, tb, k == 0 and tb == 0, k == KD - 1)
                        continue
                    for m in range(2):
                        if m in token:
                            for tb in range(TB):
                                c = m * T + tb * P
                                mm = by_token(bank[b][:, c:c + P], half % RING, kk * T + m * P, P,
                                              first_tile + k, tb, False, k == KD - 1)
                        else:
                            mm = passes(bank[b][:, m * T:(m + 1) * T], half % RING, kk * T + m * P,
                                        first_tile + k, k == 0 and m == 0, k == KD - 1)
                mm.then_inc(ring_free, 1)

            def col_chunk(chunk, b, **kw):
                for h in range(2):
                    col_half(chunk, h, b, **kw)

            def row_half(chunk, h, k, acc=0, first=False, last=None, ready=None):
                half = half_of(chunk) + h
                pe.wait_ge(w_done, half + 1 if ready is None else ready)
                for m in range(KD):
                    mm = passes(bank[acc + m // 2][:, (m % 2) * T:(m % 2 + 1) * T], half % RING, m * P, k,
                                first and m % 2 == 0, last is not None)
                    if last is not None and m in (1, 3, 5):
                        mm.then_inc(last, 1)
                mm.then_inc(ring_free, 1)

            def norm(n):
                for b in range(4):
                    pe.wait_ge(sq_ready, 4 * n + b + 1)
                    for k in (2 * b, 2 * b + 1):
                        for tb in range(TB):
                            mm = pe.matmul(bank[7][:, tb:tb + 1], tiles(SQ + k)[:, tb * P:(tb + 1) * P],
                                           ones[:, 0:1], start=k == 0 and tb == 0, stop=k == KD - 1,
                                           skip_group_check=True)
                mm.then_inc(ms_ready, 1)
                pe.wait_ge(rstd_ready, n + 1)
                for tb in range(TB):
                    mm = pe.matmul(bank[6][:, tb * P:(tb + 1) * P], rstd[:, tb:tb + 1].to_broadcast([P, P]),
                                   ident, start=True, stop=True)
                mm.then_inc(rb_ready, 1)

            pe.wait_ge(id_in, 16)
            pe.wait_ge(x_in, 16)
            xtok = tiles(0, 8).rearrange("p (b d) -> p b d", b=TB)
            for m in range(KD):
                for tb in range(TB):
                    c = (m % 2) * T + tb * P
                    mm = pe.transpose(bank[m // 2][:, c:c + P], xtok[:, tb, m * P:(m + 1) * P], ident)
                if m % 2:
                    mm.then_inc(acc_done, 1)
            pe.wait_ge(rows_a_in, 16 * 6)
            pe.transpose(bank[5][:, 0:ROWS_A], rows_a[:, :], con[0:ROWS_A, IDENT:IDENT + ROWS_A]).then_inc(par_t, 1)
            pe.wait_ge(set_done, 2)
            norm(0)

            for c in range(6):
                if c == 1:
                    pe.wait_ge(par_ready, 1)
                if c >= 2:
                    pe.wait_ge(conv_x, 2 * (c - 1))
                col_chunk(C_X + c, 4 + c % 2, normed=0)

            for g in range(LG):
                for gate in range(2):
                    half = H_RI + 2 * g + gate
                    pe.wait_ge(w_done, half + 1)
                    if gate == 0:
                        pe.wait_ge(xbl, (3 * g + 2) // 2 + 1)
                    if g == 1:
                        pe.wait_ge(conv_x, LT)
                    if g >= 2:
                        pe.wait_ge(ri_sig, 2 * (g - 2) + gate + 1)
                    done = [0, 0, 0]
                    for k, m, c in GATE_TILES:
                        b = bank[4 * (g % 2) + 2 * gate + m // 2]
                        done[m] += 1
                        mm = passes(b[:, (m % 2) * T:(m % 2 + 1) * T], half % RING, c, 8 + 3 * g + k,
                                    done[m] == 1 and m != 1, done[m] == (2, 3, 2)[m])
                    mm.then_inc(ring_free, 1)

            pe.wait_ge(ri_sig, 2 * LG)
            pe.wait_ge(rows_b_in, 16 * 12)
            pe.transpose(bank[6][:, 0:ROWS_B], rows_b[:, :], con[0:ROWS_B, IDENT:IDENT + ROWS_B]).then_inc(par_t, 1)
            for c in range(6):
                if c >= 2:
                    pe.wait_ge(gate_raw, c - 1)
                col_chunk(C_G + c, 4 + c % 2)
            for c in range(6):
                for h in range(2):
                    pe.wait_ge(y_lo, (2 * c + h) // 3 + 1)
                    row_half(C_AO + c, h, 8 + 2 * c + h, first=c == 0 and h == 0,
                             last=acc_done if c == 5 and h == 1 else None)
            norm(1)

            def head_squares(n):
                pe.wait_ge(hn_sq, n + 1)
                for c in range(TB if n == 0 else 2 * TB):
                    sq = tiles(49 + 2 * (n % 2), 2)[:, c * P:(c + 1) * P]
                    mm = pe.matmul(bank[7][:, 2 * c:2 * c + 2], sq, con[:, BLK2:BLK2 + 2], start=True, stop=True)
                mm.then_inc(hn_ms, 1)

            def head_roots(n):
                pe.wait_ge(hn_rstd, n + 1)
                if n:
                    pe.wait_ge(hn_done, n)
                for c in range(TB if n == 0 else 2 * TB):
                    for h in range(2):
                        spread = rstd[:, 2 * c + h:2 * c + h + 1].to_broadcast([P, HD])
                        mm = pe.matmul(bank[6][h * HD:(h + 1) * HD, c * P:(c + 1) * P], spread, ident, start=True, stop=True)
                mm.then_inc(hn_rb, 1)

            pe.wait_ge(con_in, 16)
            col_chunk(C_KV, 4, first_tile=8, normed=1, token=(1,))
            for s in range(1, 6):
                if s >= 2:
                    pe.wait_ge(q_raw, s - 1)
                col_half(C_KV + s, 0, 4 + s % 2, normed=2 if s == 1 else None)
                head_squares(s - 1)
                col_half(C_KV + s, 1, 4 + s % 2, normed=2 if s == 1 else None)
                head_roots(s - 1)
            for j in range(2):
                mm = pe.matmul(bank[2][:, j * T:(j + 1) * T], con[:, E0 + j * P:E0 + (j + 1) * P], tiles(40),
                               start=True, stop=True)
            mm.then_inc(kdup_ps, 1)
            pe.wait_ge(kdup_ready, 1)
            pe.wait_ge(hn_done, 5)

            def scores(n, q, k, hrow, t):
                if n >= 2:
                    pe.wait_ge(s_max, 2 * (n - 1))
                r = slice(hrow * HD, (hrow + 1) * HD)
                s = bank[n % 2]
                pe.matmul(s[:, 0:P], q[r, t * T:t * T + P], k[r, 0:P], start=True, stop=True)
                pe.matmul(s[:, P:SC], q[r, t * T + P:(t + 1) * T], k[r, 0:T], start=True, stop=True)\
                    .then_inc(s_done, 1)

            def turn(n):
                pe.wait_ge(p_norm, n + 1)
                if n >= 2:
                    pe.wait_ge(t_out, n - 1)
                p = score_buf(n)
                for c in range(3):
                    mm = pe.transpose(bank[2 + n % 2][:, c * P:(c + 1) * P], p[:, c * P:(c + 1) * P], ident)
                mm.then_inc(t_done, 1)

            def values(n, o, v, w):
                r = (n % 2) * HD
                dst = bank[o][r:r + HD, (n // 2 % 2) * T:(n // 2 % 2 + 1) * T]
                pe.matmul(dst, v[0], w[:, 0:T], start=True, stop=False, skip_group_check=True)
                pe.matmul(dst[:, P:T], v[1], w[:, T:SC], start=False, stop=True, skip_group_check=True)\
                    .then_inc(o_done, 1)

            vt = tiles(44)
            for r in range(NQ + 3):
                if r < NQ:
                    scores(r, tiles(0, 8), tiles(41 + r // 8), r % 2, r // 2)
                if 2 <= r < NQ + 2:
                    turn(r - 2)
                if r >= 3:
                    n = r - 3
                    pe.wait_ge(t_out, n + 1)
                    if n % 4 == 0 and n >= 8:
                        pe.wait_ge(o_out, n // 4 - 1)
                    kv = n // 8 * HD
                    values(n, 6 + (n // 4) % 2, [vt[:, tb * P + kv:tb * P + kv + HD] for tb in range(TB)], prob_t(n))
                if r % 3 == 1 and r < 18:
                    s, h = 6 + r // 6, r // 3 % 2
                    if h == 0:
                        pe.wait_ge(q_raw, s - 1)
                    col_half(C_KV + s, h, 4 + s % 2)
            pe.wait_ge(t_out, NQ)
            for c in range(4):
                pe.wait_ge(yb_lo, c + 1)
                for h in range(2):
                    row_half(C_BO + c, h, 8 + 2 * c + h, first=c == 0 and h == 0,
                             last=acc_done if c == 3 and h == 1 else None)
            norm(2)

            def ffn(n, c_pair, c_down, normed):
                first = n * (FT // 2)

                def pair(j, i=0, normed=None):
                    if j >= 2:
                        pe.wait_ge(ff_f, first + j - 1 + i * 2)
                    for u in range(2):
                        for h in range(2):
                            half = half_of(c_pair) + 4 * j + 2 * u + h
                            col_half(c_pair + u, h, 4 + 2 * (j % 2) + u, normed=normed if u == 0 else None,
                                     ready=half + 1 + i * 8)

                pair(0, normed=normed)
                pair(1)
                pair(2)
                with pe.Fori(0, (FT // 2 - 3) // 2) as i:
                    pair(3, i)
                    pair(4, i)
                for c in range(2):
                    pe.wait_ge(ff_lo, first + c + 1)
                    for h in range(2):
                        row_half(c_down + c, h, 8 + 2 * c + h, first=c == 0 and h == 0)
                base = half_of(c_down)
                with pe.Fori(0, 4) as i:
                    for c in range(2):
                        pe.wait_ge(ff_lo, i * 2 + (first + c + 3))
                        for h in range(2):
                            row_half(c_down + c, h, i * 4 + (12 + 2 * c + h), ready=i * 4 + (base + 5 + 2 * c + h))
                pe.wait_ge(ff_lo, first + 11)
                row_half(c_down + 10, 0, 8 + 20)
                row_half(c_down + 10, 1, 8 + 21, last=acc_done)

            ffn(0, C_F1, C_D1, normed=3)
            norm(3)

            for c in range(12):
                if c >= 2:
                    pe.wait_ge(m_raw, c - 1)
                col_chunk(C_MIX + c, 4 + c % 2, normed=4 if c == 0 else None, token=(0, 1) if c in (4, 5, 10, 11) else ())
                if c in (1, 2, 3, 4):
                    n = c - 1
                    pe.wait_ge(m_raw, n + 1)
                    if n >= 1:
                        pe.wait_ge(rope_done, n)
                    pe.matmul(bank[6][:, :], con[:, PERM:PERM + P], tiles(48 + 2 * (n % 2), 2), start=True, stop=True)\
                        .then_inc(rope_p, 1)
            pe.wait_ge(m_raw, 12)
            pe.wait_ge(rope_done, 4)

            def g_half(j):
                c, h = divmod(j, 2)
                if h == 0:
                    pe.wait_ge(m_raw, 12 + c - 1)
                col_half(C_MIX + 12 + c, h, 4 + c % 2)

            v = tiles(16, 4)
            for r in range(NH + 3):
                n = NQ + r
                if r < NH:
                    scores(n, tiles(0, 4), tiles(4 + r // 2), r % 2, r // 2)
                if 2 <= r < NH + 2:
                    turn(n - 2)
                if r >= 3:
                    h = r - 3
                    pe.wait_ge(t_out, NQ + h + 1)
                    values(NQ + h, 6 + h // 4, [v[:, tb * 512 + h * HD:tb * 512 + (h + 1) * HD] for tb in range(TB)],
                           prob_t(NQ + h))
                if 1 <= r <= 8:
                    g_half(r - 1)
            pe.wait_ge(t_out, NQ + NH)
            pe.wait_ge(s_max, 2 * (NQ + NH))
            v = tiles(20, 4)
            for r in range(NH + 4):
                if r < NH:
                    if r >= 2:
                        pe.wait_ge(z_sb, r - 1)
                    q, k, z = tiles(8 + r // 2), tiles(12 + r // 2), bank[r % 2]
                    s = slice((r % 2) * HD, (r % 2 + 1) * HD)
                    pe.matmul(z[:, 0:T], k[s, 0:P], q[s, 0:T], start=True, stop=True)
                    pe.matmul(z[:, T:SC], k[s, P:T], q[s, P:T], start=True, stop=True).then_inc(z_done, 1)
                if 2 <= r < NH + 2:
                    n = r - 2
                    pe.wait_ge(sp_done, n + 1)
                    if n >= 2:
                        pe.wait_ge(d_done, n - 1)
                    sums, sp_n = bank[2 + n % 2], stick_sp(n)
                    pe.matmul(sums[:, 0:SC], con[:, TRI:TRI + P], sp_n, start=True, stop=False, skip_group_check=True)
                    pe.matmul(sums[:, P:T], ones[:, :], sp_n[:, T:SC], start=False, stop=True, skip_group_check=True)\
                        .then_inc(c_done, 1)
                if r >= 4:
                    h = r - 4
                    pe.wait_ge(w_exp, h + 1)
                    if h % 4 == 0:
                        pe.wait_ge(ym_lo, h // 4 + 1)
                    values(h, 6 + h // 4, [v[:, tb * 512 + h * HD:tb * 512 + (h + 1) * HD] for tb in range(TB)], stick_z(h))
                if 1 <= r <= 8:
                    g_half(7 + r)
            pe.wait_ge(d_done, NH)
            for c in range(2):
                for h in range(2):
                    row_half(C_BR + c, h, 8 + 2 * c + h, first=c == 0 and h == 0, last=br_done if c and h else None)
            pe.wait_ge(m_raw, 20)
            pe.wait_ge(ym_lo, 4)
            for c in range(2):
                for h in range(2):
                    row_half(C_BR + 2 + c, h, 12 + 2 * c + h, acc=4, first=c == 0 and h == 0,
                             last=br_done if c and h else None)
            pe.wait_ge(mg_a, 4)
            for c in range(4):
                pe.wait_ge(mg_lo, c + 1)
                for h in range(2):
                    row_half(C_WO + c, h, 16 + 2 * c + h, first=c == 0 and h == 0,
                             last=acc_done if c == 3 and h == 1 else None)
            norm(4)
            ffn(1, C_F2, C_D2, normed=5)
            norm(5)

            for k in range(KD):
                pe.wait_ge(xn_ready, KD * 6 + k + 1)
                for tb in range(TB):
                    c = (k % 4) * P
                    mm = pe.transpose(bank[(k // 4) * 2 + tb][:, c:c + P], tiles(XNF + k)[:, tb * P:(tb + 1) * P], ident)
                    if k % 4 == 3:
                        mm.then_inc(fin_t, 1)

        @block.scalar
        def _(act):
            def f(out_, in_, func, **kw):
                return nc.scalar.activation(out_, in_, func, **kw)

            def hi(n, i=0, step=0):
                if n >= half_of(C_END):
                    return
                src, landed, count = source(n)
                act.wait_ge(landed, count + i * (16 * step // 4))
                if n >= RING:
                    act.wait_ge(ring_free, n - RING + 1 + i * step)
                f(w_hi[:, n % RING, 0:src.shape[-1]], src, ACT.Copy).then_inc(hi_done, 1)

            def squares(n):
                for b in range(4):
                    act.wait_ge(x_ready, 4 * n + b + 1)
                    f(tiles(SQ + 2 * b, 2), wide(xres[:, 2 * b:2 * b + 2, :]), ACT.Square).then_inc(sq_ready, 1)

            def root(n):
                act.wait_ge(ms_ready, n + 1)
                f(std[:, 0:TB], bank[7][:, 0:TB], ACT.Sqrt, scale=1.0 / D, bias=eps[:, 0:1]).then_inc(std_ready, 1)

            def normed_hi(s, dst):
                for k in range(KD):
                    act.wait_ge(xn_ready, KD * s + k + 1)
                    f(a_hi[:, dst + k, :], tiles(XNF + k), ACT.Copy).then_inc(xh_ready, 1)

            def norm(n, half, sets):
                for h in range(3):
                    hi(half + h)
                squares(n)
                root(n)
                hi(half + 3)
                for s, dst in sets:
                    normed_hi(s, dst)

            hi(0)
            hi(1)
            act.wait_ge(set_done, 3)
            squares(0)
            root(0)
            hi(2)
            hi(3)
            normed_hi(0, 0)
            act.wait_ge(par_ready, 1)
            lam_p = par_a[:, LAM:LAM + LT]
            f(lam[:, 0, :], lam_p, ACT.Abs).then_inc(lam_e, 1)
            act.wait_ge(lam_e, 1)
            f(lam[:, 1, :], lam[:, 0, :], ACT.Exp, scale=-1.0).then_inc(lam_e, 1)

            def xb_hi(c):
                act.wait_ge(conv_x, 2 * c + 2)
                f(wide(a_hi[:, 8 + 2 * c:10 + 2 * c, :]), tiles(XB + 2 * c, 2), ACT.Copy).then_inc(xbh, 1)

            for c in range(6):
                hi(2 * c + 4)
                act.wait_ge(ring_free, 2 * c + 2)
                for m in range(2):
                    t = 2 * c + m
                    f(tiles(XB + t), bank[4 + c % 2][:, m * T:(m + 1) * T], ACT.Identity,
                      scale=par_a[:, CONV_W + 3 * LT + t:CONV_W + 3 * LT + t + 1],
                      bias=par_a[:, CONV_B + t:CONV_B + t + 1]).then_inc(conv_b, 1)
                hi(2 * c + 5)
                if c >= 1:
                    xb_hi(c - 1)
            xb_hi(5)
            for g in range(LG):
                for w in range(2):
                    n = H_RI + 2 * g + w
                    hi(n + 4)
                    act.wait_ge(ring_free, n + 1)
                    for m in range(3):
                        t = 3 * g + m
                        b = bank[4 * (g % 2) + 2 * w + m // 2]
                        s = f(tiles((RR, II)[w] + t), b[:, (m % 2) * T:(m % 2 + 1) * T], ACT.Sigmoid,
                              bias=par_a[:, (BR, BI)[w] + t:(BR, BI)[w] + t + 1])
                    s.then_inc(ri_sig, 1)

            def decay(g):
                act.wait_ge(ri_sig, 2 * g + 1)
                for m in range(3):
                    t = 3 * g + m
                    s = f(tiles(AA + t), tiles(RR + t), ACT.Exp, scale=lam[:, 7, t:t + 1])
                s.then_inc(lru_a, 1)
                for m in range(3):
                    t = 3 * g + m
                    s = f(tiles(RR + t), tiles(RR + t), ACT.Tanh, scale=lam[:, 7, t:t + 1])
                s.then_inc(lru_t, 1)

            def lru_root(g):
                act.wait_ge(lru_m, g + 1)
                f(tiles(RR + 3 * g, 3), tiles(RR + 3 * g, 3), ACT.Sqrt, scale=-1.0).then_inc(lru_s, 1)

            act.wait_ge(lam_ready, 1)
            decay(0)
            decay(1)
            for c in range(6):
                hi(24 + 2 * c)
                act.wait_ge(ring_free, 22 + 2 * c)
                f(tiles(GATE + 2 * c, 2), bank[4 + c % 2][:, :], ACT.Copy).then_inc(gate_raw, 1)
                hi(25 + 2 * c)
                if c == 0:
                    decay(2)
                    decay(3)
                if c in (2, 3):
                    lru_root(2 * c - 4)
                    lru_root(2 * c - 3)
            act.wait_ge(gate_raw, 6)
            for g in range(LG):
                f(tiles(GATE + 3 * g, 3), tiles(GATE + 3 * g, 3), ACT.Silu).then_inc(lru_silu, 1)
            for g in range(LG):
                act.wait_ge(y_f, g + 1)
                f(wide(a_hi[:, 8 + 3 * g:11 + 3 * g, :]), tiles(XB + 3 * g, 3), ACT.Copy).then_inc(y_hi, 1)
                if g >= 2:
                    hi(32 + 2 * g)
                    hi(33 + 2 * g)
            for n in range(40, 44):
                hi(n)
            norm(1, half_of(C_KV), [(1, 8), (2, 0)])

            def swa_out(s):
                act.wait_ge(ring_free, 46 + 2 * s)
                b = bank[4 + s % 2]
                if s <= 4:
                    w = T if s == 0 else 2 * T
                    if s >= 2:
                        act.wait_ge(hn_ms, s - 1)
                    f(flat[:, (49 + 2 * (s % 2)) * T:(49 + 2 * (s % 2)) * T + w], b[:, 0:w], ACT.Square)\
                        .then_inc(hn_sq, 1)
                if s == 0:
                    f(tiles(40), b[:, 0:T], ACT.Copy)
                    f(tiles(44), b[:, T:2 * T], ACT.Copy).then_inc(q_raw, 1)
                else:
                    f(tiles(2 * s - 2, 2), b[:, :], ACT.Copy).then_inc(q_raw, 1)

            def head_root(n):
                w = 2 * TB * (1 if n == 0 else 2)
                act.wait_ge(hn_ms, n + 1)
                f(std[:, 0:w], bank[7][:, 0:w], ACT.Sqrt, scale=1.0 / HD, bias=eps[:, 0:1]).then_inc(hn_std, 1)

            for s in range(6):
                hi(48 + 2 * s)
                if s >= 1:
                    head_root(s - 1)
                swa_out(s)
                hi(49 + 2 * s)
            act.wait_ge(kdup_ps, 1)
            f(tiles(41, 2), bank[2][:, :], ACT.Copy).then_inc(kdup_ready, 1)

            def softmax_exp(n, sinks=None):
                act.wait_ge(s_neg, n + 1)
                s = score_buf(n)
                e = f(s[:, 0:P], s[:, 0:P], ACT.Exp, bias=ntop[:, 2 * n:2 * n + 1], accum_out=rsum[:, 2 * n:2 * n + 1])
                e = f(s[:, P:SC], s[:, P:SC], ACT.Exp, bias=ntop[:, 2 * n + 1:2 * n + 2],
                      accum_out=rsum[:, 2 * n + 1:2 * n + 2])
                if sinks is not None:
                    e = f(esink[:, 2 * n:2 * n + 2], ntop[:, 2 * n:2 * n + 2], ACT.Exp, bias=sinks)
                e.then_inc(p_exp, 1)

            def turned(n):
                act.wait_ge(t_done, n + 1)
                if n >= 2:
                    act.wait_ge(o_done, n - 1)
                f(prob_t(n), bank[2 + n % 2][:, 0:SC], ACT.Copy).then_inc(t_out, 1)

            act.wait_ge(sink_in, 16)
            for r in range(NQ + 2):
                if r < NQ:
                    softmax_exp(r, sink[:, r:r + 1])
                if r >= 2:
                    turned(r - 2)
                if r % 3 == 2:
                    hi(60 + r // 3)
                    if r % 6 == 5:
                        swa_out(6 + r // 6)
            act.wait_ge(q_raw, 9)
            for c in range(4):
                f(tiles(8 + 2 * c, 2), tiles(8 + 2 * c, 2), ACT.Silu).then_inc(silu_b, 1)
            for c in range(4):
                act.wait_ge(yb_f, c + 1)
                f(wide(a_hi[:, 8 + 2 * c:10 + 2 * c, :]), tiles(16 + 2 * c, 2), ACT.Copy).then_inc(yb_hi, 1)
            for n in range(66, 70):
                hi(n)
            norm(2, half_of(C_F1), [(3, 0)])

            def ffn(n, c_pair, c_down):
                first, base = n * (FT // 2), half_of(c_pair) + 4

                def pair(j, i=0):
                    for h in range(3):
                        hi(base + 4 * j + h, i, 8)
                    act.wait_ge(ring_free, base + 4 * j + i * 8)
                    if j >= 2:
                        act.wait_ge(ff_f, first + j - 1 + i * 2)
                    f(tiles(40 + 2 * (j % 2), 2), bank[4 + 2 * (j % 2)][:, :], ACT.Silu).then_inc(ff_silu, 1)
                    hi(base + 4 * j + 3, i, 8)
                    act.wait_ge(ff_f, first + j + 1 + i * 2)
                    f(wide(a_hi[:, bass.ds(i * 4 + (8 + 2 * j), 2), :]) if j >= 3 else wide(a_hi[:, 8 + 2 * j:10 + 2 * j, :]),
                      tiles(44 + 2 * (j % 2), 2), ACT.Copy).then_inc(ff_hi, 1)

                for j in range(3):
                    pair(j)
                with act.Fori(0, (FT // 2 - 3) // 2) as i:
                    pair(3, i)
                    pair(4, i)
                if n == 0:
                    act.wait_ge(trig_r, 1)
                    f(sine[:, :], tiles(58), ACT.Sin).then_inc(trig_abs, 1)
                    f(tiles(59), tiles(58), ACT.Abs).then_inc(trig_abs, 1)
                    act.wait_ge(trig_abs, 2)
                    f(cosine[:, :], tiles(59), ACT.Sin, scale=-1.0, bias=half_pi[:, 0:1]).then_inc(trig_ready, 1)
                base_d = half_of(c_down) + 4
                with act.Fori(0, 4) as i:
                    for h in range(4):
                        hi(base_d + h, i, 4)
                hi(base_d + 16)
                hi(base_d + 17)

            ffn(0, C_F1, C_D1)
            norm(3, half_of(C_MIX), [(4, 0)])

            def mix_out(c):
                act.wait_ge(ring_free, half_of(C_MIX) + 2 * c + 2)
                b = bank[4 + c % 2]
                if c < 4:
                    if c >= 2:
                        act.wait_ge(rope_done, c - 1)
                    f(tiles(48 + 2 * (c % 2), 2), b[:, :], ACT.Copy, scale=SCALE if c < 2 else 1.0).then_inc(m_raw, 1)
                elif c in (4, 5, 10, 11):
                    v = tiles(16 if c < 6 else 20, 4).rearrange("p (b n) -> p b n", b=TB)
                    f(v[:, :, (c % 2) * T:(c % 2 + 1) * T], b[:, :].rearrange("p (b n) -> p b n", b=TB), ACT.Copy)\
                        .then_inc(m_raw, 1)
                elif c < 10:
                    f(tiles(2 * c - 4, 2), b[:, :], ACT.Copy, scale=SCALE if c < 8 else 1.0).then_inc(m_raw, 1)
                else:
                    f(tiles(2 * c + 8, 2), b[:, :], ACT.Copy).then_inc(m_raw, 1)

            def branch_hi(b):
                act.wait_ge(o_done, NQ + 4 * b + 4)
                f(wide(a_hi[:, 8 + 2 * b:10 + 2 * b, :]), bank[6 + b % 2][:, :], ACT.Copy).then_inc(ym_hi, 1)

            H_M = half_of(C_MIX)
            for c in range(12):
                hi(H_M + 2 * c + 4)
                mix_out(c)
                hi(H_M + 2 * c + 5)
            for r in range(NH + 4):
                if r < NH:
                    softmax_exp(NQ + r)
                if 2 <= r < NH + 2:
                    turned(NQ + r - 2)
                if 2 <= r <= 9:
                    hi(H_M + 26 + r)
                    if r % 2:
                        mix_out(12 + (r - 3) // 2)
                if r == 7:
                    branch_hi(0)
                if r == 11:
                    branch_hi(1)
            for r in range(NH + 5):
                if r < NH:
                    act.wait_ge(z_sb, r + 1)
                    if r >= 3:
                        act.wait_ge(sp_done, r - 2)
                    f(stick_ln(r), stick_z(r), ACT.Abs).then_inc(sb_abs, 1)
                    act.wait_ge(sb_abs, r + 1)
                    f(stick_ln(r), stick_ln(r), ACT.Exp, scale=-1.0).then_inc(sb_exp, 1)
                    act.wait_ge(sb_exp, r + 1)
                    f(stick_ln(r), stick_ln(r), ACT.Ln, bias=ones[:, 0:1]).then_inc(sb_ln, 1)
                if 3 <= r < NH + 3:
                    act.wait_ge(d_done, r - 2)
                    f(stick_z(r - 3), stick_z(r - 3), ACT.Exp).then_inc(w_exp, 1)
                if 2 <= r <= 9:
                    hi(H_M + 34 + r)
                    if r % 2:
                        mix_out(16 + (r - 3) // 2)
                if r == 8:
                    branch_hi(2)
                if r == 12:
                    branch_hi(3)
            act.wait_ge(m_raw, 20)
            H_B = half_of(C_BR)
            for m in range(2 * KD):
                f(tiles(32 + m), tiles(32 + m), ACT.Sigmoid, bias=par_b[:, B_GATE + m:B_GATE + m + 1]).then_inc(g_sig, 1)
                if m % 4 == 3:
                    hi(H_B + 4 + m // 4)
            hi(H_B + 8)
            hi(H_B + 9)
            for c in range(4):
                act.wait_ge(mg_f, c + 1)
                f(wide(a_hi[:, 16 + 2 * c:18 + 2 * c, :]), tiles(2 * c, 2), ACT.Copy).then_inc(mg_hi, 1)
                if c == 0:
                    hi(H_B + 10)
                    hi(H_B + 11)
            for h in range(12, 16):
                hi(H_B + h)
            norm(4, half_of(C_F2), [(5, 0)])
            ffn(1, C_F2, C_D2)
            squares(5)
            root(5)

        @block.vector
        def _(dve):
            def lo(n, i=0, step=0):
                if n >= half_of(C_END):
                    return
                src, _, _ = source(n)
                w = src.shape[-1]
                dve.wait_ge(hi_done, n + 1 + i * step)
                dve.tensor_tensor(w_lo[:, n % RING, 0:w], src, w_hi[:, n % RING, 0:w].bitcast(F32), ALU.subtract)\
                    .then_inc(w_done, 1)

            def low(dst, src, n):
                return dve.tensor_tensor(dst_lo(dst, n), src, dst_hi(dst, n).bitcast(F32), ALU.subtract)

            def dst_lo(t, n):
                return wide(a_lo[:, t:t + n, :])

            def dst_hi(t, n):
                return wide(a_hi[:, t:t + n, :])

            NEXT = [0, C_KV, C_F1, C_MIX, C_F2, C_END]

            def residual(n, scale=1.0):
                for b in range(4):
                    if n and b == 3:
                        dve.wait_ge(ring_free, half_of(NEXT[n]))
                    else:
                        dve.wait_ge(acc_done, (3 * n + 1 if n else 0) + b + 1)
                    x = wide(xres[:, 2 * b:2 * b + 2, :])
                    if n == 0:
                        dve.tensor_copy(x, bank[b][:, :]).then_inc(x_ready, 1)
                    else:
                        dve.scalar_tensor_tensor(x, bank[b][:, :], scale, x, ALU.mult, ALU.add).then_inc(x_ready, 1)

            def root_inv(n):
                dve.wait_ge(std_ready, n + 1)
                dve.reciprocal(rstd[:, 0:TB], std[:, 0:TB]).then_inc(rstd_ready, 1)

            def scaled(n, s, dst=None):
                dve.wait_ge(rb_ready, n + 1)
                dve.wait_ge(x_ready, 4 * n + 4)
                for k in range(KD + 1):
                    if k < KD:
                        dve.scalar_tensor_tensor(tiles(XNF + k), xres[:, k, :], GAINS[s][:, k:k + 1], bank[6][:, 0:T],
                                                 ALU.mult, ALU.mult).then_inc(xn_ready, 1)
                    if k >= 1 and dst is not None:
                        dve.wait_ge(xh_ready, KD * s + k)
                        low(dst + k - 1, tiles(XNF + k - 1), 1).then_inc(xl_ready, 1)

            def norm(n, scale, half, sets):
                for h in range(3):
                    lo(half + h)
                residual(n, scale)
                root_inv(n)
                for s, dst in sets:
                    scaled(n, s, dst)
                lo(half + 3)

            residual(0)
            lo(0)
            lo(1)
            root_inv(0)
            dve.wait_ge(par_t, 1)
            dve.tensor_copy(par_a[:, :], bank[5][:, 0:ROWS_A]).then_inc(par_ready, 1)
            dve.wait_ge(par_ready, 1)
            scaled(0, 0, 0)
            lo(2)
            lo(3)

            steps = [0]

            def lam_op(op):
                steps[0] += 1
                op.then_inc(lam_step, 1)
                dve.wait_ge(lam_step, steps[0])

            dve.wait_ge(lam_e, 2)
            e, den, z, z2, ser, big = (lam[:, j, :] for j in range(1, 7))
            lam_op(dve.tensor_scalar(den, e, 2.0, 1.0, ALU.add, ALU.mult))
            lam_op(dve.reciprocal(z, den))
            lam_op(dve.tensor_tensor(z, z, e, ALU.mult))
            lam_op(dve.tensor_tensor(z2, z, z, ALU.mult))
            lam_op(dve.tensor_scalar(ser, z2, 1.0 / 15.0, 1.0, ALU.mult, ALU.mult))
            for odd in range(13, 1, -2):
                lam_op(dve.scalar_tensor_tensor(ser, ser, 1.0 / odd, z2, ALU.add, ALU.mult))
            lam_op(dve.scalar_tensor_tensor(ser, ser, 1.0, z, ALU.add, ALU.mult))
            lam_op(dve.tensor_scalar(big, par_a[:, LAM:LAM + LT], -1.0, 0.0, ALU.mult, ALU.max))
            lam_op(dve.scalar_tensor_tensor(ser, ser, 2.0, big, ALU.mult, ALU.add))
            dve.tensor_scalar(lam[:, 7, :], ser, -LRU_C, 1.0, ALU.mult, ALU.mult).then_inc(lam_ready, 1)

            def xb_lo(c):
                dve.wait_ge(xbh, c + 1)
                low(8 + 2 * c, tiles(XB + 2 * c, 2), 2).then_inc(xbl, 1)

            for c in range(6):
                lo(2 * c + 4)
                dve.wait_ge(conv_b, 2 * c + 2)
                for s in range(1, CONV):
                    for m in range(2):
                        t = 2 * c + m
                        x = tiles(XB + t)
                        if s >= 2:
                            dve.wait_ge(conv_s, 4 * c + 2 * (s - 2) + m + 1)
                        w = CONV_W + (CONV - 1 - s) * LT + t
                        dve.scalar_tensor_tensor(x[:, s:T], bank[4 + c % 2][:, m * T:(m + 1) * T - s], par_a[:, w:w + 1],
                                                 x[:, s:T], ALU.mult, ALU.add)\
                            .then_inc(conv_x if s == CONV - 1 else conv_s, 1)
                lo(2 * c + 5)
                if c >= 1:
                    xb_lo(c - 1)
            xb_lo(5)
            for n in range(H_RI + 4, H_RI + 12):
                lo(n)

            def lru_square(g):
                dve.wait_ge(lru_t, g + 1)
                dve.wait_ge(lru_aa, g + 1)
                r = tiles(RR + 3 * g, 3)
                dve.scalar_tensor_tensor(r, tiles(XB + 3 * g, 3), 1.0, r, ALU.add, ALU.mult).then_inc(lru_m, 1)

            def lru_scan(g):
                dve.wait_ge(lru_s, g + 1)
                dve.wait_ge(lru_bx, g + 1)
                i3 = tiles(II + 3 * g, 3)
                dve.tensor_tensor(i3, i3, tiles(RR + 3 * g, 3), ALU.mult).then_inc(lru_b, 1)
                dve.wait_ge(lru_b, g + 1)
                dve.wait_ge(lru_a, g + 1)
                for m in range(3):
                    t = 3 * g + m
                    s = dve.tensor_tensor_scan(tiles(XB + t), tiles(AA + t), tiles(II + t), 0.0, ALU.mult, ALU.add)
                s.then_inc(lru_h, 1)

            for c in range(6):
                lo(24 + 2 * c)
                lo(25 + 2 * c)
                if c == 0:
                    lru_square(0)
                    lru_square(1)
                if c == 1:
                    lru_square(2)
                    lru_square(3)
                if c == 0:
                    dve.wait_ge(par_t, 2)
                    dve.tensor_copy(par_b[:, :], bank[6][:, 0:ROWS_B]).then_inc(par_ready, 1)
                    dve.wait_ge(par_ready, 2)
                    dve.tensor_scalar(q_gain[:, :], par_b[:, Q_G:Q_G + 1], SCALE, 1.0, ALU.mult, ALU.mult)\
                        .then_inc(qg_ready, 1)
                if c in (3, 4):
                    lru_scan(2 * c - 6)
                    lru_scan(2 * c - 5)
            for g in range(LG):
                dve.wait_ge(lru_silu, g + 1)
                dve.wait_ge(lru_h, g + 1)
                h3 = tiles(XB + 3 * g, 3)
                dve.tensor_tensor(h3, h3, tiles(GATE + 3 * g, 3), ALU.mult).then_inc(y_f, 1)
            for g in range(LG):
                dve.wait_ge(y_hi, g + 1)
                low(8 + 3 * g, tiles(XB + 3 * g, 3), 3).then_inc(y_lo, 1)
                if g >= 2:
                    lo(32 + 2 * g)
                    lo(33 + 2 * g)
            for n in range(40, 44):
                lo(n)
            norm(1, 1.0, half_of(C_KV), [(1, 8), (2, 0)])

            def head_inv(n):
                w = 2 * TB * (1 if n == 0 else 2)
                dve.wait_ge(hn_std, n + 1)
                dve.reciprocal(rstd[:, 0:w], std[:, 0:w]).then_inc(hn_rstd, 1)

            def head_scaled(n):
                dve.wait_ge(hn_rb, n + 1)
                dve.wait_ge(q_raw, n + 1)
                if n == 0:
                    t, w, g = 40, 1, par_b[:, K_G:K_G + 1]
                else:
                    t, w, g = 2 * n - 2, 2, q_gain[:, 0:1]
                dve.scalar_tensor_tensor(tiles(t, w), tiles(t, w), g, bank[6][:, 0:w * T], ALU.mult, ALU.mult)\
                    .then_inc(hn_done, 1)

            dve.wait_ge(qg_ready, 1)
            for s in range(6):
                lo(48 + 2 * s)
                if s >= 1:
                    head_inv(s - 1)
                    head_scaled(s - 1)
                lo(49 + 2 * s)

            def masked_max(n, bias, low_q, floor):
                dve.wait_ge(s_done, n + 1)
                if n >= 3:
                    dve.wait_ge(t_done, n - 2)
                s, ps = score_buf(n), bank[n % 2]
                for q, (c, w) in enumerate(((0, P), (P, T))):
                    dve.tensor_tensor_reduce(s[:, c:c + w], ps[:, c:c + w], bias[:, T - w:T], 1.0, floor, ALU.add, ALU.max,
                                             accum_out=top[:, 2 * n + q:2 * n + q + 1]).then_inc(s_max, 1)
                dve.wait_ge(s_max, 2 * n + 2)
                dve.tensor_scalar(ntop[:, 2 * n:2 * n + 2], top[:, 2 * n:2 * n + 2], -1.0, 1.0, ALU.mult, ALU.mult)\
                    .then_inc(s_neg, 1)

            def normalise(n, sinks):
                dve.wait_ge(p_exp, n + 1)
                c = slice(2 * n, 2 * n + 2)
                total = rsum
                if sinks:
                    dve.tensor_tensor(esink[:, c], esink[:, c], rsum[:, c], ALU.add).then_inc(den_sum, 1)
                    dve.wait_ge(den_sum, n + 1)
                    total = esink
                dve.reciprocal(rden[:, c], total[:, c]).then_inc(den_inv, 1)
                dve.wait_ge(den_inv, n + 1)
                s = score_buf(n)
                dve.tensor_scalar(s[:, 0:P], s[:, 0:P], rden[:, 2 * n:2 * n + 1], 1.0, ALU.mult, ALU.mult)
                dve.tensor_scalar(s[:, P:SC], s[:, P:SC], rden[:, 2 * n + 1:2 * n + 2], 1.0, ALU.mult, ALU.mult)\
                    .then_inc(p_norm, 1)

            dve.wait_ge(sink_in, 16)
            dve.wait_ge(con_in, 16)
            for r in range(NQ + 4):
                if r < NQ:
                    dve.wait_ge(bias_ready, r + 1)
                    masked_max(r, tiles(53 + r % 3), 0, sink[:, r:r + 1])
                if 1 <= r <= NQ:
                    normalise(r - 1, True)
                if r % 3 == 2 and r < 18:
                    lo(60 + r // 3)
                if r % 4 == 3 and r >= 7:
                    b = r // 4 - 1
                    dve.wait_ge(o_done, 4 * b + 4)
                    dve.tensor_copy(tiles(16 + 2 * b, 2), bank[6 + b % 2][:, :]).then_inc(o_out, 1)
            for c in range(4):
                dve.wait_ge(silu_b, c + 1)
                dve.wait_ge(o_out, c + 1)
                o2 = tiles(16 + 2 * c, 2)
                dve.tensor_tensor(o2, o2, tiles(8 + 2 * c, 2), ALU.mult).then_inc(yb_f, 1)
            for c in range(4):
                dve.wait_ge(yb_hi, c + 1)
                low(8 + 2 * c, tiles(16 + 2 * c, 2), 2).then_inc(yb_lo, 1)
            for n in range(66, 70):
                lo(n)
            norm(2, 1.0, half_of(C_F1), [(3, 0)])

            def angles():
                t, turns, r = tiles(56), tiles(57), tiles(58)
                n = [0]

                def step(op):
                    n[0] += 1
                    op.then_inc(trig_s, 1)
                    dve.wait_ge(trig_s, n[0])

                dve.wait_ge(pos_in, 16)
                step(dve.tensor_copy(t, pos[:, :]))
                step(dve.tensor_scalar(r, t, par_b[:, FREQ:FREQ + 1], 1.0, ALU.mult, ALU.mult))
                step(dve.tensor_scalar(t, r, 1.0 / TWO_PI, ROUND, ALU.mult, ALU.add))
                step(dve.tensor_scalar(turns, t, -ROUND, 1.0, ALU.add, ALU.mult))
                for part in TURN_PARTS:
                    step(dve.scalar_tensor_tensor(r, turns, -part, r, ALU.mult, ALU.add))
                dve.tensor_scalar(r, r, -PI_LOW, PI_LOW, ALU.max, ALU.min).then_inc(trig_r, 1)

            def ffn(n, c_pair, c_down):
                first, base = n * (FT // 2), half_of(c_pair) + 4

                def pair(j, i=0):
                    for h in range(3):
                        lo(base + 4 * j + h, i, 8)
                    dve.wait_ge(ff_silu, first + j + 1 + i * 2)
                    hid = tiles(44 + 2 * (j % 2), 2)
                    dve.tensor_tensor(hid, tiles(40 + 2 * (j % 2), 2), bank[5 + 2 * (j % 2)][:, :], ALU.mult)\
                        .then_inc(ff_f, 1)
                    lo(base + 4 * j + 3, i, 8)
                    dve.wait_ge(ff_hi, first + j + 1 + i * 2)
                    if j < 3:
                        low(8 + 2 * j, hid, 2).then_inc(ff_lo, 1)
                    else:
                        at = bass.ds(i * 4 + (8 + 2 * j), 2)
                        dve.tensor_tensor(wide(a_lo[:, at, :]), hid, wide(a_hi[:, at, :]).bitcast(F32), ALU.subtract)\
                            .then_inc(ff_lo, 1)

                for j in range(3):
                    pair(j)
                with dve.Fori(0, (FT // 2 - 3) // 2) as i:
                    pair(3, i)
                    pair(4, i)
                if n == 0:
                    angles()
                base_d = half_of(c_down) + 4
                with dve.Fori(0, 4) as i:
                    for h in range(4):
                        lo(base_d + h, i, 4)
                lo(base_d + 16)
                lo(base_d + 17)

            ffn(0, C_F1, C_D1)
            norm(3, FFN_RES, half_of(C_MIX), [(4, 0)])

            def rope(n):
                dve.wait_ge(rope_p, n + 1)
                x = tiles(48 + 2 * (n % 2), 2).rearrange("p (t n) -> p t n", t=2)
                one, two = (tiles(t, 2).rearrange("p (t n) -> p t n", t=2) for t in (52, 54))
                dve.tensor_tensor(one, x, cosine[:, :].unsqueeze(1).to_broadcast([P, 2, T]), ALU.mult).then_inc(rope_a, 1)
                dve.tensor_tensor(two, bank[6][:, :].rearrange("p (t n) -> p t n", t=2),
                                  sine[:, :].unsqueeze(1).to_broadcast([P, 2, T]), ALU.mult).then_inc(rope_a, 1)
                dve.wait_ge(rope_a, 2 * n + 2)
                dve.tensor_tensor(tiles(2 * n, 2), tiles(52, 2), tiles(54, 2), ALU.add).then_inc(rope_done, 1)

            def branch_lo(b):
                dve.wait_ge(ym_hi, b + 1)
                low(8 + 2 * b, bank[6 + b % 2][:, :], 2).then_inc(ym_lo, 1)

            H_M = half_of(C_MIX)
            dve.wait_ge(trig_ready, 1)
            for c in range(12):
                lo(H_M + 2 * c + 4)
                if 1 <= c <= 4:
                    rope(c - 1)
                lo(H_M + 2 * c + 5)
            for r in range(NH + 4):
                if r < NH:
                    masked_max(NQ + r, con[:, CMASK:CMASK + T], 0, -3e38)
                if 1 <= r <= NH:
                    normalise(NQ + r - 1, False)
                if 2 <= r <= 9:
                    lo(H_M + 26 + r)
                if r == 7:
                    branch_lo(0)
                if r == 11:
                    branch_lo(1)
            dve.wait_ge(o_done, NQ + NH)
            for r in range(NH + 5):
                if r < NH:
                    dve.wait_ge(z_done, r + 1)
                    if r >= 5:
                        dve.wait_ge(o_done, NQ + NH + r - 4)
                    dve.tensor_tensor(stick_z(r), bank[r % 2][:, 0:SC], con[:, SBMASK:SBMASK + SC], ALU.add)\
                        .then_inc(z_sb, 1)
                if 1 <= r <= NH:
                    n = r - 1
                    dve.wait_ge(sb_ln, n + 1)
                    if n >= 2:
                        dve.wait_ge(c_done, n - 1)
                    dve.scalar_tensor_tensor(stick_sp(n), stick_z(n), 0.0, stick_ln(n), ALU.max, ALU.add)\
                        .then_inc(sp_done, 1)
                if 3 <= r < NH + 3:
                    n = r - 3
                    dve.wait_ge(c_done, n + 1)
                    dve.tensor_tensor(stick_z(n), stick_z(n), bank[2 + n % 2][:, 0:SC], ALU.subtract).then_inc(d_done, 1)
                if 2 <= r <= 9:
                    lo(H_M + 34 + r)
                if r == 8:
                    branch_lo(2)
                if r == 12:
                    branch_lo(3)
            H_B = half_of(C_BR)
            for h in range(4, 8):
                lo(H_B + h)
            for b in range(4):
                if b < 3:
                    dve.wait_ge(br_done, b + 1)
                else:
                    dve.wait_ge(ring_free, H_B + 4)
                dve.wait_ge(g_sig, 2 * b + 2)
                dve.tensor_tensor(tiles(32 + 2 * b, 2), tiles(32 + 2 * b, 2), bank[b][:, :], ALU.mult).then_inc(mg_a, 1)
            lo(H_B + 8)
            lo(H_B + 9)
            for b in range(5):
                if b < 4:
                    if b < 3:
                        dve.wait_ge(br_done, b + 4)
                    else:
                        dve.wait_ge(ring_free, H_B + 8)
                    dve.wait_ge(g_sig, KD + 2 * b + 2)
                    gb = tiles(40 + 2 * b, 2)
                    dve.tensor_tensor(gb, gb, bank[4 + b][:, :], ALU.mult).then_inc(mg_b, 1)
                    dve.wait_ge(mg_a, b + 1)
                    dve.wait_ge(mg_b, b + 1)
                    dve.tensor_tensor(tiles(2 * b, 2), tiles(32 + 2 * b, 2), gb, ALU.add).then_inc(mg_f, 1)
                if b >= 1:
                    dve.wait_ge(mg_hi, b)
                    low(16 + 2 * b - 2, tiles(2 * b - 2, 2), 2).then_inc(mg_lo, 1)
                if b == 1:
                    lo(H_B + 10)
                    lo(H_B + 11)
            for h in range(12, 16):
                lo(H_B + h)
            norm(4, 1.0, half_of(C_F2), [(5, 0)])
            ffn(1, C_F2, C_D2)

            residual(5, FFN_RES)
            root_inv(5)
            scaled(5, 6)
            for q, (half, b) in enumerate(((0, 0), (0, 1), (1, 0), (1, 1))):
                dve.wait_ge(fin_t, q + 1)
                dve.tensor_copy(tiles(8 + 2 * q, 2), bank[q][:, :]).then_inc(fin_sb, 1)



_INS = ["x", "a_norm_g", "a_w_in", "a_conv_w", "a_conv_b", "a_gate_r_w", "a_gate_r_b", "a_gate_i_w", "a_gate_i_b",
        "a_lambda", "a_w_out", "kv_norm_g", "w_kv", "k_norm_g", "b_norm_g", "b_w_in", "q_norm_g", "sinks", "b_w_out",
        "positions_2", "ffn1_norm_2", "ffn1_w_gate_2", "ffn1_w_up_2", "ffn1_w_down_2", "mix_norm_2", "w_in_2",
        "b_gate_2", "w_branch_moba_2", "w_branch_sb_2", "w_out_2", "ffn2_norm_2", "ffn2_w_gate_2", "ffn2_w_up_2",
        "ffn2_w_down_2", "final_norm_2"]


def kernel(**inputs):
    import concourse.bacc as _bacc
    from concourse import mybir as _mybir
    from concourse.bass_utils import run_bass_kernel_spmd as _run

    nc = _bacc.Bacc("TRN2", target_bir_lowering=False, num_devices=1)
    con, freq = constants()
    arrays, args = {"constants": con, "freq": freq}, {}
    for name in _INS:
        arrays[name] = np.ascontiguousarray(inputs[name])
    for name, a in arrays.items():
        args[name] = nc.dram_tensor(name, a.shape, _mybir.dt.from_np(a.dtype), kind="ExternalInput").ap()
    out = nc.dram_tensor("out", (1, T, D), _mybir.dt.float32, kind="ExternalOutput").ap()
    build(nc, args, out)
    r = _run(nc, [arrays], core_ids=[0])
    return r.results[0]["out"]
```

```python
from contextlib import ExitStack

import numpy as np

import concourse.bass as bass
from concourse import mybir

F32 = mybir.dt.float32
F32R = mybir.dt.float32r
I32 = mybir.dt.int32
ACT = mybir.ActivationFunctionType
ALU = mybir.AluOpType

P = 128
T = 256
TB = T // P
D = 1024
KD = D // P
LRU = 1536
LT = LRU // P
LB = 96
LG = 4
CONV = 4
LRU_C = 8.0
HD = 64
NQ = 16
NH = 8
DFF = 2816
FT = DFF // P
EPS = 1e-6
SCALE = HD ** -0.5
FFN_RES = 0.5
SLOPES = [float(np.float32(2.0 ** (-8.0 * (h + 1) / NQ))) for h in range(NQ)]
SC = T + P
BIG = 1e30
TWO_PI = 2.0 * np.pi
ROUND = 1.5 * 2.0 ** 23
TURN_1 = 6.28125
TURN_2 = float(np.float32(np.round((TWO_PI - TURN_1) * 2.0 ** 19) / 2.0 ** 19))
TURN_PARTS = [TURN_1, TURN_2, TWO_PI - TURN_1 - TURN_2]
PI_LOW = float(np.nextafter(np.float32(np.pi), np.float32(0)))

HALF = 4 * T
RING = 4
GATE_COLS = 896
GATE_TILES = [(0, 0, 0), (1, 0, 256), (0, 1, 128), (1, 1, 384), (2, 1, 640), (1, 2, 512), (2, 2, 768)]
GATE_PIECES = [(0, 0, 96, 0, 0), (1, 0, 32, 96, 96), (1, 32, 64, 0, 256 + 96),
               (2, 0, 64, 64, 256 + 192), (2, 64, 32, 0, 640 + 64), (3, 0, 96, 32, 640 + 160)]

C_X, C_G, C_AO, C_KV, C_Q, C_BG, C_BO, C_F1, C_D1 = 0, 6, 12, 18, 19, 23, 27, 31, 53
C_MIX, C_BR, C_WO, C_F2, C_D2, C_END = 64, 84, 88, 92, 114, 125
H_RI = [8, 12, 16, 18]


def half_of(chunk):
    return 2 * chunk + 2 * sum(h <= 2 * chunk + 2 * g for g, h in enumerate(H_RI))


SPLIT_BY_DVE = range(24, 30)


CONV_W, CONV_B, BR, BI, LAM = 0, 48, 60, 72, 84
ROWS_A = 96
KV_G, B_G, F1_G, MIX_G, F2_G, FIN_G, B_GATE, K_G, Q_G, FREQ = 0, 8, 16, 24, 32, 40, 48, 64, 65, 66
ROWS_B = 67

IDENT, PERM, TRI, E0, E1, DIST, CMASK, SBMASK, BLK2 = 0, 128, 256, 384, 512, 640, 896, 1152, 1536
N_CONST = 1538

ROPE_AT = (5, 6, 8, 9)
HEAD_SQUARES = {5: 0, 6: 1, 7: 2, 9: 3}
HEAD_ROOTS = {6: 0, 7: 1, 8: 2, 10: 3}
SWA_FILL = {0: 11, 1: 12, 2: 13, 4: 14, 7: 15, 11: 16, 16: 17}
SWA_HI = {2: 12, 4: 13, 7: 14, 11: 15, 14: 16}
SWA_LO = {2: 12, 5: 13, 8: 14, 12: 15, 15: 16}
LAG = 4


def swa_bank(s):
    return 0 if s == 2 else 4 + s % 2


def mix_bank(c):
    return 7 if c == 2 else 4 + c % 2


def constants():
    c = np.zeros((P, N_CONST), np.float32)
    p = np.arange(P)[:, None]
    j = np.arange(P)[None, :]
    c[:, IDENT:IDENT + P] = p == j
    same = p // HD == j // HD
    c[:, PERM:PERM + P] = same * (1.0 * ((p % HD == j % HD - 8) & (j % HD < 16) & (j % HD >= 8))
                                  - 1.0 * ((p % HD == j % HD + 8) & (j % HD < 8)))
    c[:, TRI:TRI + P] = p >= j
    c[:, E0:E0 + P] = p == j % HD
    c[:, E1:E1 + P] = p == HD + j % HD
    k = np.arange(T)[None, :]
    dist = P + p - k
    c[:, DIST:DIST + T] = np.where((dist >= 0) & (dist < P), dist, np.float32(1e33))
    c[:, CMASK:CMASK + T] = np.where(dist >= 0, 0.0, -BIG)
    past = np.where(p < j, 0.0, -BIG)
    c[:, SBMASK:SBMASK + P] = past
    c[:, SBMASK + T:SBMASK + SC] = past
    c[:, BLK2] = np.arange(P) < HD
    c[:, BLK2 + 1] = np.arange(P) >= HD
    freq = np.zeros((1, P), np.float32)
    half = np.float32(500000.0) ** (-np.arange(8, dtype=np.float32) * np.float32(2.0) / np.float32(16))
    for h in range(2):
        freq[0, h * HD:h * HD + 8] = half
        freq[0, h * HD + 8:h * HD + 16] = half
    return c, freq


def build(nc, I, out):
    ctx = ExitStack()
    with ctx:
        def sb(name, shape, dt=F32):
            return ctx.enter_context(nc.sbuf_tensor(name, shape, dt))

        def sem(name):
            return ctx.enter_context(nc.semaphore(name))

        stage = sb("stage", [P, 2, 2, HALF])
        w_hi = sb("w_hi", [P, RING, HALF], F32R)
        w_lo = sb("w_lo", [P, RING, HALF], F32R)
        gate_st = sb("gate_st", [P, 2, 2, GATE_COLS])
        xres = sb("xres", [P, KD, T])
        a_hi = sb("a_hi", [P, 30, T], F32R)
        a_lo = sb("a_lo", [P, 30, T], F32R)
        arena = sb("arena", [P, 62, T])
        rows_n = sb("rows_n", [KD, P])
        rows_a = sb("rows_a", [ROWS_A, P])
        rows_b = sb("rows_b", [ROWS_B, P])
        par_n = sb("par_n", [P, KD])
        par_a = sb("par_a", [P, ROWS_A])
        par_b = sb("par_b", [P, ROWS_B])
        con = sb("con", [P, N_CONST])
        ones = sb("ones", [P, P])
        eps = sb("eps", [P, 1])
        pos = sb("pos", [P, T], I32)
        sink = sb("sink", [P, NQ])
        cosine = sb("cosine", [P, T])
        sine = sb("sine", [P, T])
        half_pi = sb("half_pi", [P, 1])
        q_gain = sb("q_gain", [P, 1])
        lam = sb("lam", [P, 8, LT])
        n_ms = sb("n_ms", [P, TB])
        n_std = sb("n_std", [P, TB])
        n_rstd = sb("n_rstd", [P, TB])
        spread = sb("spread", [P, T])
        std = sb("std", [P, 8])
        rstd = sb("rstd", [P, 8])
        top = sb("top", [P, 2 * (NQ + NH)])
        ntop = sb("ntop", [P, 2 * (NQ + NH)])
        rsum = sb("rsum", [P, 2 * (NQ + NH)])
        esink = sb("esink", [P, 2 * (NQ + NH)])
        rden = sb("rden", [P, 2 * (NQ + NH)])
        bank = [ctx.enter_context(nc.psum_tensor(f"bank{b}", [P, 512], F32)) for b in range(8)]

        def tiles(t, n=1):
            return arena[:, t:t + n, :].rearrange("p t n -> p (t n)")

        flat = arena[:, :, :].rearrange("p t n -> p (t n)")
        SQ, XNF = 24, 32
        XB, GATE, RR, II, AA = 0, 12, 24, 36, 48

        gate_hi = tiles(AA, 14).rearrange("p (g w n) -> p g w n", g=2, w=2)


        x_in, con_in = sem("x_in"), sem("con_in")
        rows_n_in, rows_a_in, rows_b_in = sem("rows_n_in"), sem("rows_a_in"), sem("rows_b_in")
        pos_in, sink_in, id_in = sem("pos_in"), sem("sink_in"), sem("id_in")
        stage_in = [sem(f"stage_in{q}") for q in range(4)]
        gate_in = [sem("gate_in0"), sem("gate_in1")]
        set_done = sem("set_done")
        hi_done, w_done, ring_free = sem("hi_done"), sem("w_done"), sem("ring_free")
        acc_done, x_ready, sq_ready, ms_ready = sem("acc_done"), sem("x_ready"), sem("sq_ready"), sem("ms_ready")
        std_ready, rstd_ready, rb_ready, rb_sb = sem("std_ready"), sem("rstd_ready"), sem("rb_ready"), sem("rb_sb")
        xn_ready, xh_ready, xl_ready = sem("xn_ready"), sem("xh_ready"), sem("xl_ready")
        par_t, par_ready, lam_e, lam_step, lam_ready = (
            sem(n) for n in ("par_t", "par_ready", "lam_e", "lam_step", "lam_ready"))
        conv_b, conv_s, conv_x, xbh, xbl = sem("conv_b"), sem("conv_s"), sem("conv_x"), sem("xbh"), sem("xbl")
        ri_sig = sem("ri_sig")
        lru_a, lru_t, lru_aa, lru_m, lru_s, lru_bx, lru_b, lru_h, lru_silu = (
            sem(n) for n in ("lru_a", "lru_t", "lru_aa", "lru_m", "lru_s", "lru_bx", "lru_b", "lru_h", "lru_silu"))
        gate_raw, y_f, y_hi, y_lo = sem("gate_raw"), sem("y_f"), sem("y_hi"), sem("y_lo")
        qg_ready = sem("qg_ready")
        hn_inv, hi_dve = sem("hn_inv"), sem("hi_dve")
        v_raw, k_tok, k_turned = sem("v_raw"), sem("k_tok"), sem("k_turned")
        sq_add, sq_sum = sem("sq_add"), sem("sq_sum")
        q_raw, hn_sq, hn_ms, hn_std, hn_rstd, hn_rb, hn_done = (
            sem(n) for n in ("q_raw", "hn_sq", "hn_ms", "hn_std", "hn_rstd", "hn_rb", "hn_done"))
        kdup_ps, kdup_ready = sem("kdup_ps"), sem("kdup_ready")
        bias_ready, s_done, s_max, s_neg, p_exp, den_sum, den_inv, p_norm, t_done, t_out, o_done, o_out = (
            sem(n) for n in ("bias_ready", "s_done", "s_max", "s_neg", "p_exp", "den_sum", "den_inv", "p_norm",
                             "t_done", "t_out", "o_done", "o_out"))
        ff_g, ff_u, m_val = sem("ff_g"), sem("ff_u"), sem("m_val")
        silu_b, yb_f, yb_hi, yb_lo = sem("silu_b"), sem("yb_f"), sem("yb_hi"), sem("yb_lo")
        ff_silu, ff_f, ff_hi, ff_lo = sem("ff_silu"), sem("ff_f"), sem("ff_hi"), sem("ff_lo")
        trig_s, trig_r, trig_abs, trig_ready = sem("trig_s"), sem("trig_r"), sem("trig_abs"), sem("trig_ready")
        m_raw, rope_p, rope_a, rope_done = sem("m_raw"), sem("rope_p"), sem("rope_a"), sem("rope_done")
        z_done, z_sb, sb_abs, sb_exp, sb_ln, sp_done, c_done, d_done, w_exp = (
            sem(n) for n in ("z_done", "z_sb", "sb_abs", "sb_exp", "sb_ln", "sp_done", "c_done", "d_done", "w_exp"))
        ym_hi, ym_lo, g_sig = sem("ym_hi"), sem("ym_lo"), sem("g_sig")
        br_done, mg_a, mg_b, mg_f, mg_hi, mg_lo = (
            sem(n) for n in ("br_done", "mg_a", "mg_b", "mg_f", "mg_hi", "mg_lo"))
        fin_t, fin_a, fin_d, out_done = sem("fin_t"), sem("fin_a"), sem("fin_d"), sem("out_done")

        def source(n):
            for g, h in enumerate(H_RI):
                if n in (h, h + 1):
                    return (gate_st, gate_hi)[g // 2][:, g % 2, n - h, :], gate_in[g // 2], 16 * 2 * len(GATE_PIECES)
            chunk = next(c for c in range(C_END) if half_of(c) == n - n % 2)
            return stage[:, chunk % 2, n % 2, :], stage_in[2 * (chunk % 2) + n % 2], 16 * (chunk // 2 + 1)

        def wide(t3):
            return t3.rearrange("p t n -> p (t n)")

        def score_buf(n):
            return flat[:, 24 * T + n % (LAG + 1) * SC:24 * T + (n % (LAG + 1) + 1) * SC]

        def prob_t(n):
            at = 24 * T + (LAG + 1 + n % 3) * SC
            return flat[:, at:at + SC]

        def dist_bias(n):
            return tiles(53 + n % 6)

        def stick_z(n):
            return flat[:, 48 * T + (n % 6) * SC:48 * T + (n % 6 + 1) * SC]

        def stick_sp(n):
            return flat[:, 24 * T + (n % 2) * SC:24 * T + (n % 2 + 1) * SC]

        def stick_ln(n):
            return flat[:, 27 * T + (n % 3) * SC:27 * T + (n % 3 + 1) * SC]

        heads_rstd = tiles(45, 2)
        ident = con[:, IDENT:IDENT + P]
        GAINS = [par_n[:, :]] + [par_b[:, g:g + KD] for g in (KV_G, B_G, F1_G, MIX_G, F2_G, FIN_G)]

        block = ctx.enter_context(nc.Block())

        @block.sync
        def _(sp):
            sp.dma_start(ident, I["constants"][:, IDENT:IDENT + P]).then_inc(id_in, 16)
            sp.dma_start(rows_n[:, :], I["a_norm_g"].rearrange("o (k p) -> (o k) p", p=P)).then_inc(rows_n_in, 16)
            xt = I["x"].rearrange("o (b p) d -> p (o b) d", p=P)
            sp.dma_start(tiles(0, 8).rearrange("p (b d) -> p b d", b=TB), xt).then_inc(x_in, 16)

            def load(chunk, src, first=None):
                n = src.shape[1] // 2
                for h in range(2):
                    if first is not None:
                        sp.wait_ge(w_done, first + h)
                    sp.dma_start(stage[:, chunk % 2, h, :].rearrange("p (b n) -> p b n", b=n),
                                 src[:, h * n:(h + 1) * n, :]).then_inc(stage_in[2 * (chunk % 2) + h], 16)

            def col(w, j):
                return w.rearrange("(k p) n -> p k n", p=P)[:, :, bass.ds(j * T, T)]

            def row(w, j):
                return w[bass.ds(j * T, T), :].rearrange("(k p) n -> p k n", p=P)

            def split(chunk):
                return half_of(chunk) + 1

            def stream(chunk, n, view):
                j = 0
                while j < n and chunk + j < C_G + 2:
                    load(chunk + j, view(j), split(chunk + j - 2) if chunk + j >= 2 else None)
                    j += 1
                turns = (n - j) // 2
                if turns > 1:
                    base = split(chunk + j - 2)
                    with sp.Fori(0, turns) as i:
                        for b in range(2):
                            load(chunk + j + b, view(i * 2 + (j + b)), base + 2 * b + i * 4)
                    j += 2 * turns
                for r in range(j, n):
                    load(chunk + r, view(r), split(chunk + r - 2))

            def pairs(chunk, wa, wb):
                base = split(chunk - 2)
                with sp.Fori(0, DFF // T) as i:
                    load(chunk, col(wa, i), base + i * 4)
                    load(chunk + 1, col(wb, i), base + 2 + i * 4)

            w_in, w_out = I["a_w_in"][0], I["a_w_out"][0]
            stream(C_X, 6, lambda j: col(w_in, j))
            stream(C_G, 6, lambda j: col(w_in, j + 6))
            stream(C_AO, 6, lambda j: row(w_out, j))
            stream(C_KV, 1, lambda j: col(I["w_kv"], j))
            stream(C_Q, 8, lambda j: col(I["b_w_in"][0], j))
            stream(C_BO, 4, lambda j: row(I["b_w_out"][0], j))
            pairs(C_F1, I["ffn1_w_gate_2"][0], I["ffn1_w_up_2"][0])
            stream(C_D1, 11, lambda j: row(I["ffn1_w_down_2"][0], j))
            stream(C_MIX, 20, lambda j: col(I["w_in_2"][0], j))
            stream(C_BR, 2, lambda j: row(I["w_branch_moba_2"][0], j))
            stream(C_BR + 2, 2, lambda j: row(I["w_branch_sb_2"][0], j))
            stream(C_WO, 4, lambda j: row(I["w_out_2"][0], j))
            pairs(C_F2, I["ffn2_w_gate_2"][0], I["ffn2_w_up_2"][0])
            stream(C_D2, 11, lambda j: row(I["ffn2_w_down_2"][0], j))

            o = out.rearrange("o (b p) (h n) -> (o b) h p n", p=P, h=2)
            for q, (half, b) in enumerate([(0, 0), (0, 1), (1, 0), (1, 1)]):
                sp.wait_ge((fin_a, fin_d)[q % 2], q // 2 + 1)
                sp.dma_start(o[b, half], tiles(8 + 2 * q, 2)).then_inc(out_done, 16)
            sp.wait_ge(out_done, 64)

        @block.gpsimd
        def _(pool):
            pool.memset(ones[:, :], 1.0).then_inc(set_done, 1)
            pool.memset(eps[:, :], EPS).then_inc(set_done, 1)
            pool.memset(half_pi[:, :], float(np.pi / 2)).then_inc(set_done, 1)
            pool.memset(gate_st[:, :, :, :], 0.0).then_inc(set_done, 1)
            pool.memset(tiles(AA, 14), 0.0).then_inc(set_done, 1)

            for pair, place in enumerate((gate_st, gate_hi)):
                pool.wait_ge(set_done, 4 + pair)
                for w, name in enumerate(("a_gate_r_w", "a_gate_i_w")):
                    blocks = I[name][0].rearrange("(g b) i j -> b i g j", b=4)
                    for b, r, n, p, c in GATE_PIECES:
                        pool.dma_start(place[p:p + n, :, w, c:c + LB], blocks[b, r:r + n, 2 * pair:2 * pair + 2, :])\
                            .then_inc(gate_in[pair], 16)
            for first, name, n in ((F1_G, "ffn1_norm_2", KD), (MIX_G, "mix_norm_2", KD), (F2_G, "ffn2_norm_2", KD),
                                   (B_GATE, "b_gate_2", 2 * KD), (B_G, "b_norm_g", KD)):
                pool.dma_start(rows_b[first:first + n, :], I[name].rearrange("o (k p) -> (o k) p", p=P))\
                    .then_inc(rows_b_in, 16)
            for first, name in ((KV_G, "kv_norm_g"), (FIN_G, "final_norm_2")):
                pool.dma_start(rows_b[first:first + KD, :], I[name].rearrange("(k p) -> k p", p=P))\
                    .then_inc(rows_b_in, 16)
            for h in range(2):
                pool.dma_start(rows_b[K_G:K_G + 1, h * HD:(h + 1) * HD], I["k_norm_g"].rearrange("(o d) -> o d", o=1))\
                    .then_inc(rows_b_in, 16)
                pool.dma_start(rows_b[Q_G:Q_G + 1, h * HD:(h + 1) * HD], I["q_norm_g"]).then_inc(rows_b_in, 16)
            pool.dma_start(rows_b[FREQ:FREQ + 1, :], I["freq"]).then_inc(rows_b_in, 16)
            pool.dma_start(con[:, P:N_CONST], I["constants"][:, P:N_CONST]).then_inc(con_in, 16)
            pool.dma_start(pos[:, :], I["positions_2"].to_broadcast([P, T])).then_inc(pos_in, 16)
            pool.dma_start(sink[:, :], I["sinks"].to_broadcast([P, NQ])).then_inc(sink_in, 16)
            pool.wait_ge(xbl, 6)
            for g in range(LG):
                pool.wait_ge(ri_sig, 2 * g + 2)
                pool.tensor_tensor(tiles(II + 3 * g, 3), tiles(II + 3 * g, 3), tiles(XB + 3 * g, 3), ALU.mult)\
                    .then_inc(lru_bx, 1)
            for g in range(LG):
                pool.wait_ge(lru_a, g + 1)
                pool.wait_ge(lru_bx, g + 1)
                pool.tensor_tensor(tiles(XB + 3 * g, 3), tiles(AA + 3 * g, 3), tiles(AA + 3 * g, 3), ALU.mult)\
                    .then_inc(lru_aa, 1)
            for g in range(LG):
                pool.wait_ge(lru_s, g + 1)
                pool.wait_ge(lru_bx, g + 1)
                i3 = tiles(II + 3 * g, 3)
                pool.tensor_tensor(i3, i3, tiles(RR + 3 * g, 3), ALU.mult).then_inc(lru_b, 1)

            def square_sums(n):
                def square(b):
                    x = wide(xres[:, 2 * b:2 * b + 2, :])
                    pool.wait_ge(x_ready, 4 * n + b + 1)
                    pool.tensor_tensor(tiles(SQ + 2 * b, 2), x, x, ALU.mult).then_inc(sq_ready, 1)

                def plus(a, b, w):
                    pool.tensor_tensor(tiles(SQ + a, w), tiles(SQ + a, w), tiles(SQ + b, w), ALU.add).then_inc(sq_add, 1)

                square(0)
                square(1)
                pool.wait_ge(sq_ready, 4 * n - 2)
                plus(0, 2, 2)
                square(2)
                square(3)
                pool.wait_ge(sq_ready, 4 * n)
                plus(4, 6, 2)
                pool.wait_ge(sq_add, 3 * n - 1)
                plus(0, 4, 2)
                pool.wait_ge(sq_add, 3 * n)
                pool.tensor_tensor(tiles(SQ), tiles(SQ), tiles(SQ + 1), ALU.add).then_inc(sq_sum, 1)

            square_sums(1)
            def normalise(n):
                pool.wait_ge(den_inv, n + 1)
                s = score_buf(n)
                pool.tensor_scalar(s[:, 0:P], s[:, 0:P], rden[:, 2 * n:2 * n + 1], 1.0, ALU.mult, ALU.mult)\
                    .then_inc(p_norm, 1)
                pool.tensor_scalar(s[:, P:SC], s[:, P:SC], rden[:, 2 * n + 1:2 * n + 2], 1.0, ALU.mult, ALU.mult)\
                    .then_inc(p_norm, 1)

            pool.wait_ge(con_in, 16)
            pool.wait_ge(hn_done, 1)
            for r in range(-3, NQ + 2):
                if r + 3 < NQ:
                    if r >= 3:
                        pool.wait_ge(s_max, 2 * (r - 2))
                    pool.tensor_scalar(dist_bias(r + 3), con[:, DIST:DIST + T], -SLOPES[r + 3], 1.0, ALU.mult, ALU.mult)\
                        .then_inc(bias_ready, 1)
                if r >= 2:
                    normalise(r - 2)
            square_sums(2)
            square_sums(3)
            for h in range(NH):
                normalise(NQ + h)
            square_sums(4)

        @block.tensor
        def _(pe):
            SPLIT = ((w_hi, a_hi), (w_hi, a_lo), (w_lo, a_hi))

            def passes(dst, slot, c, k, start, stop):
                for n, (w, a) in enumerate(SPLIT):
                    mm = pe.matmul(dst, w[:, slot, c:c + P],
                                   a[:, k, :] if isinstance(k, int) else wide(a[:, bass.ds(k, 1), :]),
                                   start=start and n == 0, stop=stop and n == 2, skip_group_check=True)
                return mm

            def by_token(dst, slot, c, n, k, tb, start, stop):
                for i, (w, a) in enumerate(SPLIT):
                    mm = pe.matmul(dst, a[:, k, tb * P:(tb + 1) * P], w[:, slot, c:c + n],
                                   start=start and i == 0, stop=stop and i == 2, skip_group_check=True)
                return mm

            def col_half(chunk, h, b, first_tile=0, normed=None, ready=None, token=False):
                half = half_of(chunk) + h
                pe.wait_ge(w_done, half + 1 if ready is None else ready)
                for kk in range(4):
                    k = 4 * h + kk
                    if normed is not None:
                        pe.wait_ge(xl_ready, KD * normed + k + 1)
                    if token:
                        for tb in range(TB):
                            mm = by_token(bank[b][:, tb * T:(tb + 1) * T], half % RING, kk * T, T,
                                          first_tile + k, tb, k == 0 and tb == 0, k == KD - 1)
                        continue
                    for m in range(2):
                        mm = passes(bank[b][:, m * T:(m + 1) * T], half % RING, kk * T + m * P,
                                    first_tile + k, k == 0 and m == 0, k == KD - 1)
                mm.then_inc(ring_free, 1)

            def col_chunk(chunk, b, **kw):
                for h in range(2):
                    col_half(chunk, h, b, **kw)

            def row_half(chunk, h, k, acc=(0, 1, 2, 3), first=False, last=None, ready=None, later=None):
                half = half_of(chunk) + h
                pe.wait_ge(w_done, half + 1 if ready is None else ready)
                for m in range(KD):
                    if later is not None and m == KD // 2:
                        pe.wait_ge(*later)
                    mm = passes(bank[acc[m // 2]][:, (m % 2) * T:(m % 2 + 1) * T], half % RING, m * P, k,
                                first and m % 2 == 0, last is not None)
                    if last is not None and m in (1, 3, 5):
                        mm.then_inc(last, 1)
                mm.then_inc(ring_free, 1)

            def mean_squares(n, b):
                pe.wait_ge(sq_sum, n)
                for tb in range(TB):
                    mm = pe.matmul(bank[b][:, tb:tb + 1], tiles(SQ)[:, tb * P:(tb + 1) * P], ones[:, 0:1],
                                   start=True, stop=True)
                mm.then_inc(ms_ready, 1)

            def roots(n, b):
                pe.wait_ge(rstd_ready, n + 1)
                for tb in range(TB):
                    mm = pe.matmul(bank[b][:, tb * P:(tb + 1) * P], n_rstd[:, tb:tb + 1].to_broadcast([P, P]),
                                   ident, start=True, stop=True)
                mm.then_inc(rb_ready, 1)

            pe.wait_ge(id_in, 16)
            pe.wait_ge(rows_n_in, 16)
            pe.transpose(bank[5][:, 0:KD], rows_n[:, :], con[0:KD, IDENT:IDENT + KD]).then_inc(par_t, 1)
            pe.wait_ge(x_in, 16)
            xtok = tiles(0, 8).rearrange("p (b d) -> p b d", b=TB)
            for m in range(KD):
                for tb in range(TB):
                    c = (m % 2) * T + tb * P
                    mm = pe.transpose(bank[m // 2][:, c:c + P], xtok[:, tb, m * P:(m + 1) * P], ident)
                if m % 2:
                    mm.then_inc(acc_done, 1)
            roots(0, 6)

            def gates(g):
                banks = ((0, 1, 2), (3, 6, 7))[g % 2]
                for w in range(2):
                    half = H_RI[g] + w
                    pe.wait_ge(w_done, half + 1)
                    if w == 0:
                        pe.wait_ge(xbl, (3 * g + 2) // 2 + 1)
                        if g == 1:
                            pe.wait_ge(par_ready, 2)
                        if g >= 2:
                            pe.wait_ge(ri_sig, 2 * (g - 1))
                    done = [0, 0, 0]
                    for k, m, c in GATE_TILES:
                        q = 3 * w + m
                        done[m] += 1
                        mm = passes(bank[banks[q // 2]][:, (q % 2) * T:(q % 2 + 1) * T], half % RING, c, 8 + 3 * g + k,
                                    done[m] == 1 and q % 2 == 0, done[m] == (2, 3, 2)[m])
                    mm.then_inc(ring_free, 1)

            for c in range(6):
                if c == 1:
                    pe.wait_ge(par_ready, 1)
                if c >= 2:
                    pe.wait_ge(conv_x, 2 * (c - 1))
                col_chunk(C_X + c, 4 + c % 2, normed=0)
                if c == 0:
                    pe.wait_ge(rows_a_in, 16 * 5)
                    pe.transpose(bank[3][:, 0:ROWS_A], rows_a[:, :], con[0:ROWS_A, IDENT:IDENT + ROWS_A])\
                        .then_inc(par_t, 1)
                if c in (3, 4):
                    gates(c - 3)
            gates(2)
            gates(3)

            pe.wait_ge(conv_x, LT)
            for c in range(6):
                if 2 <= c < 5:
                    pe.wait_ge(gate_raw, c - 1)
                if c == 5:
                    pe.wait_ge(lru_silu, 4)
                col_chunk(C_G + c, 4 + c % 2)
                if c == 2:
                    pe.wait_ge(ri_sig, 2 * LG)
                    pe.wait_ge(rows_b_in, 16 * 12)
                    pe.transpose(bank[6][:, 0:ROWS_B], rows_b[:, :], con[0:ROWS_B, IDENT:IDENT + ROWS_B])\
                        .then_inc(par_t, 1)
            for c in range(6):
                for h in range(2):
                    pe.wait_ge(y_lo, (2 * c + h) // 3 + 1)
                    row_half(C_AO + c, h, 8 + 2 * c + h, first=c == 0 and h == 0,
                             last=acc_done if c == 5 and h == 1 else None)

            def head_squares(n):
                pe.wait_ge(hn_sq, n + 1)
                for c in range(TB if n == 0 else 2 * TB):
                    sq = tiles(49 + 2 * (n % 2), 2)[:, c * P:(c + 1) * P]
                    mm = pe.matmul(bank[7][:, 2 * c:2 * c + 2], sq, con[:, BLK2:BLK2 + 2], start=True, stop=True)
                mm.then_inc(hn_ms, 1)

            def head_roots(n):
                pe.wait_ge(hn_rstd, n + 1)
                if n:
                    pe.wait_ge(hn_done, n)
                for c in range(TB if n == 0 else 2 * TB):
                    mm = pe.matmul(bank[6][:, c * P:(c + 1) * P], heads_rstd[:, c * P:(c + 1) * P], ident,
                                   start=True, stop=True)
                mm.then_inc(hn_rb, 1)

            def swa_half(j):
                s, h = divmod(j, 2)
                if h == 0 and s >= 3:
                    pe.wait_ge(q_raw, s - 1)
                    if s == 4:
                        pe.wait_ge(v_raw, 2)
                if s == 0:
                    col_half(C_KV, h, 4, first_tile=8, normed=1, token=True)
                else:
                    col_half(C_KV + s, h, swa_bank(s), normed=2 if s == 1 else None)

            pe.wait_ge(con_in, 16)
            for j in range(11):
                swa_half(j)
                if j == 3:
                    mean_squares(1, 2)
                    pe.wait_ge(k_tok, 1)
                    for tb in range(TB):
                        mm = pe.transpose(bank[7][:, tb * P:(tb + 1) * P], tiles(47)[:, tb * P:(tb + 1) * P], ident)
                    mm.then_inc(k_turned, 1)
                if j == 4:
                    roots(1, 3)
                if j in HEAD_ROOTS:
                    head_roots(HEAD_ROOTS[j])
                if j in HEAD_SQUARES:
                    head_squares(HEAD_SQUARES[j])
                if j == 8:
                    pe.wait_ge(hn_done, 1)
                    for i in range(2):
                        mm = pe.matmul(bank[2][:, i * T:(i + 1) * T], con[:, E0 + i * P:E0 + (i + 1) * P], tiles(40),
                                       start=True, stop=True)
                    mm.then_inc(kdup_ps, 1)
            pe.wait_ge(kdup_ready, 1)

            def scores(n, q, k, hrow, t):
                if n < NQ:
                    pe.wait_ge(hn_done, 2 + n // 4)
                if n >= 2:
                    pe.wait_ge(s_max, 2 * (n - 1))
                r = slice(hrow * HD, (hrow + 1) * HD)
                s = bank[n % 2]
                pe.matmul(s[:, 0:P], q[r, t * T:t * T + P], k[r, 0:P], start=True, stop=True)
                pe.matmul(s[:, P:SC], q[r, t * T + P:(t + 1) * T], k[r, 0:T], start=True, stop=True)\
                    .then_inc(s_done, 1)

            def turn(n):
                pe.wait_ge(p_norm, 2 * n + 2)
                if n >= 2:
                    pe.wait_ge(t_out, n - 1)
                p = score_buf(n)
                for c in range(3):
                    mm = pe.transpose(bank[2 + n % 2][:, c * P:(c + 1) * P], p[:, c * P:(c + 1) * P], ident)
                mm.then_inc(t_done, 1)

            def values(n, o, v, w):
                r = (n % 2) * HD
                dst = bank[o][r:r + HD, (n // 2 % 2) * T:(n // 2 % 2 + 1) * T]
                pe.matmul(dst, v[0], w[:, 0:T], start=True, stop=False, skip_group_check=True)
                pe.matmul(dst[:, P:T], v[1], w[:, T:SC], start=False, stop=True, skip_group_check=True)\
                    .then_inc(o_done, 1)

            def gated_out(c, h):
                if c == 0 and h == 0:
                    pe.wait_ge(s_max, 2 * NQ)
                if h == 0:
                    pe.wait_ge(yb_lo, c + 1)
                row_half(C_BO + c, h, 8 + 2 * c + h, acc=(0, 1, 4, 5), first=c == 0 and h == 0,
                         last=acc_done if c == 3 and h == 1 else None,
                         later=(q_raw, 9) if c == 0 and h == 0 else None)

            vt = tiles(44)
            pe.wait_ge(q_raw, 3)
            for r in range(NQ + LAG + 2):
                if r < NQ:
                    scores(r, tiles(0, 8), tiles(41 + r // 8), r % 2, r // 2)
                if LAG <= r < NQ + LAG:
                    turn(r - LAG)
                if r >= LAG + 2:
                    n = r - LAG - 2
                    pe.wait_ge(t_out, n + 1)
                    if n == 0:
                        pe.wait_ge(hn_done, 5)
                    if n % 4 == 0 and n >= 8:
                        pe.wait_ge(o_out, n // 4 - 1)
                    kv = n // 8 * HD
                    values(n, 6 + (n // 4) % 2, [vt[:, tb * P + kv:tb * P + kv + HD] for tb in range(TB)], prob_t(n))
                if r in SWA_FILL:
                    swa_half(SWA_FILL[r])
                if r == 0:
                    head_squares(4)
                if r == 1:
                    head_roots(4)
                if r > NQ:
                    gated_out(*divmod(r - NQ - 1, 2))
            for j in range(LAG + 1, 8):
                gated_out(*divmod(j, 2))

            def ffn(n, c_pair, c_down, normed):
                first = n * (FT // 2)

                def pair(j, i=0, normed=None):
                    if j >= 2:
                        pe.wait_ge(ff_u, first + j - 1 + i * 2)
                    for u in range(2):
                        for h in range(2):
                            half = half_of(c_pair) + 4 * j + 2 * u + h
                            col_half(c_pair + u, h, 6 - 2 * (j % 2) + u, normed=normed if u == 0 else None,
                                     ready=half + 1 + i * 8)
                            if j == 0 and (u, h) == (1, 1):
                                mean_squares(2 * n + 2, 2)
                            if j == 1 and (u, h) == (0, 0):
                                roots(2 * n + 2, 3)

                pair(0, normed=normed)
                pair(1)
                pair(2)
                with pe.Fori(0, (FT // 2 - 3) // 2) as i:
                    pair(3, i)
                    pair(4, i)
                for c in range(2):
                    pe.wait_ge(ff_lo, first + c + 1)
                    for h in range(2):
                        row_half(c_down + c, h, 8 + 2 * c + h, first=c == 0 and h == 0)
                base = half_of(c_down)
                with pe.Fori(0, 4) as i:
                    for c in range(2):
                        pe.wait_ge(ff_lo, i * 2 + (first + c + 3))
                        for h in range(2):
                            row_half(c_down + c, h, i * 4 + (12 + 2 * c + h), ready=i * 4 + (base + 5 + 2 * c + h))
                pe.wait_ge(ff_lo, first + 11)
                row_half(c_down + 10, 0, 8 + 20)
                row_half(c_down + 10, 1, 8 + 21, last=acc_done)

            ffn(0, C_F1, C_D1, normed=3)

            VALUES = (4, 5, 10, 11)

            def mix_half(j):
                c, h = divmod(j, 2)
                if h == 0 and c >= 3:
                    p = c - 2
                    before = sum(v < p for v in VALUES)
                    if p in VALUES:
                        pe.wait_ge(m_val, before + 1)
                    else:
                        pe.wait_ge(m_raw, p - before + 1)
                col_half(C_MIX + c, h, mix_bank(c), normed=4 if c == 0 else None, token=c in VALUES)

            for j in range(12):
                mix_half(j)
                if j == 3:
                    mean_squares(3, 2)
                if j == 4:
                    roots(3, 3)
                if j in ROPE_AT:
                    n = ROPE_AT.index(j)
                    pe.wait_ge(m_raw, n + 1)
                    if n >= 1:
                        pe.wait_ge(rope_done, n)
                    pe.matmul(bank[6][:, :], con[:, PERM:PERM + P], tiles(48 + 2 * (n % 2), 2), start=True, stop=True)\
                        .then_inc(rope_p, 1)
            pe.wait_ge(rope_done, 4)

            v = tiles(16, 4)
            for r in range(NH + LAG + 2):
                n = NQ + r
                if r < NH:
                    scores(n, tiles(0, 4), tiles(4 + r // 2), r % 2, r // 2)
                if LAG <= r < NH + LAG:
                    turn(n - LAG)
                if r >= LAG + 2:
                    h = r - LAG - 2
                    pe.wait_ge(t_out, NQ + h + 1)
                    pe.wait_ge(m_val, 2)
                    values(NQ + h, 6 + h // 4, [v[:, tb * 512 + h * HD:tb * 512 + (h + 1) * HD] for tb in range(TB)],
                           prob_t(NQ + h))
                if r < 12:
                    mix_half(12 + r)
            pe.wait_ge(m_raw, 8)
            pe.wait_ge(s_max, 2 * (NQ + NH))
            v = tiles(20, 4)
            for r in range(NH + 5):
                if r < NH:
                    if r >= 2:
                        pe.wait_ge(z_sb, r - 1)
                    q, k, z = tiles(8 + r // 2), tiles(12 + r // 2), bank[r % 2]
                    s = slice((r % 2) * HD, (r % 2 + 1) * HD)
                    pe.matmul(z[:, 0:T], k[s, 0:P], q[s, 0:T], start=True, stop=True)
                    pe.matmul(z[:, T:SC], k[s, P:T], q[s, P:T], start=True, stop=True).then_inc(z_done, 1)
                if r == 2:
                    pe.wait_ge(t_out, NQ + NH)
                if r == 5:
                    pe.wait_ge(m_val, 4)
                if 2 <= r < NH + 2:
                    n = r - 2
                    pe.wait_ge(sp_done, n + 1)
                    if n >= 2:
                        pe.wait_ge(d_done, n - 1)
                    sums, sp_n = bank[2 + n % 2], stick_sp(n)
                    pe.matmul(sums[:, 0:SC], con[:, TRI:TRI + P], sp_n, start=True, stop=False, skip_group_check=True)
                    pe.matmul(sums[:, P:T], ones[:, :], sp_n[:, T:SC], start=False, stop=True, skip_group_check=True)\
                        .then_inc(c_done, 1)
                if r >= 5:
                    h = r - 5
                    pe.wait_ge(w_exp, h + 1)
                    if h % 4 == 0:
                        pe.wait_ge(ym_lo, h // 4 + 1)
                    values(h, 6 + h // 4, [v[:, tb * 512 + h * HD:tb * 512 + (h + 1) * HD] for tb in range(TB)], stick_z(h))
                for j in (2 * r, 2 * r + 1) if r < 3 else (r + 3,):
                    mix_half(24 + j)
            pe.wait_ge(d_done, NH)
            for c in range(2):
                for h in range(2):
                    row_half(C_BR + c, h, 8 + 2 * c + h, first=c == 0 and h == 0, last=br_done if c and h else None)
            pe.wait_ge(m_raw, 16)
            pe.wait_ge(ym_lo, 4)
            for c in range(2):
                for h in range(2):
                    row_half(C_BR + 2 + c, h, 12 + 2 * c + h, acc=(4, 5, 6, 7), first=c == 0 and h == 0,
                             last=br_done if c and h else None)
            pe.wait_ge(mg_a, 4)
            for c in range(4):
                pe.wait_ge(mg_lo, c + 1)
                for h in range(2):
                    row_half(C_WO + c, h, 16 + 2 * c + h, first=c == 0 and h == 0,
                             last=acc_done if c == 3 and h == 1 else None)
            ffn(1, C_F2, C_D2, normed=5)

            for k in range(KD):
                pe.wait_ge(xn_ready, KD + k + 1)
                for tb in range(TB):
                    c = (k % 4) * P
                    mm = pe.transpose(bank[4 + (k // 4) * 2 + tb][:, c:c + P], tiles(XNF + k)[:, tb * P:(tb + 1) * P],
                                      ident)
                    if k % 4 == 3:
                        mm.then_inc(fin_t, 1)
                if k % 2:
                    pe.wait_ge(sq_ready, 16 + k // 2 + 1)
                    for i in (k - 1, k):
                        for tb in range(TB):
                            mm = pe.matmul(bank[0][:, tb:tb + 1], tiles(SQ + i)[:, tb * P:(tb + 1) * P], ones[:, 0:1],
                                           start=i == 0 and tb == 0, stop=i == KD - 1, skip_group_check=True)
            mm.then_inc(ms_ready, 1)

        @block.scalar
        def _(act):
            def f(out_, in_, func, **kw):
                return nc.scalar.activation(out_, in_, func, **kw)

            def hi(n, i=0, step=0):
                if n >= half_of(C_END) or n in SPLIT_BY_DVE:
                    return
                src, landed, count = source(n)
                act.wait_ge(landed, count + i * (16 * step // 4))
                if n >= RING:
                    act.wait_ge(ring_free, n - RING + 1 + i * step)
                f(w_hi[:, n % RING, 0:src.shape[-1]], src, ACT.Copy).then_inc(hi_done, 1)

            def squares(n):
                for b in range(4):
                    act.wait_ge(x_ready, 4 * n + b + 1)
                    f(tiles(SQ + 2 * b, 2), wide(xres[:, 2 * b:2 * b + 2, :]), ACT.Square).then_inc(sq_ready, 1)

            def root(n):
                act.wait_ge(ms_ready, TB + n)
                f(n_std[:, :], bank[0 if n == 5 else 2][:, 0:TB], ACT.Sqrt, scale=1.0 / D, bias=eps[:, 0:1])\
                    .then_inc(std_ready, 1)

            def gained_hi(s, dst, k):
                f(a_hi[:, dst + k, :], xres[:, k, :], ACT.Identity, scale=GAINS[s][:, k:k + 1]).then_inc(xh_ready, 1)

            def norm(n, half, sets):
                act.preload_act_table(ACT.Sqrt)
                for h in range(3):
                    hi(half + h)
                for b in range(4):
                    act.wait_ge(x_ready, 4 * n + b + 1)
                    for k in (2 * b, 2 * b + 1):
                        gained_hi(*sets[0], k)
                hi(half + 3)
                for s, dst in sets[1:]:
                    for k in range(KD):
                        gained_hi(s, dst, k)

            act.preload_act_table(ACT.Sqrt)
            act.wait_ge(rows_n_in, 16)
            for first, name, n in ((CONV_B, "a_conv_b", LT), (BR, "a_gate_r_b", LT), (BI, "a_gate_i_b", LT),
                                   (LAM, "a_lambda", LT)):
                act.dma_start(rows_a[first:first + n, :], I[name].rearrange("o (k p) -> (o k) p", p=P))\
                    .then_inc(rows_a_in, 16)
            act.dma_start(rows_a[CONV_W:CONV_W + CONV * LT, :],
                          I["a_conv_w"].rearrange("o c (k p) -> (o c k) p", p=P)).then_inc(rows_a_in, 16)
            act.wait_ge(set_done, 3)
            act.wait_ge(x_in, 16)
            for tb in range(TB):
                f(tiles(SQ + 4 * tb, 4), tiles(4 * tb, 4), ACT.Square, accum_out=n_ms[:, tb:tb + 1]).then_inc(ms_ready, 1)
            act.wait_ge(ms_ready, 2)
            f(n_std[:, :], n_ms[:, :], ACT.Sqrt, scale=1.0 / D, bias=eps[:, 0:1]).then_inc(std_ready, 1)
            hi(0)
            hi(1)
            for k in range(KD):
                act.wait_ge(xn_ready, k + 1)
                f(a_hi[:, k, :], tiles(XNF + k), ACT.Copy).then_inc(xh_ready, 1)
            hi(2)
            hi(3)

            def xb_hi(c):
                act.wait_ge(conv_x, 2 * c + 2)
                f(wide(a_hi[:, 8 + 2 * c:10 + 2 * c, :]), tiles(XB + 2 * c, 2), ACT.Copy).then_inc(xbh, 1)

            x_end = {half_of(c) + 1: c for c in range(6)}
            gate_end = {H_RI[g] + 1: g for g in range(LG)}
            for n in range(half_of(C_G)):
                if n - 1 in x_end:
                    xb_hi(x_end[n - 1])
                if n == 6:
                    f(lam[:, 0, :], par_a[:, LAM:LAM + LT], ACT.Abs).then_inc(lam_e, 1)
                    act.wait_ge(lam_e, 1)
                    f(lam[:, 1, :], lam[:, 0, :], ACT.Exp, scale=-1.0).then_inc(lam_e, 1)
                if n not in x_end:
                    hi(n + 4)
                act.wait_ge(ring_free, n + 1)
                if n in x_end:
                    c = x_end[n]
                    if c == 0:
                        act.wait_ge(par_ready, 2)
                    for m in range(2):
                        t = 2 * c + m
                        f(tiles(XB + t), bank[4 + c % 2][:, m * T:(m + 1) * T], ACT.Identity,
                          scale=par_a[:, CONV_W + 3 * LT + t:CONV_W + 3 * LT + t + 1],
                          bias=par_a[:, CONV_B + t:CONV_B + t + 1]).then_inc(conv_b, 1)
                    hi(n + 4)
                if n in gate_end:
                    g = gate_end[n]
                    for q in range(6):
                        w, t = q // 3, 3 * g + q % 3
                        b = bank[((0, 1, 2), (3, 6, 7))[g % 2][q // 2]]
                        y = f(tiles((RR, II)[w] + t), b[:, (q % 2) * T:(q % 2 + 1) * T], ACT.Sigmoid,
                              bias=par_a[:, (BR, BI)[w] + t:(BR, BI)[w] + t + 1])
                        if q % 3 == 2:
                            y.then_inc(ri_sig, 1)

            def decay(g):
                act.wait_ge(ri_sig, 2 * g + 1)
                for m in range(3):
                    t = 3 * g + m
                    s = f(tiles(AA + t), tiles(RR + t), ACT.Exp, scale=lam[:, 7, t:t + 1])
                s.then_inc(lru_a, 1)
                for m in range(3):
                    t = 3 * g + m
                    s = f(tiles(RR + t), tiles(RR + t), ACT.Tanh, scale=lam[:, 7, t:t + 1])
                s.then_inc(lru_t, 1)

            def lru_root(g):
                act.wait_ge(lru_m, g + 1)
                f(tiles(RR + 3 * g, 3), tiles(RR + 3 * g, 3), ACT.Sqrt, scale=-1.0).then_inc(lru_s, 1)

            act.wait_ge(lam_ready, 1)
            for g in range(LG):
                decay(g)
            act.preload_act_table(ACT.Sqrt)
            lru_root(0)
            lru_root(1)
            lru_root(2)
            lru_root(3)
            act.preload_act_table(ACT.Silu)

            def silu(c):
                if c < 3:
                    act.wait_ge(gate_raw, c + 1)
                    f(tiles(GATE + 2 * c, 2), tiles(GATE + 2 * c, 2), ACT.Silu).then_inc(lru_silu, 1)
                else:
                    act.wait_ge(ring_free, 22 + 2 * c)
                    f(tiles(GATE + 2 * c, 2), bank[4 + c % 2][:, :], ACT.Silu).then_inc(lru_silu, 1)

            def y_up(g):
                act.wait_ge(y_f, g + 1)
                f(wide(a_hi[:, 8 + 3 * g:11 + 3 * g, :]), tiles(XB + 3 * g, 3), ACT.Copy).then_inc(y_hi, 1)

            silu(0)
            silu(1)
            silu(2)
            for c in (3, 4, 5):
                hi(24 + 2 * c)
                silu(c)
                if c == 4:
                    y_up(0)
                hi(25 + 2 * c)
                if c == 4:
                    y_up(1)
            y_up(2)
            y_up(3)
            for n in range(36, 40):
                hi(n)
            for n in range(40, 44):
                hi(n)
            norm(1, half_of(C_KV), [(1, 8), (2, 0)])

            def head_square(s):
                act.wait_ge(q_raw, s + 1)
                if s >= 2:
                    act.wait_ge(hn_ms, s - 1)
                t, w = (40, 1) if s == 0 else (2 * s - 2, 2)
                f(tiles(49 + 2 * (s % 2), w), tiles(t, w), ACT.Square).then_inc(hn_sq, 1)

            def head_root(n):
                w = 2 * TB * (1 if n == 0 else 2)
                act.wait_ge(hn_ms, n + 1)
                f(std[:, 0:w], bank[7][:, 0:w], ACT.Sqrt, scale=1.0 / HD, bias=eps[:, 0:1]).then_inc(hn_std, 1)

            for j in range(12):
                if j == 2:
                    act.wait_ge(ring_free, half_of(C_KV) + 2)
                    f(tiles(47).rearrange("p (b n) -> p b n", b=TB),
                      bank[4][:, :].rearrange("p (b n) -> p b n", b=TB)[:, :, 0:P], ACT.Copy).then_inc(k_tok, 1)
                if j == 3:
                    root(1)
                if j in HEAD_SQUARES:
                    head_root(HEAD_SQUARES[j])
                if j == 11:
                    head_root(4)
                if j == 4:
                    head_square(0)
                    head_square(1)
                if j in (5, 7, 9):
                    head_square(j // 2)
                hi(48 + j)
                if j == 8:
                    act.wait_ge(kdup_ps, 1)
                    f(tiles(41, 2), bank[2][:, :], ACT.Copy).then_inc(kdup_ready, 1)
            act.preload_act_table(ACT.Exp)

            def softmax_exp(n, sinks=None):
                act.wait_ge(s_neg, n + 1)
                s = score_buf(n)
                e = f(s[:, 0:P], s[:, 0:P], ACT.Exp, bias=ntop[:, 2 * n:2 * n + 1], accum_out=rsum[:, 2 * n:2 * n + 1])
                e = f(s[:, P:SC], s[:, P:SC], ACT.Exp, bias=ntop[:, 2 * n + 1:2 * n + 2],
                      accum_out=rsum[:, 2 * n + 1:2 * n + 2])
                if sinks is not None:
                    e = f(esink[:, 2 * n:2 * n + 2], ntop[:, 2 * n:2 * n + 2], ACT.Exp, bias=sinks)
                e.then_inc(p_exp, 1)

            def turned(n):
                act.wait_ge(t_done, n + 1)
                if n >= 3:
                    act.wait_ge(o_done, n - 2)
                f(prob_t(n), bank[2 + n % 2][:, 0:SC], ACT.Copy).then_inc(t_out, 1)

            act.wait_ge(sink_in, 16)
            def out_hi(c):
                act.wait_ge(yb_f, c + 1)
                f(wide(a_hi[:, 8 + 2 * c:10 + 2 * c, :]), tiles(16 + 2 * c, 2), ACT.Copy).then_inc(yb_hi, 1)

            def gate_silu(c):
                act.wait_ge(q_raw, 6 + c)
                f(tiles(8 + 2 * c, 2), tiles(8 + 2 * c, 2), ACT.Silu).then_inc(silu_b, 1)

            for r in range(NQ + LAG):
                if r < NQ:
                    softmax_exp(r, sink[:, r:r + 1])
                if r >= LAG:
                    turned(r - LAG)
                if r in SWA_HI:
                    hi(48 + SWA_HI[r])
                if r == NQ - 1:
                    act.preload_act_table(ACT.Silu)
                if r == NQ:
                    gate_silu(0)
                    gate_silu(1)
                    out_hi(0)
                if r == NQ + 1:
                    gate_silu(2)
                    out_hi(1)
                    hi(65)
            out_hi(2)
            gate_silu(3)
            hi(66)
            hi(67)
            out_hi(3)
            hi(68)
            hi(69)
            norm(2, half_of(C_F1), [(3, 0)])

            def ffn(n, c_pair, c_down):
                first, base = n * (FT // 2), half_of(c_pair) + 4

                def pair(j, i=0):
                    hi(base + 4 * j, i, 8)
                    hi(base + 4 * j + 1, i, 8)
                    if j == 0:
                        hi(base + 2)
                        root(2 * n + 2)
                        act.preload_act_table(ACT.Silu)
                        hi(base + 3)
                    act.wait_ge(ff_g, first + j + 1 + i * 2)
                    gate = tiles(40 + 2 * (j % 2), 2)
                    f(gate, gate, ACT.Silu).then_inc(ff_silu, 1)
                    if j:
                        hi(base + 4 * j + 2, i, 8)
                        hi(base + 4 * j + 3, i, 8)
                    act.wait_ge(ff_f, first + j + 1 + i * 2)
                    f(wide(a_hi[:, bass.ds(i * 4 + (8 + 2 * j), 2), :]) if j >= 3 else wide(a_hi[:, 8 + 2 * j:10 + 2 * j, :]),
                      tiles(44 + 2 * (j % 2), 2), ACT.Copy).then_inc(ff_hi, 1)

                for j in range(3):
                    pair(j)
                with act.Fori(0, (FT // 2 - 3) // 2) as i:
                    pair(3, i)
                    pair(4, i)
                if n == 0:
                    act.wait_ge(trig_r, 1)
                    f(sine[:, :], tiles(58), ACT.Sin).then_inc(trig_abs, 1)
                    f(tiles(59), tiles(58), ACT.Abs).then_inc(trig_abs, 1)
                    act.wait_ge(trig_abs, 2)
                    f(cosine[:, :], tiles(59), ACT.Sin, scale=-1.0, bias=half_pi[:, 0:1]).then_inc(trig_ready, 1)
                base_d = half_of(c_down) + 4
                with act.Fori(0, 4) as i:
                    for h in range(4):
                        hi(base_d + h, i, 4)
                hi(base_d + 16)
                hi(base_d + 17)

            ffn(0, C_F1, C_D1)
            norm(3, half_of(C_MIX), [(4, 0)])

            def mix_values(c):
                act.wait_ge(ring_free, half_of(C_MIX) + 2 * c + 2)
                for tb in range(TB):
                    at = (16 if c < 6 else 20) * T + tb * 512 + (c % 2) * T
                    v = f(flat[:, at:at + T], bank[4 + c % 2][:, tb * T:(tb + 1) * T], ACT.Identity,
                          scale=n_rstd[:, tb:tb + 1])
                v.then_inc(m_val, 1)

            def branch_hi(b):
                act.wait_ge(o_done, NQ + 4 * b + 4)
                f(wide(a_hi[:, 8 + 2 * b:10 + 2 * b, :]), bank[6 + b % 2][:, :], ACT.Copy).then_inc(ym_hi, 1)

            H_M = half_of(C_MIX)
            def mix_slot(j):
                if j == 3:
                    root(3)
                hi(H_M + 4 + j)
                if j in (9, 11, 21, 23):
                    mix_values(j // 2)

            for j in range(12):
                mix_slot(j)
            act.preload_act_table(ACT.Exp)
            for r in range(NH + 5):
                if r < NH:
                    softmax_exp(NQ + r)
                if LAG <= r < NH + LAG:
                    turned(NQ + r - LAG)
                if r >= 1:
                    mix_slot(11 + r)
                if r == LAG + 6:
                    branch_hi(0)
            branch_hi(1)
            act.preload_act_table_set("natural_log_exp_and_others")
            for r in range(NH + 5):
                if r < NH:
                    act.wait_ge(z_sb, r + 1)
                    if r >= 3:
                        act.wait_ge(sp_done, r - 2)
                    f(stick_ln(r), stick_z(r), ACT.Abs).then_inc(sb_abs, 1)
                    act.wait_ge(sb_abs, r + 1)
                    f(stick_ln(r), stick_ln(r), ACT.Exp, scale=-1.0).then_inc(sb_exp, 1)
                    act.wait_ge(sb_exp, r + 1)
                    f(stick_ln(r), stick_ln(r), ACT.Ln, bias=ones[:, 0:1]).then_inc(sb_ln, 1)
                if 3 <= r < NH + 3:
                    act.wait_ge(d_done, r - 2)
                    f(stick_z(r - 3), stick_z(r - 3), ACT.Exp).then_inc(w_exp, 1)
                for j in (() if r == 0 else (2 * r - 2, 2 * r - 1) if r < 4 else (r + 2,)):
                    mix_slot(24 + j)
                if r == 9:
                    branch_hi(2)
            mix_slot(39)
            branch_hi(3)
            act.wait_ge(m_raw, 16)
            H_B = half_of(C_BR)
            for m in range(2 * KD):
                f(tiles(32 + m), tiles(32 + m), ACT.Sigmoid, bias=par_b[:, B_GATE + m:B_GATE + m + 1]).then_inc(g_sig, 1)
                if m % 4 == 3:
                    hi(H_B + 4 + m // 4)
            hi(H_B + 8)
            hi(H_B + 9)
            for c in range(4):
                act.wait_ge(mg_f, c + 1)
                f(wide(a_hi[:, 16 + 2 * c:18 + 2 * c, :]), tiles(2 * c, 2), ACT.Copy).then_inc(mg_hi, 1)
                if c == 1:
                    hi(H_B + 10)
                    hi(H_B + 11)
            for h in range(12, 16):
                hi(H_B + h)
            norm(4, half_of(C_F2), [(5, 0)])
            ffn(1, C_F2, C_D2)
            act.preload_act_table(ACT.Sqrt)
            squares(5)
            root(5)
            act.wait_ge(rstd_ready, 6)
            for q in (0, 2):
                act.wait_ge(fin_t, q + 1)
                f(tiles(8 + 2 * q, 2), bank[4 + q][:, :], ACT.Identity, scale=n_rstd[:, 0:1]).then_inc(fin_a, 1)

        @block.vector
        def _(dve):
            def lo(n, i=0, step=0):
                if n >= half_of(C_END):
                    return
                src, landed, count = source(n)
                w = src.shape[-1]
                if n in SPLIT_BY_DVE:
                    dve.wait_ge(landed, count)
                    dve.wait_ge(ring_free, n - RING + 1)
                    dve.tensor_copy(w_hi[:, n % RING, 0:w], src).then_inc(hi_dve, 1)
                    dve.wait_ge(hi_dve, n - SPLIT_BY_DVE[0] + 1)
                else:
                    dve.wait_ge(hi_done, n + 1 - sum(m < n for m in SPLIT_BY_DVE) + i * step)
                dve.tensor_tensor(w_lo[:, n % RING, 0:w], src, w_hi[:, n % RING, 0:w].bitcast(F32), ALU.subtract)\
                    .then_inc(w_done, 1)

            def low(dst, src, n):
                return dve.tensor_tensor(dst_lo(dst, n), src, dst_hi(dst, n).bitcast(F32), ALU.subtract)

            def dst_lo(t, n):
                return wide(a_lo[:, t:t + n, :])

            def dst_hi(t, n):
                return wide(a_hi[:, t:t + n, :])

            NEXT = [0, C_KV, C_F1, C_MIX, C_F2, C_END]

            def add(n, b, scale=1.0):
                if n and b == 3:
                    dve.wait_ge(ring_free, half_of(NEXT[n]))
                else:
                    dve.wait_ge(acc_done, (3 * n + 1 if n else 0) + b + 1)
                x, acc = wide(xres[:, 2 * b:2 * b + 2, :]), bank[(0, 1, 4, 5)[b] if n == 2 else b]
                if n == 0:
                    dve.tensor_copy(x, acc[:, :]).then_inc(x_ready, 1)
                else:
                    dve.scalar_tensor_tensor(x, acc[:, :], scale, x, ALU.mult, ALU.add).then_inc(x_ready, 1)

            def residual(n, scale=1.0):
                for b in range(4):
                    add(n, b, scale)

            def root_inv(n):
                dve.wait_ge(std_ready, n + 1)
                dve.reciprocal(n_rstd[:, :], n_std[:, :]).then_inc(rstd_ready, 1)

            def gained_lo(s, dst, k):
                dve.wait_ge(xh_ready, KD * s + k + 1)
                dve.scalar_tensor_tensor(a_lo[:, dst + k, :], xres[:, k, :], GAINS[s][:, k:k + 1],
                                         a_hi[:, dst + k, :].bitcast(F32), ALU.mult, ALU.subtract).then_inc(xl_ready, 1)

            def norm(n, scale, half, sets):
                lo(half)
                lo(half + 1)
                for b in range(5):
                    if b < 4:
                        add(n, b, scale)
                    if b >= 1:
                        for k in (2 * b - 2, 2 * b - 1):
                            gained_lo(*sets[0], k)
                lo(half + 2)
                lo(half + 3)
                for s, dst in sets[1:]:
                    for k in range(KD):
                        gained_lo(s, dst, k)

            def roots_out(n):
                dve.wait_ge(rb_ready, n + 1)
                dve.tensor_copy(spread[:, :], bank[3][:, 0:T]).then_inc(rb_sb, 1)
                dve.wait_ge(rb_sb, n)

            def rooted(t, b, scale=1.0):
                y = tiles(t, 2).rearrange("p (t n) -> p t n", t=2)
                x = bank[b][:, :].rearrange("p (t n) -> p t n", t=2)
                by = spread[:, :].unsqueeze(1).to_broadcast([P, 2, T])
                if scale == 1.0:
                    return dve.tensor_tensor(y, x, by, ALU.mult)
                return dve.scalar_tensor_tensor(y, x, scale, by, ALU.mult, ALU.mult)

            root_inv(0)
            add(0, 0)
            add(0, 1)
            dve.wait_ge(par_t, 1)
            dve.tensor_copy(par_n[:, :], bank[5][:, 0:KD]).then_inc(par_ready, 1)
            add(0, 2)
            dve.wait_ge(par_ready, 1)
            dve.wait_ge(rb_ready, 1)
            for k in range(KD + 1):
                if k < KD:
                    dve.scalar_tensor_tensor(tiles(XNF + k), xres[:, k, :], GAINS[0][:, k:k + 1], bank[6][:, 0:T],
                                             ALU.mult, ALU.mult).then_inc(xn_ready, 1)
                if k == 1:
                    lo(0)
                if k == 3:
                    add(0, 3)
                if k >= 1:
                    dve.wait_ge(xh_ready, k)
                    low(k - 1, tiles(XNF + k - 1), 1).then_inc(xl_ready, 1)
                if k == 4:
                    lo(1)
            lo(2)
            lo(3)

            dve.wait_ge(par_t, 2)
            dve.tensor_copy(par_a[:, :], bank[3][:, 0:ROWS_A]).then_inc(par_ready, 1)
            dve.wait_ge(par_ready, 2)

            def xb_lo(c):
                dve.wait_ge(xbh, c + 1)
                low(8 + 2 * c, tiles(XB + 2 * c, 2), 2).then_inc(xbl, 1)

            x_end = {half_of(c) + 1: c for c in range(6)}
            for n in range(half_of(C_G)):
                if n - 1 in x_end:
                    xb_lo(x_end[n - 1])
                if n in x_end:
                    c = x_end[n]
                    dve.wait_ge(conv_b, 2 * c + 2)
                    for tap in range(1, CONV):
                        for m in range(2):
                            t = 2 * c + m
                            x = tiles(XB + t)
                            if tap >= 2:
                                dve.wait_ge(conv_s, 4 * c + 2 * (tap - 2) + m + 1)
                            w = CONV_W + (CONV - 1 - tap) * LT + t
                            dve.scalar_tensor_tensor(x[:, tap:T], bank[4 + c % 2][:, m * T:(m + 1) * T - tap],
                                                     par_a[:, w:w + 1], x[:, tap:T], ALU.mult, ALU.add)\
                                .then_inc(conv_x if tap == CONV - 1 else conv_s, 1)
                if n == half_of(C_X + 5) + 2:
                    lo(n + 3)
                if n != half_of(C_X + 5) + 1:
                    lo(n + 4)

            steps = [0]

            def lam_op(op):
                steps[0] += 1
                op.then_inc(lam_step, 1)
                dve.wait_ge(lam_step, steps[0])

            dve.wait_ge(lam_e, 2)
            e, den, z, z2, ser, big = (lam[:, j, :] for j in range(1, 7))
            lam_op(dve.tensor_scalar(den, e, 2.0, 1.0, ALU.add, ALU.mult))
            lam_op(dve.reciprocal(z, den))
            lam_op(dve.tensor_tensor(z, z, e, ALU.mult))
            lam_op(dve.tensor_tensor(z2, z, z, ALU.mult))
            lam_op(dve.tensor_scalar(ser, z2, 1.0 / 15.0, 1.0, ALU.mult, ALU.mult))
            for odd in range(13, 1, -2):
                lam_op(dve.scalar_tensor_tensor(ser, ser, 1.0 / odd, z2, ALU.add, ALU.mult))
            lam_op(dve.scalar_tensor_tensor(ser, ser, 1.0, z, ALU.add, ALU.mult))
            lam_op(dve.tensor_scalar(big, par_a[:, LAM:LAM + LT], -1.0, 0.0, ALU.mult, ALU.max))
            lam_op(dve.scalar_tensor_tensor(ser, ser, 2.0, big, ALU.mult, ALU.add))
            dve.tensor_scalar(lam[:, 7, :], ser, -LRU_C, 1.0, ALU.mult, ALU.mult).then_inc(lam_ready, 1)

            def lru_square(g):
                dve.wait_ge(lru_t, g + 1)
                dve.wait_ge(lru_aa, g + 1)
                r = tiles(RR + 3 * g, 3)
                dve.scalar_tensor_tensor(r, tiles(XB + 3 * g, 3), 1.0, r, ALU.add, ALU.mult).then_inc(lru_m, 1)

            def lru_scan(g):
                dve.wait_ge(lru_b, g + 1)
                dve.wait_ge(lru_a, g + 1)
                for m in range(3):
                    t = 3 * g + m
                    s = dve.tensor_tensor_scan(tiles(XB + t), tiles(AA + t), tiles(II + t), 0.0, ALU.mult, ALU.add)
                s.then_inc(lru_h, 1)

            def gate_out(c):
                dve.wait_ge(ring_free, 22 + 2 * c)
                dve.tensor_copy(tiles(GATE + 2 * c, 2), bank[4 + c % 2][:, :]).then_inc(gate_raw, 1)

            def gated_h(g):
                dve.wait_ge(lru_silu, (3 * g + 2) // 2 + 1)
                dve.wait_ge(lru_h, g + 1)
                h3 = tiles(XB + 3 * g, 3)
                dve.tensor_tensor(h3, h3, tiles(GATE + 3 * g, 3), ALU.mult).then_inc(y_f, 1)

            def gated_h_lo(g):
                dve.wait_ge(y_hi, g + 1)
                low(8 + 3 * g, tiles(XB + 3 * g, 3), 3).then_inc(y_lo, 1)

            lo(24)
            lo(25)
            gate_out(0)
            lru_square(0)
            lo(26)
            gate_out(1)
            lru_square(1)
            lo(27)
            lru_square(2)
            lo(28)
            gate_out(2)
            lru_square(3)
            lo(29)
            lru_scan(0)
            lo(30)
            lru_scan(1)
            gated_h(0)
            lo(31)
            gated_h(1)
            lru_scan(2)
            gated_h_lo(0)
            lo(32)
            lru_scan(3)
            gated_h_lo(1)
            lo(33)
            dve.wait_ge(par_t, 3)
            dve.tensor_copy(par_b[:, :], bank[6][:, 0:ROWS_B]).then_inc(par_ready, 1)
            dve.wait_ge(par_ready, 3)
            dve.tensor_scalar(q_gain[:, :], par_b[:, Q_G:Q_G + 1], SCALE, 1.0, ALU.mult, ALU.mult).then_inc(qg_ready, 1)
            gated_h(2)
            lo(34)
            gated_h(3)
            gated_h_lo(2)
            lo(35)
            gated_h_lo(3)
            for n in range(36, 40):
                lo(n)
            for n in range(40, 44):
                lo(n)
            norm(1, 1.0, half_of(C_KV), [(1, 8), (2, 0)])

            def head_inv(n):
                w = 2 * TB * (1 if n == 0 else 2)
                dve.wait_ge(hn_std, n + 1)
                dve.reciprocal(rstd[:, 0:w], std[:, 0:w]).then_inc(hn_inv, 1)
                dve.wait_ge(hn_inv, n + 1)
                dve.tensor_copy(heads_rstd[:, 0:w * HD].rearrange("p (h n) -> p h n", n=HD),
                                rstd[:, 0:w].unsqueeze(2).to_broadcast([P, w, HD])).then_inc(hn_rstd, 1)

            def head_scaled(n):
                dve.wait_ge(hn_rb, n + 1)
                dve.wait_ge(q_raw, n + 1)
                if n == 0:
                    t, w, g = 40, 1, par_b[:, K_G:K_G + 1]
                else:
                    t, w, g = 2 * n - 2, 2, q_gain[:, 0:1]
                dve.scalar_tensor_tensor(tiles(t, w), tiles(t, w), g, bank[6][:, 0:w * T], ALU.mult, ALU.mult)\
                    .then_inc(hn_done, 1)

            def swa_out(s):
                dve.wait_ge(ring_free, half_of(C_KV) + 2 + 2 * s)
                if s == 0:
                    dve.wait_ge(k_turned, 1)
                    y = dve.tensor_tensor(tiles(40), bank[7][:, 0:T], spread[:, :], ALU.mult)
                    for tb in range(TB):
                        dve.tensor_scalar(tiles(44)[:, tb * P:(tb + 1) * P], bank[4][:, tb * T + P:(tb + 1) * T],
                                          n_rstd[:, tb:tb + 1], 1.0, ALU.mult, ALU.mult).then_inc(v_raw, 1)
                else:
                    y = rooted(2 * s - 2, swa_bank(s))
                y.then_inc(q_raw, 1)

            dve.wait_ge(qg_ready, 1)
            def swa_slot(j):
                if j == 3:
                    root_inv(1)
                if j == 4:
                    roots_out(1)
                    dve.wait_ge(rstd_ready, 2)
                    swa_out(0)
                    swa_out(1)
                if j % 2 and j >= 5:
                    swa_out(j // 2)
                if j in HEAD_ROOTS:
                    head_scaled(HEAD_ROOTS[j])
                if j == 12:
                    head_scaled(4)
                if j in HEAD_SQUARES:
                    head_inv(HEAD_SQUARES[j])
                if j == 11:
                    head_inv(4)
                lo(48 + j)

            for j in range(12):
                swa_slot(j)

            def masked_max(n, bias, floor):
                dve.wait_ge(s_done, n + 1)
                if n > LAG:
                    dve.wait_ge(t_done, n - LAG)
                s, ps = score_buf(n), bank[n % 2]
                for q, (c, w) in enumerate(((0, P), (P, T))):
                    dve.tensor_tensor_reduce(s[:, c:c + w], ps[:, c:c + w], bias[:, T - w:T], 1.0, floor, ALU.add, ALU.max,
                                             accum_out=top[:, 2 * n + q:2 * n + q + 1]).then_inc(s_max, 1)
                dve.wait_ge(s_max, 2 * n + 2)
                dve.tensor_scalar(ntop[:, 2 * n:2 * n + 2], top[:, 2 * n:2 * n + 2], -1.0, 1.0, ALU.mult, ALU.mult)\
                    .then_inc(s_neg, 1)

            def inverse_sum(n, sinks):
                dve.wait_ge(p_exp, n + 1)
                c = slice(2 * n, 2 * n + 2)
                total = rsum
                if sinks:
                    dve.tensor_tensor(esink[:, c], esink[:, c], rsum[:, c], ALU.add).then_inc(den_sum, 1)
                    dve.wait_ge(den_sum, n + 1)
                    total = esink
                dve.reciprocal(rden[:, c], total[:, c]).then_inc(den_inv, 1)

            dve.wait_ge(sink_in, 16)
            dve.wait_ge(con_in, 16)

            def gated(c):
                dve.wait_ge(silu_b, c + 1)
                dve.wait_ge(o_out, c + 1)
                o2 = tiles(16 + 2 * c, 2)
                dve.tensor_tensor(o2, o2, tiles(8 + 2 * c, 2), ALU.mult).then_inc(yb_f, 1)

            def gated_lo(c):
                dve.wait_ge(yb_hi, c + 1)
                low(8 + 2 * c, tiles(16 + 2 * c, 2), 2).then_inc(yb_lo, 1)

            def heads_out(b):
                dve.wait_ge(o_done, 4 * b + 4)
                dve.tensor_copy(tiles(16 + 2 * b, 2), bank[6 + b % 2][:, :]).then_inc(o_out, 1)

            for r in range(NQ + 2):
                if r < NQ:
                    dve.wait_ge(bias_ready, r + 1)
                    masked_max(r, dist_bias(r), sink[:, r:r + 1])
                if r >= 2:
                    inverse_sum(r - 2, True)
                if r in SWA_LO:
                    swa_slot(SWA_LO[r])
                if r in (11, 14):
                    heads_out((r - 11) // 3)
            gated(0)
            swa_out(8)
            gated_lo(0)
            gated(1)
            lo(65)
            gated_lo(1)
            heads_out(2)
            gated(2)
            gated_lo(2)
            lo(66)
            lo(67)
            heads_out(3)
            gated(3)
            gated_lo(3)
            lo(68)
            lo(69)
            norm(2, 1.0, half_of(C_F1), [(3, 0)])

            def angles():
                t, turns, r = tiles(56), tiles(57), tiles(58)
                n = [0]

                def step(op):
                    n[0] += 1
                    op.then_inc(trig_s, 1)
                    dve.wait_ge(trig_s, n[0])

                dve.wait_ge(pos_in, 16)
                step(dve.tensor_copy(t, pos[:, :]))
                step(dve.tensor_scalar(r, t, par_b[:, FREQ:FREQ + 1], 1.0, ALU.mult, ALU.mult))
                step(dve.tensor_scalar(t, r, 1.0 / TWO_PI, ROUND, ALU.mult, ALU.add))
                step(dve.tensor_scalar(turns, t, -ROUND, 1.0, ALU.add, ALU.mult))
                for part in TURN_PARTS:
                    step(dve.scalar_tensor_tensor(r, turns, -part, r, ALU.mult, ALU.add))
                dve.tensor_scalar(r, r, -PI_LOW, PI_LOW, ALU.max, ALU.min).then_inc(trig_r, 1)

            def ffn(n, c_pair, c_down):
                first, base = n * (FT // 2), half_of(c_pair) + 4

                def pair(j, i=0):
                    gate, up, hid = (tiles(t + 2 * (j % 2), 2) for t in (40, 36, 44))
                    lo(base + 4 * j, i, 8)
                    lo(base + 4 * j + 1, i, 8)
                    if j == 0:
                        lo(base + 2)
                        root_inv(2 * n + 2)
                        lo(base + 3)
                        roots_out(2 * n + 2)
                    dve.wait_ge(ring_free, base + 4 * j - 2 + i * 8)
                    rooted(40 + 2 * (j % 2), 6 - 2 * (j % 2)).then_inc(ff_g, 1)
                    if j:
                        lo(base + 4 * j + 2, i, 8)
                    dve.wait_ge(ring_free, base + 4 * j + i * 8)
                    rooted(36 + 2 * (j % 2), 7 - 2 * (j % 2)).then_inc(ff_u, 1)
                    dve.wait_ge(ff_silu, first + j + 1 + i * 2)
                    dve.wait_ge(ff_u, first + j + 1 + i * 2)
                    dve.tensor_tensor(hid, gate, up, ALU.mult).then_inc(ff_f, 1)
                    if j:
                        lo(base + 4 * j + 3, i, 8)
                    dve.wait_ge(ff_hi, first + j + 1 + i * 2)
                    if j < 3:
                        low(8 + 2 * j, hid, 2).then_inc(ff_lo, 1)
                    else:
                        at = bass.ds(i * 4 + (8 + 2 * j), 2)
                        dve.tensor_tensor(wide(a_lo[:, at, :]), hid, wide(a_hi[:, at, :]).bitcast(F32), ALU.subtract)\
                            .then_inc(ff_lo, 1)

                for j in range(3):
                    pair(j)
                with dve.Fori(0, (FT // 2 - 3) // 2) as i:
                    pair(3, i)
                    pair(4, i)
                if n == 0:
                    angles()
                base_d = half_of(c_down) + 4
                with dve.Fori(0, 4) as i:
                    for h in range(4):
                        lo(base_d + h, i, 4)
                lo(base_d + 16)
                lo(base_d + 17)

            ffn(0, C_F1, C_D1)
            norm(3, FFN_RES, half_of(C_MIX), [(4, 0)])

            def rope(n):
                dve.wait_ge(rope_p, n + 1)
                x = tiles(48 + 2 * (n % 2), 2).rearrange("p (t n) -> p t n", t=2)
                one, two = (tiles(t, 2).rearrange("p (t n) -> p t n", t=2) for t in (52, 54))
                dve.tensor_tensor(one, x, cosine[:, :].unsqueeze(1).to_broadcast([P, 2, T]), ALU.mult).then_inc(rope_a, 1)
                dve.tensor_tensor(two, bank[6][:, :].rearrange("p (t n) -> p t n", t=2),
                                  sine[:, :].unsqueeze(1).to_broadcast([P, 2, T]), ALU.mult).then_inc(rope_a, 1)
                dve.wait_ge(rope_a, 2 * n + 2)
                dve.tensor_tensor(tiles(2 * n, 2), tiles(52, 2), tiles(54, 2), ALU.add).then_inc(rope_done, 1)

            def branch_lo(b):
                dve.wait_ge(ym_hi, b + 1)
                low(8 + 2 * b, bank[6 + b % 2][:, :], 2).then_inc(ym_lo, 1)

            H_M = half_of(C_MIX)

            def mix_out(c):
                dve.wait_ge(ring_free, H_M + 2 * c + 2)
                t = 48 + 2 * (c % 2) if c < 4 else 2 * c - 4 if c < 10 else 2 * c + 8
                rooted(t, mix_bank(c), SCALE if c in (0, 1, 6, 7) else 1.0).then_inc(m_raw, 1)

            def mix_slot(j):
                c = j // 2
                if j == 3:
                    root_inv(3)
                if j == 4:
                    roots_out(3)
                    mix_out(0)
                    mix_out(1)
                if j in ROPE_AT:
                    rope(ROPE_AT.index(j))
                if j == 6:
                    mix_out(2)
                if j % 2 and j >= 7 and c not in (4, 5, 10, 11):
                    mix_out(c)
                lo(H_M + 4 + j)

            dve.wait_ge(trig_ready, 1)
            for j in range(12):
                mix_slot(j)
            for r in range(NH + 5):
                if r < NH:
                    masked_max(NQ + r, con[:, CMASK:CMASK + T], -3e38)
                if 2 <= r < NH + 2:
                    inverse_sum(NQ + r - 2, False)
                if r >= 1:
                    mix_slot(11 + r)
                if r == LAG + 6:
                    branch_lo(0)
            branch_lo(1)
            dve.wait_ge(o_done, NQ + NH)
            for r in range(NH + 5):
                if r < NH:
                    dve.wait_ge(z_done, r + 1)
                    if r >= 6:
                        dve.wait_ge(o_done, NQ + NH + r - 5)
                    dve.tensor_tensor(stick_z(r), bank[r % 2][:, 0:SC], con[:, SBMASK:SBMASK + SC], ALU.add)\
                        .then_inc(z_sb, 1)
                if 1 <= r <= NH:
                    n = r - 1
                    dve.wait_ge(sb_ln, n + 1)
                    if n >= 2:
                        dve.wait_ge(c_done, n - 1)
                    dve.scalar_tensor_tensor(stick_sp(n), stick_z(n), 0.0, stick_ln(n), ALU.max, ALU.add)\
                        .then_inc(sp_done, 1)
                if 3 <= r < NH + 3:
                    n = r - 3
                    dve.wait_ge(c_done, n + 1)
                    dve.tensor_tensor(stick_z(n), stick_z(n), bank[2 + n % 2][:, 0:SC], ALU.subtract).then_inc(d_done, 1)
                for j in (() if r == 0 else (2 * r - 2, 2 * r - 1) if r < 4 else (r + 2,)):
                    mix_slot(24 + j)
                if r == 9:
                    branch_lo(2)
            mix_slot(39)
            branch_lo(3)
            H_B = half_of(C_BR)
            for h in range(4, 8):
                lo(H_B + h)
            for b in range(4):
                if b < 3:
                    dve.wait_ge(br_done, b + 1)
                else:
                    dve.wait_ge(ring_free, H_B + 4)
                dve.wait_ge(g_sig, 2 * b + 2)
                dve.tensor_tensor(tiles(32 + 2 * b, 2), tiles(32 + 2 * b, 2), bank[b][:, :], ALU.mult).then_inc(mg_a, 1)
            lo(H_B + 8)
            lo(H_B + 9)
            def other(b):
                if b < 3:
                    dve.wait_ge(br_done, b + 4)
                else:
                    dve.wait_ge(ring_free, H_B + 8)
                dve.wait_ge(g_sig, KD + 2 * b + 2)
                gb = tiles(40 + 2 * b, 2)
                dve.tensor_tensor(gb, gb, bank[4 + b][:, :], ALU.mult).then_inc(mg_b, 1)

            def merged(b):
                dve.wait_ge(mg_a, b + 1)
                dve.wait_ge(mg_b, b + 1)
                dve.tensor_tensor(tiles(2 * b, 2), tiles(32 + 2 * b, 2), tiles(40 + 2 * b, 2), ALU.add).then_inc(mg_f, 1)

            def merged_lo(b):
                dve.wait_ge(mg_hi, b + 1)
                low(16 + 2 * b, tiles(2 * b, 2), 2).then_inc(mg_lo, 1)

            other(0)
            merged(0)
            other(1)
            merged_lo(0)
            merged(1)
            other(2)
            merged_lo(1)
            lo(H_B + 10)
            merged(2)
            lo(H_B + 11)
            merged_lo(2)
            other(3)
            merged(3)
            merged_lo(3)
            for h in range(12, 16):
                lo(H_B + h)
            norm(4, 1.0, half_of(C_F2), [(5, 0)])
            ffn(1, C_F2, C_D2)

            for b in range(4):
                add(5, b, FFN_RES)
                dve.wait_ge(x_ready, 21 + b)
                for k in (2 * b, 2 * b + 1):
                    dve.tensor_scalar(tiles(XNF + k), xres[:, k, :], GAINS[6][:, k:k + 1], 1.0, ALU.mult, ALU.mult)\
                        .then_inc(xn_ready, 1)
            root_inv(5)
            dve.wait_ge(rstd_ready, 6)
            for q in (1, 3):
                dve.wait_ge(fin_t, q + 1)
                dve.tensor_scalar(tiles(8 + 2 * q, 2), bank[4 + q][:, :], n_rstd[:, 1:2], 1.0, ALU.mult, ALU.mult)\
                    .then_inc(fin_d, 1)


_INS = ["x", "a_norm_g", "a_w_in", "a_conv_w", "a_conv_b", "a_gate_r_w", "a_gate_r_b", "a_gate_i_w", "a_gate_i_b",
        "a_lambda", "a_w_out", "kv_norm_g", "w_kv", "k_norm_g", "b_norm_g", "b_w_in", "q_norm_g", "sinks", "b_w_out",
        "positions_2", "ffn1_norm_2", "ffn1_w_gate_2", "ffn1_w_up_2", "ffn1_w_down_2", "mix_norm_2", "w_in_2",
        "b_gate_2", "w_branch_moba_2", "w_branch_sb_2", "w_out_2", "ffn2_norm_2", "ffn2_w_gate_2", "ffn2_w_up_2",
        "ffn2_w_down_2", "final_norm_2"]


def kernel(**inputs):
    import concourse.bacc as _bacc
    from concourse import mybir as _mybir
    from concourse.bass_utils import run_bass_kernel_spmd as _run

    nc = _bacc.Bacc("TRN2", target_bir_lowering=False, num_devices=1)
    con, freq = constants()
    arrays, args = {"constants": con, "freq": freq}, {}
    for name in _INS:
        arrays[name] = np.ascontiguousarray(inputs[name])
    for name, a in arrays.items():
        args[name] = nc.dram_tensor(name, a.shape, _mybir.dt.from_np(a.dtype), kind="ExternalInput").ap()
    out = nc.dram_tensor("out", (1, T, D), _mybir.dt.float32, kind="ExternalOutput").ap()
    build(nc, args, out)
    r = _run(nc, [arrays], core_ids=[0])
    return r.results[0]["out"]
```

```python
from contextlib import ExitStack

import numpy as np

import concourse.bass as bass
from concourse import mybir

F32 = mybir.dt.float32
F32R = mybir.dt.float32r
I32 = mybir.dt.int32
ACT = mybir.ActivationFunctionType
ALU = mybir.AluOpType
AX = mybir.AxisListType

P = 128
T = 256
TB = T // P
D = 1024
KD = D // P
LRU = 1536
LT = LRU // P
LB = 96
LG = 4
CONV = 4
LRU_C = 8.0
HD = 64
NQ = 16
NH = 8
DFF = 2816
FT = DFF // P
EPS = 1e-6
SCALE = HD ** -0.5
FFN_RES = 0.5
SLOPES = [float(np.float32(2.0 ** (-8.0 * (h + 1) / NQ))) for h in range(NQ)]
SC = T + P
BIG = 1e30
TWO_PI = 2.0 * np.pi
ROUND = 1.5 * 2.0 ** 23
TURN_1 = 6.28125
TURN_2 = float(np.float32(np.round((TWO_PI - TURN_1) * 2.0 ** 19) / 2.0 ** 19))
TURN_PARTS = [TURN_1, TURN_2, TWO_PI - TURN_1 - TURN_2]
PI_LOW = float(np.nextafter(np.float32(np.pi), np.float32(0)))

HALF = 4 * T
RING = 4
GATE_COLS = 896
GATE_TILES = [(0, 0, 0), (1, 0, 256), (0, 1, 128), (1, 1, 384), (2, 1, 640), (1, 2, 512), (2, 2, 768)]
GATE_PIECES = [(0, 0, 96, 0, 0), (1, 0, 32, 96, 96), (1, 32, 64, 0, 256 + 96),
               (2, 0, 64, 64, 256 + 192), (2, 64, 32, 0, 640 + 64), (3, 0, 96, 32, 640 + 160)]

C_X, C_G, C_AO, C_KV, C_Q, C_BG, C_BO, C_F1, C_D1 = 0, 6, 12, 18, 19, 23, 27, 31, 53
C_MIX, C_BR, C_WO, C_F2, C_D2, C_END = 64, 84, 88, 92, 114, 125
H_RI = [8, 14, 16, 18]


def half_of(chunk):
    return 2 * chunk + 2 * sum(h <= 2 * chunk + 2 * g for g, h in enumerate(H_RI))


SPLIT_BY_DVE = range(24, 30)


CONV_W, CONV_B, BR, BI, LAM = 0, 48, 60, 72, 84
ROWS_A = 96
KV_G, B_G, F1_G, MIX_G, F2_G, FIN_G, B_GATE, K_G, Q_G = 0, 8, 16, 24, 32, 40, 48, 64, 65
ROWS_B = 66

ROT = 8
IDENT, TRI, DIST, CMASK, SBMASK, FREQ = 0, 128, 256, 512, 768, 1152
N_CONST = FREQ + ROT

HEAD_ROOT = {5: (0, 1), 6: (2,), 8: (3,), 10: (4,)}
HEAD_TURN = {6: (0, 1), 8: (2,), 10: (3,), 11: (4,)}
SWA_FILL = {0: 10, 1: 11, 2: 12, 3: 13, 5: 14, 8: 15, 12: 16, 16: 17}
SWA_HI = {1: 11, 2: 12, 4: 13, 6: 14, 11: 15, 12: 16}
SWA_LO = {2: 11, 3: 12, 7: 13, 10: 14, 12: 15, 15: 16}
LAG = 4
MIX_TURN = {5: 0, 6: 1, 7: 2, 8: 3}
MOBA_FILL = [1] * 12
STICK_FILL = [1, 2, 2, 1, 1, 2, 1, 1, 2, 1, 0, 2, 0]


def fill(counts, first, r):
    return range(first + sum(counts[:r]), first + sum(counts[:r + 1]))


def swa_bank(s):
    return 0 if s == 2 else 4 + s % 2


MERGED = [(0, 1), (1, 1), (2, 2), (4, 2), (6, 2)]


def mix_bank(c):
    return 7 if c == 2 else 4 + c % 2


def constants():
    c = np.zeros((P, N_CONST), np.float32)
    p = np.arange(P)[:, None]
    j = np.arange(P)[None, :]
    c[:, IDENT:IDENT + P] = p == j
    c[:, TRI:TRI + P] = p >= j
    k = np.arange(T)[None, :]
    dist = P + p - k
    c[:, DIST:DIST + T] = np.where((dist >= 0) & (dist < P), dist, np.float32(1e33))
    c[:, CMASK:CMASK + T] = np.where(dist >= 0, 0.0, -BIG)
    past = np.where(p < j, 0.0, -BIG)
    c[:, SBMASK:SBMASK + P] = past
    c[:, SBMASK + T:SBMASK + SC] = past
    c[:, FREQ:FREQ + ROT] = np.float32(500000.0) ** (-np.arange(ROT, dtype=np.float32) * np.float32(2.0) / np.float32(2 * ROT))
    return c


def build(nc, I, out):
    ctx = ExitStack()
    with ctx:
        def sb(name, shape, dt=F32):
            return ctx.enter_context(nc.sbuf_tensor(name, shape, dt))

        def sem(name):
            return ctx.enter_context(nc.semaphore(name))

        stage = sb("stage", [P, 2, 2, HALF])
        w_hi = sb("w_hi", [P, RING, HALF], F32R)
        w_lo = sb("w_lo", [P, RING, HALF], F32R)
        gate_st = sb("gate_st", [P, 2, 2, GATE_COLS])
        xres = sb("xres", [P, KD, T])
        a_hi = sb("a_hi", [P, 30, T], F32R)
        a_lo = sb("a_lo", [P, 30, T], F32R)
        arena = sb("arena", [P, 62, T])
        rows_n = sb("rows_n", [KD, P])
        rows_a = sb("rows_a", [ROWS_A, P])
        rows_b = sb("rows_b", [ROWS_B, P])
        par_n = sb("par_n", [P, KD])
        par_a = sb("par_a", [P, ROWS_A])
        par_b = sb("par_b", [P, ROWS_B])
        con = sb("con", [P, N_CONST])
        ones = sb("ones", [P, P])
        eps = sb("eps", [P, 1])
        pos = sb("pos", [P, TB], I32)
        angle = sb("angle", [P, 3, TB * ROT])
        sink = sb("sink", [P, NQ])
        cosine = sb("cosine", [P, TB, 2 * ROT])
        sine = sb("sine", [P, TB, 2 * ROT])
        half_pi = sb("half_pi", [P, 1])
        q_gain = sb("q_gain", [P, 1])
        lam = sb("lam", [P, 8, LT])
        n_ms = sb("n_ms", [P, TB])
        n_std = sb("n_std", [P, TB])
        n_rstd = sb("n_rstd", [P, TB])
        spread = sb("spread", [P, T])
        head_sq = sb("head_sq", [P, 5 * 8])
        head_std = sb("head_std", [P, 5 * 8])
        head_inv = sb("head_inv", [P, 5 * 8])
        top = sb("top", [P, 2 * (NQ + NH)])
        ntop = sb("ntop", [P, 2 * (NQ + NH)])
        rsum = sb("rsum", [P, 2 * (NQ + NH)])
        esink = sb("esink", [P, 2 * (NQ + NH)])
        rden = sb("rden", [P, 2 * (NQ + NH)])
        bank = [ctx.enter_context(nc.psum_tensor(f"bank{b}", [P, 512], F32)) for b in range(8)]

        def tiles(t, n=1):
            return arena[:, t:t + n, :].rearrange("p t n -> p (t n)")

        flat = arena[:, :, :].rearrange("p t n -> p (t n)")
        SQ, XNF = 24, 32
        XB, GATE, RR, II, AA = 0, 12, 24, 36, 48

        gate_hi = tiles(AA, 14).rearrange("p (g w n) -> p g w n", g=2, w=2)


        x_in, con_in = sem("x_in"), sem("con_in")
        rows_n_in, rows_a_in, rows_b_in = sem("rows_n_in"), sem("rows_a_in"), sem("rows_b_in")
        pos_in, sink_in, id_in = sem("pos_in"), sem("sink_in"), sem("id_in")
        stage_in = [sem(f"stage_in{q}") for q in range(4)]
        gate_in = [sem("gate_in0"), sem("gate_in1")]
        set_done = sem("set_done")
        hi_done, w_done, ring_free = sem("hi_done"), sem("w_done"), sem("ring_free")
        acc_done, x_ready, sq_ready, ms_ready = sem("acc_done"), sem("x_ready"), sem("sq_ready"), sem("ms_ready")
        std_ready, rstd_ready, rb_ready, rb_sb = sem("std_ready"), sem("rstd_ready"), sem("rb_ready"), sem("rb_sb")
        xn_ready, xh_ready, xl_ready = sem("xn_ready"), sem("xh_ready"), sem("xl_ready")
        par_t, par_ready, lam_e, lam_step, lam_ready = (
            sem(n) for n in ("par_t", "par_ready", "lam_e", "lam_step", "lam_ready"))
        conv_b, conv_s, conv_x, xbh, xbl = sem("conv_b"), sem("conv_s"), sem("conv_x"), sem("xbh"), sem("xbl")
        ri_sig = sem("ri_sig")
        lru_a, lru_t, lru_aa, lru_m, lru_s, lru_bx, lru_b, lru_h, lru_silu = (
            sem(n) for n in ("lru_a", "lru_t", "lru_aa", "lru_m", "lru_s", "lru_bx", "lru_b", "lru_h", "lru_silu"))
        gate_raw, y_f, y_hi, y_lo = sem("gate_raw"), sem("y_f"), sem("y_hi"), sem("y_lo")
        qg_ready = sem("qg_ready")
        hn_inv, hi_dve = sem("hn_inv"), sem("hi_dve")
        v_raw, tok_raw = sem("v_raw"), sem("tok_raw")
        sq_add, sq_sum = sem("sq_add"), sem("sq_sum")
        q_raw, hn_sq, hn_sum, hn_std, hn_tok, hn_turn, hn_done = (
            sem(n) for n in ("q_raw", "hn_sq", "hn_sum", "hn_std", "hn_tok", "hn_turn", "hn_done"))
        bias_ready, s_done, s_max, s_neg, p_exp, den_sum, den_inv, p_norm, t_done, t_out, o_done, o_out = (
            sem(n) for n in ("bias_ready", "s_done", "s_max", "s_neg", "p_exp", "den_sum", "den_inv", "p_norm",
                             "t_done", "t_out", "o_done", "o_out"))
        ff_g, ff_u, m_val = sem("ff_g"), sem("ff_u"), sem("m_val")
        silu_b, yb_f, yb_hi, yb_lo = sem("silu_b"), sem("yb_f"), sem("yb_hi"), sem("yb_lo")
        ff_silu, ff_f, ff_hi, ff_lo = sem("ff_silu"), sem("ff_f"), sem("ff_hi"), sem("ff_lo")
        trig_s, trig_r, trig_abs, trig_ready = sem("trig_s"), sem("trig_r"), sem("trig_abs"), sem("trig_ready")
        m_raw, rope_a, rope_done = sem("m_raw"), sem("rope_a"), sem("rope_done")
        rope_turn, rope_out = sem("rope_turn"), sem("rope_out")
        z_done, z_sb, sb_abs, sb_exp, sb_ln, sp_done, c_done, d_done, w_exp = (
            sem(n) for n in ("z_done", "z_sb", "sb_abs", "sb_exp", "sb_ln", "sp_done", "c_done", "d_done", "w_exp"))
        ym_hi, ym_lo, g_sig = sem("ym_hi"), sem("ym_lo"), sem("g_sig")
        br_done, mg_a, mg_b, mg_f, mg_hi, mg_lo = (
            sem(n) for n in ("br_done", "mg_a", "mg_b", "mg_f", "mg_hi", "mg_lo"))
        fin_t, fin_a, fin_d, out_done = sem("fin_t"), sem("fin_a"), sem("fin_d"), sem("out_done")

        def source(n):
            for g, h in enumerate(H_RI):
                if n in (h, h + 1):
                    return (gate_st, gate_hi)[g // 2][:, g % 2, n - h, :], gate_in[g // 2], 16 * 2 * len(GATE_PIECES)
            chunk = next(c for c in range(C_END) if half_of(c) == n - n % 2)
            return stage[:, chunk % 2, n % 2, :], stage_in[2 * (chunk % 2) + n % 2], 16 * (chunk // 2 + 1)

        def wide(t3):
            return t3.rearrange("p t n -> p (t n)")

        def score_buf(n):
            return flat[:, 24 * T + n % (LAG + 1) * SC:24 * T + (n % (LAG + 1) + 1) * SC]

        def prob_t(n):
            at = 24 * T + (LAG + 1 + n % 3) * SC
            return flat[:, at:at + SC]

        def dist_bias(n):
            return tiles(53 + n % 6)

        def stick_z(n):
            return flat[:, 48 * T + (n % 6) * SC:48 * T + (n % 6 + 1) * SC]

        def stick_sp(n):
            return flat[:, 24 * T + (n % 2) * SC:24 * T + (n % 2 + 1) * SC]

        def stick_ln(n):
            return flat[:, 27 * T + (n % 3) * SC:27 * T + (n % 3 + 1) * SC]


        def mix_tok(n):
            return tiles(48 + 2 * (n % 2), 2)

        def by_tok(n):
            return tiles(47) if n == 0 else tiles(36 + 2 * (n % 2), 2)

        def tok_sq(n):
            return tiles(49 + 2 * (n % 2), 1 if n == 0 else 2)

        def head_cols(n):
            return slice(8 * n, 8 * n + (4 if n == 0 else 8))

        k_twice = tiles(45, 2)
        ident = con[:, IDENT:IDENT + P]
        GAINS = [par_n[:, :]] + [par_b[:, g:g + KD] for g in (KV_G, B_G, F1_G, MIX_G, F2_G, FIN_G)]

        block = ctx.enter_context(nc.Block())

        @block.sync
        def _(sp):
            sp.dma_start(ident, I["constants"][:, IDENT:IDENT + P]).then_inc(id_in, 16)
            sp.dma_start(rows_n[:, :], I["a_norm_g"].rearrange("o (k p) -> (o k) p", p=P)).then_inc(rows_n_in, 16)
            xt = I["x"].rearrange("o (b p) d -> p (o b) d", p=P)
            sp.dma_start(tiles(0, 8).rearrange("p (b d) -> p b d", b=TB), xt).then_inc(x_in, 16)

            def load(chunk, src, first=None):
                n = src.shape[1] // 2
                for h in range(2):
                    if first is not None:
                        sp.wait_ge(w_done, first + h)
                    sp.dma_start(stage[:, chunk % 2, h, :].rearrange("p (b n) -> p b n", b=n),
                                 src[:, h * n:(h + 1) * n, :]).then_inc(stage_in[2 * (chunk % 2) + h], 16)

            def col(w, j):
                return w.rearrange("(k p) n -> p k n", p=P)[:, :, bass.ds(j * T, T)]

            def row(w, j):
                return w[bass.ds(j * T, T), :].rearrange("(k p) n -> p k n", p=P)

            def split(chunk):
                return half_of(chunk) + 1

            def stream(chunk, n, view):
                j = 0
                while j < n and chunk + j < C_G + 2:
                    load(chunk + j, view(j), split(chunk + j - 2) if chunk + j >= 2 else None)
                    j += 1
                turns = (n - j) // 2
                if turns > 1:
                    base = split(chunk + j - 2)
                    with sp.Fori(0, turns) as i:
                        for b in range(2):
                            load(chunk + j + b, view(i * 2 + (j + b)), base + 2 * b + i * 4)
                    j += 2 * turns
                for r in range(j, n):
                    load(chunk + r, view(r), split(chunk + r - 2))

            def pairs(chunk, wa, wb):
                base = split(chunk - 2)
                with sp.Fori(0, DFF // T) as i:
                    load(chunk, col(wa, i), base + i * 4)
                    load(chunk + 1, col(wb, i), base + 2 + i * 4)

            w_in, w_out = I["a_w_in"][0], I["a_w_out"][0]
            stream(C_X, 6, lambda j: col(w_in, j))
            stream(C_G, 6, lambda j: col(w_in, j + 6))
            stream(C_AO, 6, lambda j: row(w_out, j))
            stream(C_KV, 1, lambda j: col(I["w_kv"], j))
            stream(C_Q, 8, lambda j: col(I["b_w_in"][0], j))
            stream(C_BO, 4, lambda j: row(I["b_w_out"][0], j))
            pairs(C_F1, I["ffn1_w_gate_2"][0], I["ffn1_w_up_2"][0])
            stream(C_D1, 11, lambda j: row(I["ffn1_w_down_2"][0], j))
            stream(C_MIX, 20, lambda j: col(I["w_in_2"][0], j))
            stream(C_BR, 2, lambda j: row(I["w_branch_moba_2"][0], j))
            stream(C_BR + 2, 2, lambda j: row(I["w_branch_sb_2"][0], j))
            stream(C_WO, 4, lambda j: row(I["w_out_2"][0], j))
            pairs(C_F2, I["ffn2_w_gate_2"][0], I["ffn2_w_up_2"][0])
            stream(C_D2, 11, lambda j: row(I["ffn2_w_down_2"][0], j))

            o = out.rearrange("o (b p) (h n) -> (o b) h p n", p=P, h=2)
            for q, (half, b) in enumerate([(0, 0), (0, 1), (1, 0), (1, 1)]):
                sp.wait_ge((fin_a, fin_d)[q % 2], q // 2 + 1)
                sp.dma_start(o[b, half], tiles(8 + 2 * q, 2)).then_inc(out_done, 16)
            sp.wait_ge(out_done, 64)

        @block.gpsimd
        def _(pool):
            pool.memset(ones[:, :], 1.0).then_inc(set_done, 1)
            pool.memset(eps[:, :], EPS).then_inc(set_done, 1)
            pool.memset(half_pi[:, :], float(np.pi / 2)).then_inc(set_done, 1)
            pool.memset(gate_st[:, :, :, :], 0.0).then_inc(set_done, 1)
            pool.memset(tiles(AA, 14), 0.0).then_inc(set_done, 1)

            for pair, place in enumerate((gate_st, gate_hi)):
                pool.wait_ge(set_done, 4 + pair)
                for w, name in enumerate(("a_gate_r_w", "a_gate_i_w")):
                    blocks = I[name][0].rearrange("(g b) i j -> b i g j", b=4)
                    for b, r, n, p, c in GATE_PIECES:
                        pool.dma_start(place[p:p + n, :, w, c:c + LB], blocks[b, r:r + n, 2 * pair:2 * pair + 2, :])\
                            .then_inc(gate_in[pair], 16)
            for first, name, n in ((F1_G, "ffn1_norm_2", KD), (MIX_G, "mix_norm_2", KD), (F2_G, "ffn2_norm_2", KD),
                                   (B_GATE, "b_gate_2", 2 * KD), (B_G, "b_norm_g", KD)):
                pool.dma_start(rows_b[first:first + n, :], I[name].rearrange("o (k p) -> (o k) p", p=P))\
                    .then_inc(rows_b_in, 16)
            for first, name in ((KV_G, "kv_norm_g"), (FIN_G, "final_norm_2")):
                pool.dma_start(rows_b[first:first + KD, :], I[name].rearrange("(k p) -> k p", p=P))\
                    .then_inc(rows_b_in, 16)
            for h in range(2):
                pool.dma_start(rows_b[K_G:K_G + 1, h * HD:(h + 1) * HD], I["k_norm_g"].rearrange("(o d) -> o d", o=1))\
                    .then_inc(rows_b_in, 16)
                pool.dma_start(rows_b[Q_G:Q_G + 1, h * HD:(h + 1) * HD], I["q_norm_g"]).then_inc(rows_b_in, 16)
            pool.dma_start(con[:, P:N_CONST], I["constants"][:, P:N_CONST]).then_inc(con_in, 16)
            pool.dma_start(pos[:, :], I["positions_2"].rearrange("o (b p) -> p (o b)", p=P),
                           allow_slow_non_contiguous=True).then_inc(pos_in, 16)
            pool.dma_start(sink[:, :], I["sinks"].to_broadcast([P, NQ])).then_inc(sink_in, 16)
            pool.wait_ge(xbl, 6)
            for g in range(LG):
                pool.wait_ge(ri_sig, 2 * g + 2)
                pool.tensor_tensor(tiles(II + 3 * g, 3), tiles(II + 3 * g, 3), tiles(XB + 3 * g, 3), ALU.mult)\
                    .then_inc(lru_bx, 1)
            for g in range(LG):
                pool.wait_ge(lru_a, g + 1)
                pool.wait_ge(lru_bx, g + 1)
                pool.tensor_tensor(tiles(XB + 3 * g, 3), tiles(AA + 3 * g, 3), tiles(AA + 3 * g, 3), ALU.mult)\
                    .then_inc(lru_aa, 1)
            for g in range(LG):
                pool.wait_ge(lru_s, g + 1)
                pool.wait_ge(lru_bx, g + 1)
                i3 = tiles(II + 3 * g, 3)
                pool.tensor_tensor(i3, i3, tiles(RR + 3 * g, 3), ALU.mult).then_inc(lru_b, 1)
            for g in range(LG - 1):
                pool.wait_ge(lru_h, g + 1)
                pool.wait_ge(lru_silu, (3 * g + 2) // 2 + 1)
                h3 = tiles(XB + 3 * g, 3)
                pool.tensor_tensor(h3, h3, tiles(GATE + 3 * g, 3), ALU.mult).then_inc(y_f, 1)

            def square_sums(n):
                def square(b):
                    x = wide(xres[:, 2 * b:2 * b + 2, :])
                    pool.wait_ge(x_ready, 4 * n + b + 1)
                    pool.tensor_tensor(tiles(SQ + 2 * b, 2), x, x, ALU.mult).then_inc(sq_ready, 1)

                def plus(a, b, w):
                    pool.tensor_tensor(tiles(SQ + a, w), tiles(SQ + a, w), tiles(SQ + b, w), ALU.add).then_inc(sq_add, 1)

                square(0)
                square(1)
                pool.wait_ge(sq_ready, 4 * n - 2)
                plus(0, 2, 2)
                square(2)
                square(3)
                pool.wait_ge(sq_ready, 4 * n)
                plus(4, 6, 2)
                pool.wait_ge(sq_add, 3 * n - 1)
                plus(0, 4, 2)
                pool.wait_ge(sq_add, 3 * n)
                pool.tensor_tensor(tiles(SQ), tiles(SQ), tiles(SQ + 1), ALU.add).then_inc(sq_sum, 1)

            square_sums(1)
            def normalise(n):
                pool.wait_ge(den_inv, n + 1)
                s = score_buf(n)
                pool.tensor_scalar(s[:, 0:P], s[:, 0:P], rden[:, 2 * n:2 * n + 1], 1.0, ALU.mult, ALU.mult)\
                    .then_inc(p_norm, 1)
                pool.tensor_scalar(s[:, P:SC], s[:, P:SC], rden[:, 2 * n + 1:2 * n + 2], 1.0, ALU.mult, ALU.mult)\
                    .then_inc(p_norm, 1)

            pool.wait_ge(con_in, 16)
            pool.wait_ge(hn_done, 1)
            for r in range(-3, NQ + 2):
                if r + 3 < NQ:
                    if r >= 3:
                        pool.wait_ge(s_max, 2 * (r - 2))
                    pool.tensor_scalar(dist_bias(r + 3), con[:, DIST:DIST + T], -SLOPES[r + 3], 1.0, ALU.mult, ALU.mult)\
                        .then_inc(bias_ready, 1)
                if r >= 2:
                    normalise(r - 2)
            square_sums(2)
            square_sums(3)
            for h in range(NH):
                normalise(NQ + h)
            square_sums(4)
            for k in range(KD):
                pool.wait_ge(x_ready, 21 + k // 2)
                pool.tensor_scalar(tiles(XNF + k), xres[:, k, :], GAINS[6][:, k:k + 1], 1.0, ALU.mult, ALU.mult)\
                    .then_inc(xn_ready, 1)

        @block.tensor
        def _(pe):
            SPLIT = ((w_hi, a_hi), (w_hi, a_lo), (w_lo, a_hi))

            def passes(dst, slot, c, k, start, stop):
                for n, (w, a) in enumerate(SPLIT):
                    mm = pe.matmul(dst, w[:, slot, c:c + P],
                                   a[:, k, :] if isinstance(k, int) else wide(a[:, bass.ds(k, 1), :]),
                                   start=start and n == 0, stop=stop and n == 2, skip_group_check=True)
                return mm

            def by_token(dst, slot, c, n, k, tb, start, stop):
                for i, (w, a) in enumerate(SPLIT):
                    mm = pe.matmul(dst, a[:, k, tb * P:(tb + 1) * P], w[:, slot, c:c + n],
                                   start=start and i == 0, stop=stop and i == 2, skip_group_check=True)
                return mm

            def col_half(chunk, h, b, first_tile=0, normed=None, ready=None, token=False):
                half = half_of(chunk) + h
                pe.wait_ge(w_done, half + 1 if ready is None else ready)
                for kk in range(4):
                    k = 4 * h + kk
                    if normed is not None:
                        pe.wait_ge(xl_ready, KD * normed + k + 1)
                    if token:
                        for tb in range(TB):
                            mm = by_token(bank[b][:, tb * T:(tb + 1) * T], half % RING, kk * T, T,
                                          first_tile + k, tb, k == 0 and tb == 0, k == KD - 1)
                        continue
                    for m in range(2):
                        mm = passes(bank[b][:, m * T:(m + 1) * T], half % RING, kk * T + m * P,
                                    first_tile + k, k == 0 and m == 0, k == KD - 1)
                mm.then_inc(ring_free, 1)

            def col_chunk(chunk, b, **kw):
                for h in range(2):
                    col_half(chunk, h, b, **kw)

            def row_half(chunk, h, k, acc=(0, 1, 2, 3), first=False, last=None, ready=None, later=None):
                half = half_of(chunk) + h
                pe.wait_ge(w_done, half + 1 if ready is None else ready)
                for m in range(KD):
                    if later is not None and m == KD // 2:
                        pe.wait_ge(*later)
                    mm = passes(bank[acc[m // 2]][:, (m % 2) * T:(m % 2 + 1) * T], half % RING, m * P, k,
                                first and m % 2 == 0, last is not None)
                    if last is not None and m in (1, 3, 5):
                        mm.then_inc(last, 1)
                mm.then_inc(ring_free, 1)

            def mean_squares(n, b):
                pe.wait_ge(sq_sum, n)
                for tb in range(TB):
                    mm = pe.matmul(bank[b][:, tb:tb + 1], tiles(SQ)[:, tb * P:(tb + 1) * P], ones[:, 0:1],
                                   start=True, stop=True)
                mm.then_inc(ms_ready, 1)

            def roots(n, b):
                pe.wait_ge(rstd_ready, n + 1)
                for tb in range(TB):
                    mm = pe.matmul(bank[b][:, tb * P:(tb + 1) * P], n_rstd[:, tb:tb + 1].to_broadcast([P, P]),
                                   ident, start=True, stop=True)
                mm.then_inc(rb_ready, 1)

            pe.wait_ge(id_in, 16)
            pe.wait_ge(rows_n_in, 16)
            pe.transpose(bank[5][:, 0:KD], rows_n[:, :], con[0:KD, IDENT:IDENT + KD]).then_inc(par_t, 1)
            pe.wait_ge(x_in, 16)
            xtok = tiles(0, 8).rearrange("p (b d) -> p b d", b=TB)
            for m in range(KD):
                for tb in range(TB):
                    c = (m % 2) * T + tb * P
                    mm = pe.transpose(bank[m // 2][:, c:c + P], xtok[:, tb, m * P:(m + 1) * P], ident)
                if m % 2:
                    mm.then_inc(acc_done, 1)
                if m == 3:
                    roots(0, 6)

            def gates(g):
                banks = ((0, 1, 2), (3, 6, 7))[g % 2]
                for w in range(2):
                    half = H_RI[g] + w
                    pe.wait_ge(w_done, half + 1)
                    if w == 0:
                        pe.wait_ge(xbl, (3 * g + 2) // 2 + 1)
                        if g == 1:
                            pe.wait_ge(par_ready, 2)
                        if g >= 2:
                            pe.wait_ge(ri_sig, 2 * (g - 1))
                    done = [0, 0, 0]
                    for k, m, c in GATE_TILES:
                        q = 3 * w + m
                        done[m] += 1
                        mm = passes(bank[banks[q // 2]][:, (q % 2) * T:(q % 2 + 1) * T], half % RING, c, 8 + 3 * g + k,
                                    done[m] == 1 and q % 2 == 0, done[m] == (2, 3, 2)[m])
                    mm.then_inc(ring_free, 1)

            for c in range(6):
                if c == 1:
                    pe.wait_ge(par_ready, 1)
                if c >= 2:
                    pe.wait_ge(conv_x, 2 * (c - 1))
                col_chunk(C_X + c, 4 + c % 2, normed=0)
                if c == 0:
                    pe.wait_ge(rows_a_in, 16 * 5)
                    pe.wait_ge(x_ready, 4)
                    pe.transpose(bank[3][:, 0:ROWS_A], rows_a[:, :], con[0:ROWS_A, IDENT:IDENT + ROWS_A])\
                        .then_inc(par_t, 1)
                if c == 3:
                    gates(0)
            for g in range(1, LG):
                gates(g)

            pe.wait_ge(conv_x, LT)
            for c in range(6):
                if 2 <= c < 5:
                    pe.wait_ge(gate_raw, c - 1)
                if c == 5:
                    pe.wait_ge(lru_silu, 4)
                col_chunk(C_G + c, 4 + c % 2)
                if c == 2:
                    pe.wait_ge(ri_sig, 2 * LG)
                    pe.wait_ge(rows_b_in, 16 * 11)
                    pe.transpose(bank[6][:, 0:ROWS_B], rows_b[:, :], con[0:ROWS_B, IDENT:IDENT + ROWS_B])\
                        .then_inc(par_t, 1)
            for c in range(6):
                for h in range(2):
                    pe.wait_ge(y_lo, (2 * c + h) // 3 + 1)
                    row_half(C_AO + c, h, 8 + 2 * c + h, first=c == 0 and h == 0,
                             last=acc_done if c == 5 and h == 1 else None)

            def head_turn(n):
                pe.wait_ge(hn_tok, n + 1)
                if n >= 2:
                    pe.wait_ge(hn_done, n - 1)
                src = k_twice if n == 0 else by_tok(n)
                for m in range(2):
                    for tb in range(TB):
                        mm = pe.transpose(bank[6 + n % 2][:, m * T + tb * P:m * T + (tb + 1) * P],
                                          src[:, tb * T + m * P:tb * T + (m + 1) * P], ident)
                mm.then_inc(hn_turn, 1)

            def swa_half(j):
                s, h = divmod(j, 2)
                if h == 0 and s >= 3:
                    last = {3: 1, 4: 0}.get(s, s - 2)
                    if last < 5:
                        pe.wait_ge(tok_raw, last + 1)
                    else:
                        pe.wait_ge(q_raw, last - 4)
                    if last == 0:
                        pe.wait_ge(v_raw, 2)
                if s == 0:
                    col_half(C_KV, h, 4, first_tile=8, normed=1, token=True)
                else:
                    col_half(C_KV + s, h, swa_bank(s), normed=2 if s == 1 else None, token=s < 5)

            pe.wait_ge(con_in, 16)
            for j in range(min(SWA_FILL.values())):
                swa_half(j)
                if j == 3:
                    mean_squares(1, 2)
                if j == 4:
                    roots(1, 3)
                for n in HEAD_TURN.get(j, ()):
                    head_turn(n)

            def scores(n, q, k, hrow, t):
                if n < NQ:
                    pe.wait_ge(hn_done, 2 + n // 4)
                if n >= 2:
                    pe.wait_ge(s_max, 2 * (n - 1))
                r = slice(hrow * HD, (hrow + 1) * HD)
                s = bank[n % 2]
                pe.matmul(s[:, 0:P], q[r, t * T:t * T + P], k[r, 0:P], start=True, stop=True)
                pe.matmul(s[:, P:SC], q[r, t * T + P:(t + 1) * T], k[r, 0:T], start=True, stop=True)\
                    .then_inc(s_done, 1)

            def turn(n):
                pe.wait_ge(p_norm, 2 * n + 2)
                if n >= 2:
                    pe.wait_ge(t_out, n - 1)
                p = score_buf(n)
                for c in range(3):
                    mm = pe.transpose(bank[2 + n % 2][:, c * P:(c + 1) * P], p[:, c * P:(c + 1) * P], ident)
                mm.then_inc(t_done, 1)

            def values(n, o, v, w):
                r = (n % 2) * HD
                dst = bank[o][r:r + HD, (n // 2 % 2) * T:(n // 2 % 2 + 1) * T]
                pe.matmul(dst, v[0], w[:, 0:T], start=True, stop=False, skip_group_check=True)
                pe.matmul(dst[:, P:T], v[1], w[:, T:SC], start=False, stop=True, skip_group_check=True)\
                    .then_inc(o_done, 1)

            def gated_out(c, h):
                if c == 0 and h == 0:
                    pe.wait_ge(s_max, 2 * NQ)
                if h == 0:
                    pe.wait_ge(yb_lo, c + 1)
                row_half(C_BO + c, h, 8 + 2 * c + h, acc=(0, 1, 4, 5), first=c == 0 and h == 0,
                         last=acc_done if c == 3 and h == 1 else None,
                         later=(q_raw, 4) if c == 0 and h == 0 else None)

            vt = tiles(44)
            pe.wait_ge(tok_raw, 3)
            for r in range(NQ + LAG + 2):
                if r < NQ:
                    scores(r, tiles(0, 8), tiles(41 + r // 8), r % 2, r // 2)
                if LAG <= r < NQ + LAG:
                    turn(r - LAG)
                if r >= LAG + 2:
                    n = r - LAG - 2
                    pe.wait_ge(t_out, n + 1)
                    if n == 0:
                        pe.wait_ge(hn_done, 5)
                    if n % 4 == 0 and n >= 8:
                        pe.wait_ge(o_out, n // 4 - 1)
                    kv = n // 8 * HD
                    values(n, 6 + (n // 4) % 2, [vt[:, tb * P + kv:tb * P + kv + HD] for tb in range(TB)], prob_t(n))
                if r in SWA_FILL:
                    swa_half(SWA_FILL[r])
                    for i in HEAD_TURN.get(SWA_FILL[r], ()):
                        head_turn(i)
                if r > NQ:
                    gated_out(*divmod(r - NQ - 1, 2))
            for j in range(LAG + 1, 8):
                gated_out(*divmod(j, 2))

            def ffn(n, c_pair, c_down, normed):
                first = n * (FT // 2)

                def pair(j, i=0, normed=None):
                    if j >= 2:
                        pe.wait_ge(ff_u, first + j - 1 + i * 2)
                    for u in range(2):
                        for h in range(2):
                            half = half_of(c_pair) + 4 * j + 2 * u + h
                            col_half(c_pair + u, h, 6 - 2 * (j % 2) + u, normed=normed if u == 0 else None,
                                     ready=half + 1 + i * 8)
                            if j == 0 and (u, h) == (1, 1):
                                mean_squares(2 * n + 2, 2)
                            if j == 1 and (u, h) == (0, 0):
                                roots(2 * n + 2, 3)

                pair(0, normed=normed)
                pair(1)
                pair(2)
                with pe.Fori(0, (FT // 2 - 3) // 2) as i:
                    pair(3, i)
                    pair(4, i)
                for c in range(2):
                    pe.wait_ge(ff_lo, first + c + 1)
                    for h in range(2):
                        row_half(c_down + c, h, 8 + 2 * c + h, first=c == 0 and h == 0)
                base = half_of(c_down)
                with pe.Fori(0, 4) as i:
                    for c in range(2):
                        pe.wait_ge(ff_lo, i * 2 + (first + c + 3))
                        for h in range(2):
                            row_half(c_down + c, h, i * 4 + (12 + 2 * c + h), ready=i * 4 + (base + 5 + 2 * c + h))
                pe.wait_ge(ff_lo, first + 11)
                row_half(c_down + 10, 0, 8 + 20)
                row_half(c_down + 10, 1, 8 + 21, last=acc_done)

            ffn(0, C_F1, C_D1, normed=3)

            VALUES = (4, 5, 10, 11)

            def mix_half(j):
                c, h = divmod(j, 2)
                if h == 0 and c >= 3:
                    p = c - 2
                    before = sum(v < p for v in VALUES)
                    if p in VALUES:
                        pe.wait_ge(m_val, before + 1)
                    else:
                        pe.wait_ge(m_raw, p - before + 1)
                col_half(C_MIX + c, h, mix_bank(c), normed=4 if c == 0 else None, token=c < 4 or c in VALUES)

            for j in range(12):
                mix_half(j)
                if j == 3:
                    mean_squares(3, 2)
                if j == 4:
                    roots(3, 3)
                if j in MIX_TURN:
                    n = MIX_TURN[j]
                    pe.wait_ge(rope_done, n + 1)
                    if n:
                        pe.wait_ge(rope_out, n)
                    for t in range(2):
                        for tb in range(TB):
                            mm = pe.transpose(bank[6][:, t * T + tb * P:t * T + (tb + 1) * P],
                                              mix_tok(n)[:, tb * T + t * P:tb * T + (t + 1) * P], ident)
                    mm.then_inc(rope_turn, 1)
            pe.wait_ge(rope_out, 4)

            v = tiles(16, 4)
            for r in range(NH + LAG + 2):
                n = NQ + r
                if r < NH:
                    scores(n, tiles(0, 4), tiles(4 + r // 2), r % 2, r // 2)
                if LAG <= r < NH + LAG:
                    turn(n - LAG)
                if r >= LAG + 2:
                    h = r - LAG - 2
                    pe.wait_ge(t_out, NQ + h + 1)
                    pe.wait_ge(m_val, 2)
                    values(NQ + h, 6 + h // 4, [v[:, tb * 512 + h * HD:tb * 512 + (h + 1) * HD] for tb in range(TB)],
                           prob_t(NQ + h))
                for j in fill(MOBA_FILL, 12, r):
                    mix_half(j)
            pe.wait_ge(m_raw, 8)
            pe.wait_ge(s_max, 2 * (NQ + NH))
            v = tiles(20, 4)
            for r in range(NH + 5):
                if r < NH:
                    if r >= 2:
                        pe.wait_ge(z_sb, r - 1)
                    q, k, z = tiles(8 + r // 2), tiles(12 + r // 2), bank[r % 2]
                    s = slice((r % 2) * HD, (r % 2 + 1) * HD)
                    pe.matmul(z[:, 0:T], k[s, 0:P], q[s, 0:T], start=True, stop=True)
                    pe.matmul(z[:, T:SC], k[s, P:T], q[s, P:T], start=True, stop=True).then_inc(z_done, 1)
                if r == 2:
                    pe.wait_ge(t_out, NQ + NH)
                if r == 5:
                    pe.wait_ge(m_val, 4)
                if 2 <= r < NH + 2:
                    n = r - 2
                    pe.wait_ge(sp_done, n + 1)
                    if n >= 2:
                        pe.wait_ge(d_done, n - 1)
                    sums, sp_n = bank[2 + n % 2], stick_sp(n)
                    pe.matmul(sums[:, 0:SC], con[:, TRI:TRI + P], sp_n, start=True, stop=False, skip_group_check=True)
                    pe.matmul(sums[:, P:T], ones[:, :], sp_n[:, T:SC], start=False, stop=True, skip_group_check=True)\
                        .then_inc(c_done, 1)
                if r >= 5:
                    h = r - 5
                    pe.wait_ge(w_exp, h + 1)
                    if h % 4 == 0:
                        pe.wait_ge(ym_lo, h // 4 + 1)
                    values(h, 6 + h // 4, [v[:, tb * 512 + h * HD:tb * 512 + (h + 1) * HD] for tb in range(TB)], stick_z(h))
                for j in fill(STICK_FILL, 24, r):
                    mix_half(j)
            pe.wait_ge(d_done, NH)
            for c in range(2):
                for h in range(2):
                    row_half(C_BR + c, h, 8 + 2 * c + h, first=c == 0 and h == 0, last=br_done if c and h else None)
            pe.wait_ge(m_raw, 16)
            pe.wait_ge(ym_lo, 4)
            for c in range(2):
                for h in range(2):
                    row_half(C_BR + 2 + c, h, 12 + 2 * c + h, acc=(4, 5, 6, 7), first=c == 0 and h == 0,
                             last=br_done if c and h else None)
            pe.wait_ge(mg_a, 4)
            for c in range(4):
                for h in range(2):
                    pe.wait_ge(mg_lo, sum(t <= 2 * c + h for t, _ in MERGED))
                    row_half(C_WO + c, h, 16 + 2 * c + h, first=c == 0 and h == 0,
                             last=acc_done if c == 3 and h == 1 else None)
            ffn(1, C_F2, C_D2, normed=5)

            for b in range(4):
                pe.wait_ge(sq_ready, 16 + b + 1)
                for k in (2 * b, 2 * b + 1):
                    for tb in range(TB):
                        mm = pe.matmul(bank[0][:, tb:tb + 1], tiles(SQ + k)[:, tb * P:(tb + 1) * P], ones[:, 0:1],
                                       start=k == 0 and tb == 0, stop=k == KD - 1, skip_group_check=True)
            mm.then_inc(ms_ready, 1)
            for k in range(KD):
                pe.wait_ge(xn_ready, KD + k + 1)
                for tb in range(TB):
                    c = (k % 4) * P
                    mm = pe.transpose(bank[4 + (k // 4) * 2 + tb][:, c:c + P], tiles(XNF + k)[:, tb * P:(tb + 1) * P],
                                      ident)
                    if k % 4 == 3:
                        mm.then_inc(fin_t, 1)

        @block.scalar
        def _(act):
            def f(out_, in_, func, **kw):
                return nc.scalar.activation(out_, in_, func, **kw)

            def hi(n, i=0, step=0):
                if n >= half_of(C_END) or n in SPLIT_BY_DVE:
                    return
                src, landed, count = source(n)
                act.wait_ge(landed, count + i * (16 * step // 4))
                if n >= RING:
                    act.wait_ge(ring_free, n - RING + 1 + i * step)
                f(w_hi[:, n % RING, 0:src.shape[-1]], src, ACT.Copy).then_inc(hi_done, 1)

            def squares(n):
                for b in range(4):
                    act.wait_ge(x_ready, 4 * n + b + 1)
                    f(tiles(SQ + 2 * b, 2), wide(xres[:, 2 * b:2 * b + 2, :]), ACT.Square).then_inc(sq_ready, 1)

            def root(n):
                act.wait_ge(ms_ready, TB + n)
                f(n_std[:, :], bank[0 if n == 5 else 2][:, 0:TB], ACT.Sqrt, scale=1.0 / D, bias=eps[:, 0:1])\
                    .then_inc(std_ready, 1)

            def gained_hi(s, dst, k):
                f(a_hi[:, dst + k, :], xres[:, k, :], ACT.Identity, scale=GAINS[s][:, k:k + 1]).then_inc(xh_ready, 1)

            def norm(n, half, sets):
                act.preload_act_table(ACT.Sqrt)
                for h in range(3):
                    hi(half + h)
                for b in range(4):
                    act.wait_ge(x_ready, 4 * n + b + 1)
                    for k in (2 * b, 2 * b + 1):
                        gained_hi(*sets[0], k)
                hi(half + 3)
                for s, dst in sets[1:]:
                    for k in range(KD):
                        gained_hi(s, dst, k)

            act.preload_act_table(ACT.Sqrt)
            act.wait_ge(rows_n_in, 16)
            for first, name, n in ((CONV_B, "a_conv_b", LT), (BR, "a_gate_r_b", LT), (BI, "a_gate_i_b", LT),
                                   (LAM, "a_lambda", LT)):
                act.dma_start(rows_a[first:first + n, :], I[name].rearrange("o (k p) -> (o k) p", p=P))\
                    .then_inc(rows_a_in, 16)
            act.dma_start(rows_a[CONV_W:CONV_W + CONV * LT, :],
                          I["a_conv_w"].rearrange("o c (k p) -> (o c k) p", p=P)).then_inc(rows_a_in, 16)
            act.wait_ge(set_done, 3)
            act.wait_ge(x_in, 16)
            f(tiles(SQ, 4), tiles(0, 4), ACT.Square, accum_out=n_ms[:, 0:1]).then_inc(ms_ready, 1)
            act.wait_ge(ms_ready, 2)
            f(n_std[:, :], n_ms[:, :], ACT.Sqrt, scale=1.0 / D, bias=eps[:, 0:1]).then_inc(std_ready, 1)

            def normalised_hi(k):
                act.wait_ge(xn_ready, k + 1)
                f(a_hi[:, k, :], tiles(XNF + k), ACT.Copy).then_inc(xh_ready, 1)

            def input_out(b):
                f(wide(xres[:, 2 * b:2 * b + 2, :]), bank[b][:, :], ACT.Copy).then_inc(x_ready, 1)

            hi(0)
            for k in range(KD):
                normalised_hi(k)
                if k == 1:
                    hi(1)
                if k == 5:
                    hi(2)
                if k in (3, 4, 6, 7):
                    input_out((3, 4, 6, 7).index(k))
            hi(3)

            def xb_hi(c):
                act.wait_ge(conv_x, 2 * c + 2)
                f(wide(a_hi[:, 8 + 2 * c:10 + 2 * c, :]), tiles(XB + 2 * c, 2), ACT.Copy).then_inc(xbh, 1)

            x_end = {half_of(c) + 1: c for c in range(6)}
            gate_end = {H_RI[g] + 1: g for g in range(LG)}
            for n in range(half_of(C_G)):
                if n - 1 in x_end:
                    xb_hi(x_end[n - 1])
                if n == 7:
                    f(lam[:, 0, :], par_a[:, LAM:LAM + LT], ACT.Abs).then_inc(lam_e, 1)
                    act.wait_ge(lam_e, 1)
                    f(lam[:, 1, :], lam[:, 0, :], ACT.Exp, scale=-1.0).then_inc(lam_e, 1)
                if n not in x_end:
                    hi(n + 4)
                act.wait_ge(ring_free, n + 1)
                if n in x_end:
                    c = x_end[n]
                    if c == 0:
                        act.wait_ge(par_ready, 2)
                    for m in range(2):
                        t = 2 * c + m
                        f(tiles(XB + t), bank[4 + c % 2][:, m * T:(m + 1) * T], ACT.Identity,
                          scale=par_a[:, CONV_W + 3 * LT + t:CONV_W + 3 * LT + t + 1],
                          bias=par_a[:, CONV_B + t:CONV_B + t + 1]).then_inc(conv_b, 1)
                    hi(n + 4)
                if n in gate_end:
                    g = gate_end[n]
                    for q in range(6):
                        w, t = q // 3, 3 * g + q % 3
                        b = bank[((0, 1, 2), (3, 6, 7))[g % 2][q // 2]]
                        y = f(tiles((RR, II)[w] + t), b[:, (q % 2) * T:(q % 2 + 1) * T], ACT.Sigmoid,
                              bias=par_a[:, (BR, BI)[w] + t:(BR, BI)[w] + t + 1])
                        if q % 3 == 2:
                            y.then_inc(ri_sig, 1)

            def decay(g):
                act.wait_ge(ri_sig, 2 * g + 1)
                for m in range(3):
                    t = 3 * g + m
                    s = f(tiles(AA + t), tiles(RR + t), ACT.Exp, scale=lam[:, 7, t:t + 1])
                s.then_inc(lru_a, 1)
                for m in range(3):
                    t = 3 * g + m
                    s = f(tiles(RR + t), tiles(RR + t), ACT.Tanh, scale=lam[:, 7, t:t + 1])
                s.then_inc(lru_t, 1)

            def lru_root(g):
                act.wait_ge(lru_m, g + 1)
                f(tiles(RR + 3 * g, 3), tiles(RR + 3 * g, 3), ACT.Sqrt, scale=-1.0).then_inc(lru_s, 1)

            act.wait_ge(lam_ready, 1)
            for g in range(LG):
                decay(g)
            act.preload_act_table(ACT.Sqrt)
            lru_root(0)
            lru_root(1)
            lru_root(2)
            lru_root(3)
            act.preload_act_table(ACT.Silu)

            def silu(c):
                if c < 3:
                    act.wait_ge(gate_raw, c + 1)
                    f(tiles(GATE + 2 * c, 2), tiles(GATE + 2 * c, 2), ACT.Silu).then_inc(lru_silu, 1)
                else:
                    act.wait_ge(ring_free, 22 + 2 * c)
                    f(tiles(GATE + 2 * c, 2), bank[4 + c % 2][:, :], ACT.Silu).then_inc(lru_silu, 1)

            def y_up(g):
                act.wait_ge(y_f, g + 1)
                f(wide(a_hi[:, 8 + 3 * g:11 + 3 * g, :]), tiles(XB + 3 * g, 3), ACT.Copy).then_inc(y_hi, 1)

            silu(0)
            silu(1)
            silu(2)
            for c in (3, 4, 5):
                hi(24 + 2 * c)
                silu(c)
                if c == 4:
                    y_up(0)
                hi(25 + 2 * c)
                if c == 4:
                    y_up(1)
            y_up(2)
            y_up(3)
            for n in range(36, 40):
                hi(n)
            for n in range(40, 44):
                hi(n)
            norm(1, half_of(C_KV), [(1, 8), (2, 0)])

            def tok_out(n):
                act.wait_ge(ring_free, half_of(C_KV) + 2 + 2 * n)
                if n >= 3:
                    act.wait_ge(hn_turn, n - 1)
                w = P if n == 0 else T
                for tb in range(TB):
                    y = f(by_tok(n)[:, tb * w:(tb + 1) * w], bank[swa_bank(n)][:, tb * T:tb * T + w], ACT.Identity,
                          scale=n_rstd[:, tb:tb + 1])
                y.then_inc(tok_raw, 1)
                act.wait_ge(tok_raw, n + 1)
                if n >= 2:
                    act.wait_ge(hn_sum, n - 1)
                f(tok_sq(n), by_tok(n), ACT.Square).then_inc(hn_sq, 1)

            def head_root(n):
                act.wait_ge(hn_sum, n + 1)
                f(head_std[:, head_cols(n)], head_sq[:, head_cols(n)], ACT.Sqrt, scale=1.0 / HD, bias=eps[:, 0:1])\
                    .then_inc(hn_std, 1)

            def head_out(n):
                act.wait_ge(hn_turn, n + 1)
                f(tiles(41, 2) if n == 0 else tiles(2 * n - 2, 2), bank[6 + n % 2][:, :], ACT.Identity,
                  scale=par_b[:, K_G:K_G + 1] if n == 0 else q_gain[:, 0:1]).then_inc(hn_done, 1)

            act.wait_ge(qg_ready, 1)
            def swa_slot(j):
                if j == 3:
                    root(1)
                if j == 4:
                    act.wait_ge(rstd_ready, 2)
                    tok_out(0)
                    tok_out(1)
                for n in HEAD_ROOT.get(j, ()):
                    head_root(n)
                if j in (5, 7, 9):
                    tok_out(j // 2)
                for n in HEAD_TURN.get(j, ()):
                    head_out(n)
                hi(48 + j)
            for j in range(min(SWA_HI.values())):
                swa_slot(j)
            act.preload_act_table(ACT.Exp)

            def softmax_exp(n, sinks=None):
                act.wait_ge(s_neg, n + 1)
                s = score_buf(n)
                e = f(s[:, 0:P], s[:, 0:P], ACT.Exp, bias=ntop[:, 2 * n:2 * n + 1], accum_out=rsum[:, 2 * n:2 * n + 1])
                e = f(s[:, P:SC], s[:, P:SC], ACT.Exp, bias=ntop[:, 2 * n + 1:2 * n + 2],
                      accum_out=rsum[:, 2 * n + 1:2 * n + 2])
                if sinks is not None:
                    e = f(esink[:, 2 * n:2 * n + 2], ntop[:, 2 * n:2 * n + 2], ACT.Exp, bias=sinks)
                e.then_inc(p_exp, 1)

            def turned(n):
                act.wait_ge(t_done, n + 1)
                if n >= 3:
                    act.wait_ge(o_done, n - 2)
                f(prob_t(n), bank[2 + n % 2][:, 0:SC], ACT.Copy).then_inc(t_out, 1)

            act.wait_ge(sink_in, 16)
            def out_hi(c):
                act.wait_ge(yb_f, c + 1)
                f(wide(a_hi[:, 8 + 2 * c:10 + 2 * c, :]), tiles(16 + 2 * c, 2), ACT.Copy).then_inc(yb_hi, 1)

            def gate_silu(c):
                act.wait_ge(q_raw, c + 1)
                f(tiles(8 + 2 * c, 2), tiles(8 + 2 * c, 2), ACT.Silu).then_inc(silu_b, 1)

            for r in range(NQ + LAG):
                if r < NQ:
                    softmax_exp(r, sink[:, r:r + 1])
                if r == NQ:
                    gate_silu(0)
                if r >= LAG:
                    turned(r - LAG)
                if r in SWA_HI:
                    swa_slot(SWA_HI[r])
                if r == NQ - 1:
                    act.preload_act_table(ACT.Silu)
                if r == NQ:
                    gate_silu(1)
                    out_hi(0)
                if r == NQ + 1:
                    gate_silu(2)
                    out_hi(1)
                    hi(65)
            out_hi(2)
            gate_silu(3)
            hi(66)
            hi(67)
            out_hi(3)
            hi(68)
            hi(69)
            norm(2, half_of(C_F1), [(3, 0)])

            def ffn(n, c_pair, c_down):
                first, base = n * (FT // 2), half_of(c_pair) + 4

                def pair(j, i=0):
                    hi(base + 4 * j, i, 8)
                    hi(base + 4 * j + 1, i, 8)
                    if j == 0:
                        hi(base + 2)
                        root(2 * n + 2)
                        act.preload_act_table(ACT.Silu)
                        hi(base + 3)
                    act.wait_ge(ff_g, first + j + 1 + i * 2)
                    gate = tiles(40 + 2 * (j % 2), 2)
                    f(gate, gate, ACT.Silu).then_inc(ff_silu, 1)
                    if j:
                        hi(base + 4 * j + 2, i, 8)
                        hi(base + 4 * j + 3, i, 8)
                    act.wait_ge(ff_f, first + j + 1 + i * 2)
                    f(wide(a_hi[:, bass.ds(i * 4 + (8 + 2 * j), 2), :]) if j >= 3 else wide(a_hi[:, 8 + 2 * j:10 + 2 * j, :]),
                      tiles(44 + 2 * (j % 2), 2), ACT.Copy).then_inc(ff_hi, 1)

                for j in range(3):
                    pair(j)
                with act.Fori(0, (FT // 2 - 3) // 2) as i:
                    pair(3, i)
                    pair(4, i)
                if n == 0:
                    act.wait_ge(trig_r, 1)
                    r, r_abs = (angle[:, i, :].rearrange("p (b n) -> p b n", b=TB) for i in (1, 2))
                    f(sine[:, :, 0:ROT], r, ACT.Sin, scale=-1.0).then_inc(trig_abs, 1)
                    f(sine[:, :, ROT:2 * ROT], r, ACT.Sin).then_inc(trig_abs, 1)
                    f(r_abs, r, ACT.Abs).then_inc(trig_abs, 1)
                    act.wait_ge(trig_abs, 3)
                    for h in range(2):
                        f(cosine[:, :, h * ROT:(h + 1) * ROT], r_abs, ACT.Sin, scale=-1.0, bias=half_pi[:, 0:1])\
                            .then_inc(trig_ready, 1)
                base_d = half_of(c_down) + 4
                with act.Fori(0, 4) as i:
                    for h in range(4):
                        hi(base_d + h, i, 4)
                hi(base_d + 16)
                hi(base_d + 17)

            ffn(0, C_F1, C_D1)
            norm(3, half_of(C_MIX), [(4, 0)])

            def mix_values(c):
                act.wait_ge(ring_free, half_of(C_MIX) + 2 * c + 2)
                for tb in range(TB):
                    at = (16 if c < 6 else 20) * T + tb * 512 + (c % 2) * T
                    v = f(flat[:, at:at + T], bank[4 + c % 2][:, tb * T:(tb + 1) * T], ACT.Identity,
                          scale=n_rstd[:, tb:tb + 1])
                v.then_inc(m_val, 1)

            def branch_hi(b):
                act.wait_ge(o_done, NQ + 4 * b + 4)
                f(wide(a_hi[:, 8 + 2 * b:10 + 2 * b, :]), bank[6 + b % 2][:, :], ACT.Copy).then_inc(ym_hi, 1)

            H_M = half_of(C_MIX)
            def mix_slot(j):
                if j == 3:
                    root(3)
                if j in MIX_TURN:
                    n = MIX_TURN[j]
                    act.wait_ge(rope_turn, n + 1)
                    f(tiles(2 * n, 2), bank[6][:, :], ACT.Copy, scale=SCALE if n < 2 else 1.0).then_inc(rope_out, 1)
                hi(H_M + 4 + j)
                if j in (9, 11, 21, 23):
                    mix_values(j // 2)

            for j in range(12):
                mix_slot(j)
            act.preload_act_table(ACT.Exp)
            for r in range(NH + 5):
                if r < NH:
                    softmax_exp(NQ + r)
                if LAG <= r < NH + LAG:
                    turned(NQ + r - LAG)
                if r >= 1:
                    for j in fill(MOBA_FILL, 12, r - 1):
                        mix_slot(j)
                if r == LAG + 6:
                    branch_hi(0)
            branch_hi(1)
            act.preload_act_table_set("natural_log_exp_and_others")
            for r in range(NH + 5):
                if r < NH:
                    act.wait_ge(z_sb, r + 1)
                    if r >= 3:
                        act.wait_ge(sp_done, r - 2)
                    f(stick_ln(r), stick_z(r), ACT.Abs).then_inc(sb_abs, 1)
                    act.wait_ge(sb_abs, r + 1)
                    f(stick_ln(r), stick_ln(r), ACT.Exp, scale=-1.0).then_inc(sb_exp, 1)
                    act.wait_ge(sb_exp, r + 1)
                    f(stick_ln(r), stick_ln(r), ACT.Ln, bias=ones[:, 0:1]).then_inc(sb_ln, 1)
                if 3 <= r < NH + 3:
                    act.wait_ge(d_done, r - 2)
                    f(stick_z(r - 3), stick_z(r - 3), ACT.Exp).then_inc(w_exp, 1)
                if r >= 1:
                    for j in fill(STICK_FILL, 24, r - 1):
                        mix_slot(j)
                if r == 9:
                    branch_hi(2)
            for j in fill(STICK_FILL, 24, NH + 4):
                mix_slot(j)
            branch_hi(3)
            act.wait_ge(m_raw, 16)
            H_B = half_of(C_BR)
            for m in range(2 * KD):
                f(tiles(32 + m), tiles(32 + m), ACT.Sigmoid, bias=par_b[:, B_GATE + m:B_GATE + m + 1]).then_inc(g_sig, 1)
                if m % 4 == 3:
                    hi(H_B + 4 + m // 4)
            hi(H_B + 8)
            hi(H_B + 9)
            for i, (t, n) in enumerate(MERGED):
                act.wait_ge(mg_f, i + 1)
                f(wide(a_hi[:, 16 + t:16 + t + n, :]), tiles(t, n), ACT.Copy).then_inc(mg_hi, 1)
                if i == 2:
                    hi(H_B + 10)
                    hi(H_B + 11)
                if i == 3:
                    hi(H_B + 12)
            for h in range(13, 16):
                hi(H_B + h)
            norm(4, half_of(C_F2), [(5, 0)])
            ffn(1, C_F2, C_D2)
            act.preload_act_table(ACT.Sqrt)
            squares(5)
            root(5)
            act.wait_ge(rstd_ready, 6)
            for q in (0, 2):
                act.wait_ge(fin_t, q + 1)
                f(tiles(8 + 2 * q, 2), bank[4 + q][:, :], ACT.Identity, scale=n_rstd[:, 0:1]).then_inc(fin_a, 1)

        @block.vector
        def _(dve):
            def lo(n, i=0, step=0):
                if n >= half_of(C_END):
                    return
                src, landed, count = source(n)
                w = src.shape[-1]
                if n in SPLIT_BY_DVE:
                    dve.wait_ge(landed, count)
                    dve.wait_ge(ring_free, n - RING + 1)
                    dve.tensor_copy(w_hi[:, n % RING, 0:w], src).then_inc(hi_dve, 1)
                    dve.wait_ge(hi_dve, n - SPLIT_BY_DVE[0] + 1)
                else:
                    dve.wait_ge(hi_done, n + 1 - sum(m < n for m in SPLIT_BY_DVE) + i * step)
                dve.tensor_tensor(w_lo[:, n % RING, 0:w], src, w_hi[:, n % RING, 0:w].bitcast(F32), ALU.subtract)\
                    .then_inc(w_done, 1)

            def low(dst, src, n):
                return dve.tensor_tensor(dst_lo(dst, n), src, dst_hi(dst, n).bitcast(F32), ALU.subtract)

            def dst_lo(t, n):
                return wide(a_lo[:, t:t + n, :])

            def dst_hi(t, n):
                return wide(a_hi[:, t:t + n, :])

            NEXT = [0, C_KV, C_F1, C_MIX, C_F2, C_END]

            def add(n, b, scale=1.0):
                if b == 3:
                    dve.wait_ge(ring_free, half_of(NEXT[n]))
                else:
                    dve.wait_ge(acc_done, 3 * n + b + 2)
                x, acc = wide(xres[:, 2 * b:2 * b + 2, :]), bank[(0, 1, 4, 5)[b] if n == 2 else b]
                dve.scalar_tensor_tensor(x, acc[:, :], scale, x, ALU.mult, ALU.add).then_inc(x_ready, 1)

            def residual(n, scale=1.0):
                for b in range(4):
                    add(n, b, scale)

            def root_inv(n):
                dve.wait_ge(std_ready, n + 1)
                dve.reciprocal(n_rstd[:, :], n_std[:, :]).then_inc(rstd_ready, 1)

            def gained_lo(s, dst, k):
                dve.wait_ge(xh_ready, KD * s + k + 1)
                dve.scalar_tensor_tensor(a_lo[:, dst + k, :], xres[:, k, :], GAINS[s][:, k:k + 1],
                                         a_hi[:, dst + k, :].bitcast(F32), ALU.mult, ALU.subtract).then_inc(xl_ready, 1)

            def norm(n, scale, half, sets):
                lo(half)
                lo(half + 1)
                for b in range(5):
                    if b < 4:
                        add(n, b, scale)
                    if b >= 1:
                        for k in (2 * b - 2, 2 * b - 1):
                            gained_lo(*sets[0], k)
                lo(half + 2)
                for k in range(KD):
                    if k == KD // 2:
                        lo(half + 3)
                    if len(sets) > 1:
                        gained_lo(*sets[1], k)

            def roots_out(n, b=3):
                dve.wait_ge(rb_ready, n + 1)
                dve.tensor_copy(spread[:, :], bank[b][:, 0:T]).then_inc(rb_sb, 1)
                dve.wait_ge(rb_sb, n + 1)

            def rooted(t, b, scale=1.0):
                y = tiles(t, 2).rearrange("p (t n) -> p t n", t=2)
                x = bank[b][:, :].rearrange("p (t n) -> p t n", t=2)
                by = spread[:, :].unsqueeze(1).to_broadcast([P, 2, T])
                if scale == 1.0:
                    return dve.tensor_tensor(y, x, by, ALU.mult)
                return dve.scalar_tensor_tensor(y, x, scale, by, ALU.mult, ALU.mult)

            dve.wait_ge(x_in, 16)
            dve.tensor_tensor_reduce(tiles(SQ + 4, 4), tiles(4, 4), tiles(4, 4), 1.0, 0.0, ALU.mult, ALU.add,
                                     accum_out=n_ms[:, 1:2]).then_inc(ms_ready, 1)
            dve.wait_ge(par_t, 1)
            dve.tensor_copy(par_n[:, :], bank[5][:, 0:KD]).then_inc(par_ready, 1)
            root_inv(0)

            def normalised(k):
                dve.wait_ge(acc_done, k // 2 + 1)
                dve.scalar_tensor_tensor(tiles(XNF + k), bank[k // 2][:, (k % 2) * T:(k % 2 + 1) * T], GAINS[0][:, k:k + 1],
                                         spread[:, :], ALU.mult, ALU.mult).then_inc(xn_ready, 1)

            def normalised_lo(k):
                dve.wait_ge(xh_ready, k + 1)
                low(k, tiles(XNF + k), 1).then_inc(xl_ready, 1)

            dve.wait_ge(par_ready, 1)
            lo(0)
            roots_out(0, 6)
            normalised(0)
            normalised(1)
            normalised_lo(0)
            normalised(2)
            normalised_lo(1)
            normalised(3)
            normalised_lo(2)
            normalised(4)
            normalised_lo(3)
            normalised(5)
            lo(1)
            normalised_lo(4)
            normalised(6)
            normalised_lo(5)
            normalised(7)
            normalised_lo(6)
            normalised_lo(7)
            lo(2)
            lo(3)

            dve.wait_ge(par_t, 2)
            dve.tensor_copy(par_a[:, :], bank[3][:, 0:ROWS_A]).then_inc(par_ready, 1)
            dve.wait_ge(par_ready, 2)

            def xb_lo(c):
                dve.wait_ge(xbh, c + 1)
                low(8 + 2 * c, tiles(XB + 2 * c, 2), 2).then_inc(xbl, 1)

            x_end = {half_of(c) + 1: c for c in range(6)}
            for n in range(half_of(C_G)):
                if n - 1 in x_end:
                    xb_lo(x_end[n - 1])
                if n in x_end:
                    c = x_end[n]
                    dve.wait_ge(conv_b, 2 * c + 2)
                    for tap in range(1, CONV):
                        for m in range(2):
                            t = 2 * c + m
                            x = tiles(XB + t)
                            if tap >= 2:
                                dve.wait_ge(conv_s, 4 * c + 2 * (tap - 2) + m + 1)
                            w = CONV_W + (CONV - 1 - tap) * LT + t
                            dve.scalar_tensor_tensor(x[:, tap:T], bank[4 + c % 2][:, m * T:(m + 1) * T - tap],
                                                     par_a[:, w:w + 1], x[:, tap:T], ALU.mult, ALU.add)\
                                .then_inc(conv_x if tap == CONV - 1 else conv_s, 1)
                lo(n + 4)

            steps = [0]

            def lam_op(op):
                steps[0] += 1
                op.then_inc(lam_step, 1)
                dve.wait_ge(lam_step, steps[0])

            dve.wait_ge(lam_e, 2)
            e, den, z, z2, ser, big = (lam[:, j, :] for j in range(1, 7))
            lam_op(dve.tensor_scalar(den, e, 2.0, 1.0, ALU.add, ALU.mult))
            lam_op(dve.reciprocal(z, den))
            lam_op(dve.tensor_tensor(z, z, e, ALU.mult))
            lam_op(dve.tensor_tensor(z2, z, z, ALU.mult))
            lam_op(dve.tensor_scalar(ser, z2, 1.0 / 15.0, 1.0, ALU.mult, ALU.mult))
            for odd in range(13, 1, -2):
                lam_op(dve.scalar_tensor_tensor(ser, ser, 1.0 / odd, z2, ALU.add, ALU.mult))
            lam_op(dve.scalar_tensor_tensor(ser, ser, 1.0, z, ALU.add, ALU.mult))
            lam_op(dve.tensor_scalar(big, par_a[:, LAM:LAM + LT], -1.0, 0.0, ALU.mult, ALU.max))
            lam_op(dve.scalar_tensor_tensor(ser, ser, 2.0, big, ALU.mult, ALU.add))
            dve.tensor_scalar(lam[:, 7, :], ser, -LRU_C, 1.0, ALU.mult, ALU.mult).then_inc(lam_ready, 1)

            def lru_square(g):
                dve.wait_ge(lru_t, g + 1)
                dve.wait_ge(lru_aa, g + 1)
                r = tiles(RR + 3 * g, 3)
                dve.scalar_tensor_tensor(r, tiles(XB + 3 * g, 3), 1.0, r, ALU.add, ALU.mult).then_inc(lru_m, 1)

            def lru_scan(g):
                dve.wait_ge(lru_b, g + 1)
                dve.wait_ge(lru_a, g + 1)
                for m in range(3):
                    t = 3 * g + m
                    s = dve.tensor_tensor_scan(tiles(XB + t), tiles(AA + t), tiles(II + t), 0.0, ALU.mult, ALU.add)
                s.then_inc(lru_h, 1)

            def gate_out(c):
                dve.wait_ge(ring_free, 22 + 2 * c)
                dve.tensor_copy(tiles(GATE + 2 * c, 2), bank[4 + c % 2][:, :]).then_inc(gate_raw, 1)

            def gated_last():
                dve.wait_ge(lru_silu, 6)
                dve.wait_ge(lru_h, LG)
                dve.wait_ge(y_f, LG - 1)
                h3 = tiles(XB + 3 * (LG - 1), 3)
                dve.tensor_tensor(h3, h3, tiles(GATE + 3 * (LG - 1), 3), ALU.mult).then_inc(y_f, 1)

            def gated_h_lo(g):
                dve.wait_ge(y_hi, g + 1)
                low(8 + 3 * g, tiles(XB + 3 * g, 3), 3).then_inc(y_lo, 1)

            lo(24)
            lo(25)
            gate_out(0)
            lru_square(0)
            lo(26)
            gate_out(1)
            lru_square(1)
            lo(27)
            lru_square(2)
            lo(28)
            gate_out(2)
            lru_square(3)
            lo(29)
            lru_scan(0)
            lru_scan(1)
            lo(30)
            lru_scan(2)
            lo(31)
            lru_scan(3)
            gated_h_lo(0)
            lo(32)
            gated_h_lo(1)
            lo(33)
            dve.wait_ge(par_t, 3)
            dve.tensor_copy(par_b[:, :], bank[6][:, 0:ROWS_B]).then_inc(par_ready, 1)
            dve.wait_ge(par_ready, 3)
            dve.tensor_scalar(q_gain[:, :], par_b[:, Q_G:Q_G + 1], SCALE, 1.0, ALU.mult, ALU.mult).then_inc(qg_ready, 1)
            lo(34)
            gated_h_lo(2)
            gated_last()
            lo(35)
            gated_h_lo(3)
            for n in range(36, 40):
                lo(n)
            for n in range(40, 44):
                lo(n)
            norm(1, 1.0, half_of(C_KV), [(1, 8), (2, 0)])

            def head_sum(n):
                dve.wait_ge(hn_sq, n + 1)
                dve.tensor_reduce(head_sq[:, head_cols(n)], tok_sq(n).rearrange("p (g n) -> p g n", n=HD), AX.X, ALU.add)\
                    .then_inc(hn_sum, 1)

            def head_scaled(n):
                dve.wait_ge(hn_std, n + 1)
                c = head_cols(n)
                dve.reciprocal(head_inv[:, c], head_std[:, c]).then_inc(hn_inv, 1)
                dve.wait_ge(hn_inv, n + 1)
                x = by_tok(n).rearrange("p (g n) -> p g n", n=HD)
                by = head_inv[:, c].unsqueeze(2).to_broadcast([P, c.stop - c.start, HD])
                if n == 0:
                    k2 = k_twice.rearrange("p (g d n) -> p g d n", d=2, n=HD)
                    dve.tensor_tensor(k2[:, :, 0, :], x, by, ALU.mult)
                    dve.tensor_tensor(k2[:, :, 1, :], x, by, ALU.mult).then_inc(hn_tok, 1)
                else:
                    dve.tensor_tensor(x, x, by, ALU.mult).then_inc(hn_tok, 1)

            def swa_out(s):
                dve.wait_ge(ring_free, half_of(C_KV) + 2 + 2 * s)
                rooted(2 * s - 2, swa_bank(s)).then_inc(q_raw, 1)

            dve.wait_ge(qg_ready, 1)
            def swa_slot(j):
                if j == 3:
                    root_inv(1)
                if j == 4:
                    dve.wait_ge(rstd_ready, 2)
                    roots_out(1)
                    dve.wait_ge(tok_raw, 1)
                    for tb in range(TB):
                        dve.tensor_scalar(tiles(44)[:, tb * P:(tb + 1) * P], bank[4][:, tb * T + P:(tb + 1) * T],
                                          n_rstd[:, tb:tb + 1], 1.0, ALU.mult, ALU.mult).then_inc(v_raw, 1)
                    head_sum(0)
                    head_sum(1)
                for n in HEAD_ROOT.get(j, ()):
                    head_scaled(n)
                if j in (5, 7, 9):
                    head_sum(j // 2)
                if j % 2 and j >= 11:
                    swa_out(j // 2)
                lo(48 + j)

            for j in range(min(SWA_LO.values())):
                swa_slot(j)

            def masked_max(n, bias, floor):
                dve.wait_ge(s_done, n + 1)
                if n > LAG:
                    dve.wait_ge(t_done, n - LAG)
                s, ps = score_buf(n), bank[n % 2]
                for q, (c, w) in enumerate(((0, P), (P, T))):
                    dve.tensor_tensor_reduce(s[:, c:c + w], ps[:, c:c + w], bias[:, T - w:T], 1.0, floor, ALU.add, ALU.max,
                                             accum_out=top[:, 2 * n + q:2 * n + q + 1]).then_inc(s_max, 1)
                dve.wait_ge(s_max, 2 * n + 2)
                dve.tensor_scalar(ntop[:, 2 * n:2 * n + 2], top[:, 2 * n:2 * n + 2], -1.0, 1.0, ALU.mult, ALU.mult)\
                    .then_inc(s_neg, 1)

            def inverse_sum(n, sinks):
                dve.wait_ge(p_exp, n + 1)
                c = slice(2 * n, 2 * n + 2)
                total = rsum
                if sinks:
                    dve.tensor_tensor(esink[:, c], esink[:, c], rsum[:, c], ALU.add).then_inc(den_sum, 1)
                    dve.wait_ge(den_sum, n + 1)
                    total = esink
                dve.reciprocal(rden[:, c], total[:, c]).then_inc(den_inv, 1)

            dve.wait_ge(sink_in, 16)
            dve.wait_ge(con_in, 16)

            def gated(c):
                dve.wait_ge(silu_b, c + 1)
                dve.wait_ge(o_out, c + 1)
                o2 = tiles(16 + 2 * c, 2)
                dve.tensor_tensor(o2, o2, tiles(8 + 2 * c, 2), ALU.mult).then_inc(yb_f, 1)

            def gated_lo(c):
                dve.wait_ge(yb_hi, c + 1)
                low(8 + 2 * c, tiles(16 + 2 * c, 2), 2).then_inc(yb_lo, 1)

            def heads_out(b):
                dve.wait_ge(o_done, 4 * b + 4)
                dve.tensor_copy(tiles(16 + 2 * b, 2), bank[6 + b % 2][:, :]).then_inc(o_out, 1)

            for r in range(NQ + 2):
                if r < NQ:
                    dve.wait_ge(bias_ready, r + 1)
                    masked_max(r, dist_bias(r), sink[:, r:r + 1])
                if r >= 2:
                    inverse_sum(r - 2, True)
                if r in SWA_LO:
                    swa_slot(SWA_LO[r])
                if r in (11, 14):
                    heads_out((r - 11) // 3)
            gated(0)
            gated_lo(0)
            swa_out(8)
            gated(1)
            lo(65)
            gated_lo(1)
            heads_out(2)
            gated(2)
            gated_lo(2)
            lo(66)
            lo(67)
            heads_out(3)
            gated(3)
            gated_lo(3)
            lo(68)
            lo(69)
            norm(2, 1.0, half_of(C_F1), [(3, 0)])

            def angles():
                t, r, turns = (angle[:, i, :] for i in range(3))
                n = [0]

                def step(op):
                    n[0] += 1
                    op.then_inc(trig_s, 1)
                    dve.wait_ge(trig_s, n[0])

                dve.wait_ge(pos_in, 16)
                step(dve.tensor_copy(turns[:, 0:TB], pos[:, :]))
                for tb in range(TB):
                    step(dve.tensor_scalar(r[:, tb * ROT:(tb + 1) * ROT], con[:, FREQ:FREQ + ROT], turns[:, tb:tb + 1], 1.0,
                                           ALU.mult, ALU.mult))
                step(dve.tensor_scalar(t, r, 1.0 / TWO_PI, ROUND, ALU.mult, ALU.add))
                step(dve.tensor_scalar(turns, t, -ROUND, 1.0, ALU.add, ALU.mult))
                for part in TURN_PARTS:
                    step(dve.scalar_tensor_tensor(r, turns, -part, r, ALU.mult, ALU.add))
                dve.tensor_scalar(r, r, -PI_LOW, PI_LOW, ALU.max, ALU.min).then_inc(trig_r, 1)

            def ffn(n, c_pair, c_down):
                first, base = n * (FT // 2), half_of(c_pair) + 4

                def pair(j, i=0):
                    gate, up, hid = (tiles(t + 2 * (j % 2), 2) for t in (40, 36, 44))
                    lo(base + 4 * j, i, 8)
                    lo(base + 4 * j + 1, i, 8)
                    if j == 0:
                        lo(base + 2)
                        root_inv(2 * n + 2)
                        lo(base + 3)
                        roots_out(2 * n + 2)
                    dve.wait_ge(ring_free, base + 4 * j - 2 + i * 8)
                    rooted(40 + 2 * (j % 2), 6 - 2 * (j % 2)).then_inc(ff_g, 1)
                    if j:
                        lo(base + 4 * j + 2, i, 8)
                    dve.wait_ge(ring_free, base + 4 * j + i * 8)
                    rooted(36 + 2 * (j % 2), 7 - 2 * (j % 2)).then_inc(ff_u, 1)
                    dve.wait_ge(ff_silu, first + j + 1 + i * 2)
                    dve.wait_ge(ff_u, first + j + 1 + i * 2)
                    dve.tensor_tensor(hid, gate, up, ALU.mult).then_inc(ff_f, 1)
                    if j:
                        lo(base + 4 * j + 3, i, 8)
                    dve.wait_ge(ff_hi, first + j + 1 + i * 2)
                    if j < 3:
                        low(8 + 2 * j, hid, 2).then_inc(ff_lo, 1)
                    else:
                        at = bass.ds(i * 4 + (8 + 2 * j), 2)
                        dve.tensor_tensor(wide(a_lo[:, at, :]), hid, wide(a_hi[:, at, :]).bitcast(F32), ALU.subtract)\
                            .then_inc(ff_lo, 1)

                for j in range(3):
                    pair(j)
                with dve.Fori(0, (FT // 2 - 3) // 2) as i:
                    pair(3, i)
                    pair(4, i)
                if n == 0:
                    angles()
                base_d = half_of(c_down) + 4
                with dve.Fori(0, 4) as i:
                    for h in range(4):
                        lo(base_d + h, i, 4)
                lo(base_d + 16)
                lo(base_d + 17)

            ffn(0, C_F1, C_D1)
            norm(3, FFN_RES, half_of(C_MIX), [(4, 0)])

            def rope(n):
                def turned(t):
                    return t[:, 0:TB * 4 * 2 * ROT].rearrange("p (b h n) -> p b h n", b=TB, h=4)

                def per_head(t):
                    return t.unsqueeze(2).to_broadcast([P, TB, 4, t.shape[-1]])

                dve.wait_ge(m_raw, n + 1)
                x = mix_tok(n).rearrange("p (b h n) -> p b h n", b=TB, h=4)
                a, b = slice(0, ROT), slice(ROT, 2 * ROT)
                one, two = turned(tiles(52)), turned(tiles(54))
                dve.tensor_tensor(one, x[:, :, :, 0:2 * ROT], per_head(cosine[:, :, :]), ALU.mult).then_inc(rope_a, 1)
                dve.tensor_tensor(two[:, :, :, a], x[:, :, :, b], per_head(sine[:, :, a]), ALU.mult).then_inc(rope_a, 1)
                dve.tensor_tensor(two[:, :, :, b], x[:, :, :, a], per_head(sine[:, :, b]), ALU.mult).then_inc(rope_a, 1)
                dve.wait_ge(rope_a, 3 * n + 3)
                dve.tensor_tensor(x[:, :, :, 0:2 * ROT], one, two, ALU.add).then_inc(rope_done, 1)

            def branch_lo(b):
                dve.wait_ge(ym_hi, b + 1)
                low(8 + 2 * b, bank[6 + b % 2][:, :], 2).then_inc(ym_lo, 1)

            H_M = half_of(C_MIX)

            def mix_out(c):
                dve.wait_ge(ring_free, H_M + 2 * c + 2)
                if c >= 4:
                    rooted(2 * c - 4 if c < 10 else 2 * c + 8, mix_bank(c), SCALE if c in (6, 7) else 1.0).then_inc(m_raw, 1)
                    return
                if c >= 2:
                    dve.wait_ge(rope_turn, c - 1)
                for tb in range(TB):
                    y = dve.tensor_scalar(mix_tok(c)[:, tb * T:(tb + 1) * T], bank[mix_bank(c)][:, tb * T:(tb + 1) * T],
                                          n_rstd[:, tb:tb + 1], 1.0, ALU.mult, ALU.mult)
                y.then_inc(m_raw, 1)

            def mix_slot(j):
                c = j // 2
                if j == 3:
                    root_inv(3)
                if j == 4:
                    dve.wait_ge(rstd_ready, 4)
                    mix_out(0)
                    rope(0)
                    mix_out(1)
                if j == 5:
                    rope(1)
                    roots_out(3)
                if j == 6:
                    mix_out(2)
                    rope(2)
                if j % 2 and j >= 7 and c not in (4, 5, 10, 11):
                    mix_out(c)
                if j == 7:
                    rope(3)
                lo(H_M + 4 + j)

            dve.wait_ge(trig_ready, 2)
            for j in range(12):
                mix_slot(j)
            for r in range(NH + 5):
                if r < NH:
                    masked_max(NQ + r, con[:, CMASK:CMASK + T], -3e38)
                if 2 <= r < NH + 2:
                    inverse_sum(NQ + r - 2, False)
                if r >= 1:
                    for j in fill(MOBA_FILL, 12, r - 1):
                        mix_slot(j)
                if r == LAG + 6:
                    branch_lo(0)
            branch_lo(1)
            dve.wait_ge(o_done, NQ + NH)
            for r in range(NH + 5):
                if r < NH:
                    dve.wait_ge(z_done, r + 1)
                    if r >= 6:
                        dve.wait_ge(o_done, NQ + NH + r - 5)
                    dve.tensor_tensor(stick_z(r), bank[r % 2][:, 0:SC], con[:, SBMASK:SBMASK + SC], ALU.add)\
                        .then_inc(z_sb, 1)
                if 1 <= r <= NH:
                    n = r - 1
                    dve.wait_ge(sb_ln, n + 1)
                    if n >= 2:
                        dve.wait_ge(c_done, n - 1)
                    dve.scalar_tensor_tensor(stick_sp(n), stick_z(n), 0.0, stick_ln(n), ALU.max, ALU.add)\
                        .then_inc(sp_done, 1)
                if 3 <= r < NH + 3:
                    n = r - 3
                    dve.wait_ge(c_done, n + 1)
                    dve.tensor_tensor(stick_z(n), stick_z(n), bank[2 + n % 2][:, 0:SC], ALU.subtract).then_inc(d_done, 1)
                if r >= 1:
                    for j in fill(STICK_FILL, 24, r - 1):
                        mix_slot(j)
                if r == 9:
                    branch_lo(2)
            for j in fill(STICK_FILL, 24, NH + 4):
                mix_slot(j)
            branch_lo(3)
            H_B = half_of(C_BR)
            for h in range(4, 8):
                lo(H_B + h)
            for b in range(4):
                if b < 3:
                    dve.wait_ge(br_done, b + 1)
                else:
                    dve.wait_ge(ring_free, H_B + 4)
                dve.wait_ge(g_sig, 2 * b + 2)
                dve.tensor_tensor(tiles(32 + 2 * b, 2), tiles(32 + 2 * b, 2), bank[b][:, :], ALU.mult).then_inc(mg_a, 1)
            lo(H_B + 8)
            lo(H_B + 9)
            def other(i):
                t, n = MERGED[i]
                if t < 6:
                    dve.wait_ge(br_done, t // 2 + 4)
                else:
                    dve.wait_ge(ring_free, H_B + 8)
                dve.wait_ge(g_sig, KD + t + n)
                c = t % 2 * T
                dve.tensor_tensor(tiles(40 + t, n), tiles(40 + t, n), bank[4 + t // 2][:, c:c + n * T], ALU.mult)\
                    .then_inc(mg_b, 1)

            def merged(i):
                t, n = MERGED[i]
                dve.wait_ge(mg_a, t // 2 + 1)
                dve.wait_ge(mg_b, i + 1)
                dve.tensor_tensor(tiles(t, n), tiles(32 + t, n), tiles(40 + t, n), ALU.add).then_inc(mg_f, 1)

            def merged_lo(i):
                t, n = MERGED[i]
                dve.wait_ge(mg_hi, i + 1)
                low(16 + t, tiles(t, n), n).then_inc(mg_lo, 1)

            other(0)
            merged(0)
            other(1)
            merged(1)
            merged_lo(0)
            merged_lo(1)
            other(2)
            merged(2)
            other(3)
            merged_lo(2)
            lo(H_B + 10)
            merged(3)
            lo(H_B + 11)
            merged_lo(3)
            other(4)
            merged(4)
            lo(H_B + 12)
            merged_lo(4)
            for h in range(13, 16):
                lo(H_B + h)
            norm(4, 1.0, half_of(C_F2), [(5, 0)])
            ffn(1, C_F2, C_D2)

            for b in range(4):
                add(5, b, FFN_RES)
            root_inv(5)
            dve.wait_ge(rstd_ready, 6)
            for q in (1, 3):
                dve.wait_ge(fin_t, q + 1)
                dve.tensor_scalar(tiles(8 + 2 * q, 2), bank[4 + q][:, :], n_rstd[:, 1:2], 1.0, ALU.mult, ALU.mult)\
                    .then_inc(fin_d, 1)


_INS = ["x", "a_norm_g", "a_w_in", "a_conv_w", "a_conv_b", "a_gate_r_w", "a_gate_r_b", "a_gate_i_w", "a_gate_i_b",
        "a_lambda", "a_w_out", "kv_norm_g", "w_kv", "k_norm_g", "b_norm_g", "b_w_in", "q_norm_g", "sinks", "b_w_out",
        "positions_2", "ffn1_norm_2", "ffn1_w_gate_2", "ffn1_w_up_2", "ffn1_w_down_2", "mix_norm_2", "w_in_2",
        "b_gate_2", "w_branch_moba_2", "w_branch_sb_2", "w_out_2", "ffn2_norm_2", "ffn2_w_gate_2", "ffn2_w_up_2",
        "ffn2_w_down_2", "final_norm_2"]


def kernel(**inputs):
    import concourse.bacc as _bacc
    from concourse import mybir as _mybir
    from concourse.bass_utils import run_bass_kernel_spmd as _run

    nc = _bacc.Bacc("TRN2", target_bir_lowering=False, num_devices=1)
    arrays, args = {"constants": constants()}, {}
    for name in _INS:
        arrays[name] = np.ascontiguousarray(inputs[name])
    for name, a in arrays.items():
        args[name] = nc.dram_tensor(name, a.shape, _mybir.dt.from_np(a.dtype), kind="ExternalInput").ap()
    out = nc.dram_tensor("out", (1, T, D), _mybir.dt.float32, kind="ExternalOutput").ap()
    build(nc, args, out)
    r = _run(nc, [arrays], core_ids=[0])
    return r.results[0]["out"]
```
